# Optimizing a Trainium2 kernel written in Bass

```python
import math
import jax
import jax.numpy as jnp
from jax import lax
import numpy as np

D_MODEL = 1024
BATCH = 1
SEQ = 512
DEPTH = 2
DEC_BATCH = 1
DEC_SEQ = 64
PAST_LEN = 256

CHUNK = 64
N_HEADS = 4
HEAD_DIM = 64
V_DIM = 2 * HEAD_DIM
ATTN_WIDTH = N_HEADS * V_DIM
QK_COLS = N_HEADS * 2 * HEAD_DIM
ROT_DIM = HEAD_DIM // 4
ROPE_THETA = 500000.0
CONV_CH = D_MODEL - ATTN_WIDTH
CONV_WIDTH = 31
CONV_STATE = CONV_WIDTH - 1
MIX_WIDTH = ATTN_WIDTH + CONV_CH
IN_COLS = 2 * QK_COLS + ATTN_WIDTH + 2 * CONV_CH
N_EXPERTS = 16
N_GROUPS = 4
EXPERTS_PER_GROUP = N_EXPERTS // N_GROUPS
TOP_K = 2
D_EXPERT = D_MODEL // 2
DEEPNORM_ALPHA = (2 * DEPTH) ** 0.25
DEEPNORM_BETA = (8 * DEPTH) ** -0.25
Q_BLOCK = 128
LN_EPS = 1e-5

kernel_name = 'hymba_diffattn_conformer_conv_grouped_moe_stream'

def _layer_norm(x, g, b, eps=LN_EPS):
    xf = x.astype(jnp.float32)
    mu = jnp.mean(xf, -1, keepdims=True)
    var = jnp.mean(jnp.square(xf - mu), -1, keepdims=True)
    y = (xf - mu) * lax.rsqrt(var + eps) * g.astype(jnp.float32) + b.astype(jnp.float32)
    return y.astype(x.dtype)

def _rms_norm(x, g, eps=LN_EPS):
    xf = x.astype(jnp.float32)
    y = xf * lax.rsqrt(jnp.mean(xf * xf, -1, keepdims=True) + eps) * g.astype(jnp.float32)
    return y.astype(x.dtype)

def _partial_rope(x, pos):
    half = ROT_DIM // 2
    inv_freq = jnp.power(ROPE_THETA, -jnp.arange(half, dtype=jnp.float32) * 2.0 / ROT_DIM)
    ang = pos.astype(jnp.float32)[:, None] * inv_freq[None, :]
    cos = jnp.cos(ang)[None, :, None, None, :]
    sin = jnp.sin(ang)[None, :, None, None, :]
    xr = x[..., :ROT_DIM].astype(jnp.float32)
    x1, x2 = xr[..., :half], xr[..., half:]
    rot = jnp.concatenate([x1 * cos - x2 * sin, x2 * cos + x1 * sin], -1).astype(x.dtype)
    return jnp.concatenate([rot, x[..., ROT_DIM:]], -1)

def _diff_attend(q, k, v, lam, mask):
    s = jnp.einsum('bqhmd,bkhmd->bhmqk', q, k).astype(jnp.float32) * (HEAD_DIM ** -0.5)
    if mask is not None:
        s = jnp.where(mask, s, -jnp.inf)
    p = jax.nn.softmax(s, axis=-1)
    a = p[:, :, 0] - lam * p[:, :, 1]
    return jnp.einsum('bhqk,bkhe->bqhe', a.astype(v.dtype), v)

def _prompt_attention(q, k, v, lam):
    B, S = q.shape[0], q.shape[1]
    nb = S // Q_BLOCK
    qb = q.reshape(B, nb, Q_BLOCK, N_HEADS, 2, HEAD_DIM).transpose(1, 0, 2, 3, 4, 5)
    k_chunk = jnp.arange(S) // CHUNK

    def one_block(args):
        q_blk, i = args
        q_chunk = (i * Q_BLOCK + jnp.arange(Q_BLOCK)) // CHUNK
        mask = k_chunk[None, :] <= q_chunk[:, None]
        return _diff_attend(q_blk, k, v, lam, mask)

    out = lax.map(one_block, (qb, jnp.arange(nb)))
    return out.transpose(1, 0, 2, 3, 4).reshape(B, S, N_HEADS, V_DIM)

def _causal_depthwise_conv(u_pad, w, b):
    out = lax.conv_general_dilated(u_pad, w[:, None, :], window_strides=(1,), padding='VALID',
                                   dimension_numbers=('NWC', 'WIO', 'NWC'),
                                   feature_group_count=CONV_CH)
    return out + b

def _moe(h, w_router, b_router, w_gate, w_up, w_down):
    scores = jax.nn.softmax((h @ w_router).astype(jnp.float32), axis=-1)
    sel = scores + b_router.astype(jnp.float32)
    grp = sel.reshape(sel.shape[:-1] + (N_GROUPS, EXPERTS_PER_GROUP))
    group_score = lax.top_k(grp, TOP_K)[0].sum(-1)
    best_group = jnp.argmax(group_score, axis=-1)
    expert_group = jnp.arange(N_EXPERTS) // EXPERTS_PER_GROUP
    masked = jnp.where(expert_group == best_group[..., None], sel, -jnp.inf)
    _, idx = lax.top_k(masked, TOP_K)
    w_sel = jnp.take_along_axis(scores, idx, axis=-1)
    w_sel = w_sel / jnp.sum(w_sel, -1, keepdims=True)
    combine = jnp.sum(jax.nn.one_hot(idx, N_EXPERTS, dtype=jnp.float32) * w_sel[..., None], -2)
    hg = jnp.einsum('btd,edf->btef', h, w_gate)
    hu = jnp.einsum('btd,edf->btef', h, w_up)
    act = jax.nn.silu(hg) * hu * combine.astype(h.dtype)[..., None]
    return jnp.einsum('btef,efd->btd', act, w_down)

def _trunk_layer(x, c, pos, l, past_k, past_v, past_conv,
                 w_ada, b_ada, w_in, lambda_qk, subln_g, conv_w, conv_b, conv_ln_g, conv_ln_b,
                 w_out, ln1_g, ln1_b, ln2_g, ln2_b, w_router, b_router, w_gate, w_up, w_down):
    B, T = x.shape[0], x.shape[1]
    mod = jax.nn.silu(c) @ w_ada + b_ada
    sh_a, sc_a, g_a, sh_f, sc_f, g_f = jnp.split(mod[:, None, :], 6, axis=-1)
    h = x * (1.0 + sc_a) + sh_a
    proj = h @ w_in
    q, k, v, u = jnp.split(proj, [QK_COLS, 2 * QK_COLS, 2 * QK_COLS + ATTN_WIDTH], axis=-1)
    q = _partial_rope(q.reshape(B, T, N_HEADS, 2, HEAD_DIM), pos)
    k = _partial_rope(k.reshape(B, T, N_HEADS, 2, HEAD_DIM), pos)
    v = v.reshape(B, T, N_HEADS, V_DIM)
    lam_init = 0.8 - 0.6 * math.exp(-0.3 * l)
    lq = lambda_qk.astype(jnp.float32)
    lam = jnp.exp(jnp.sum(lq[0] * lq[1])) - jnp.exp(jnp.sum(lq[2] * lq[3])) + lam_init
    if past_k is None:
        o = _prompt_attention(q, k, v, lam)
        u_hist = jnp.zeros((B, CONV_STATE, CONV_CH), x.dtype)
    else:
        k_all = jnp.concatenate([past_k.astype(k.dtype), k], axis=1)
        v_all = jnp.concatenate([past_v.astype(v.dtype), v], axis=1)
        o = _diff_attend(q, k_all, v_all, lam, None)
        u_hist = past_conv
    o = (_rms_norm(o, subln_g) * (1.0 - lam_init)).reshape(B, T, ATTN_WIDTH)
    u_a, u_g = jnp.split(u, 2, axis=-1)
    glu = u_a * jax.nn.sigmoid(u_g)
    glu_pad = jnp.concatenate([u_hist.astype(glu.dtype), glu], axis=1)
    new_conv = glu_pad[:, -CONV_STATE:]
    cv = _causal_depthwise_conv(glu_pad, conv_w, conv_b)
    cv = jax.nn.silu(_layer_norm(cv, conv_ln_g, conv_ln_b))
    mix = jnp.concatenate([o, cv], axis=-1) @ w_out
    x = _layer_norm(DEEPNORM_ALPHA * x + g_a * mix, ln1_g, ln1_b)
    h = x * (1.0 + sc_f) + sh_f
    ffn = _moe(h, w_router, b_router, w_gate, w_up, w_down)
    x = _layer_norm(DEEPNORM_ALPHA * x + g_f * ffn, ln2_g, ln2_b)
    return x, k, v, new_conv

def setup_inputs(seed: int = 0) -> dict:
    key = jax.random.key(seed)
    ks = jax.random.split(key, 26)
    D = D_MODEL

    def nrm(k, shape, scale=1.0):
        return jax.random.normal(k, shape, jnp.float32) * scale

    return {
        'x_prompt': nrm(ks[0], (BATCH, SEQ, D)),
        'x_sample': nrm(ks[1], (DEC_BATCH, DEC_SEQ, D)),
        'cache_k': nrm(ks[2], (DEPTH, DEC_BATCH, PAST_LEN, N_HEADS, 2, HEAD_DIM)),
        'cache_v': nrm(ks[3], (DEPTH, DEC_BATCH, PAST_LEN, N_HEADS, V_DIM)),
        'state_conv': nrm(ks[4], (DEPTH, DEC_BATCH, CONV_STATE, CONV_CH), 0.5),
        'c_prompt': nrm(ks[5], (BATCH, D)),
        'c_sample': nrm(ks[6], (DEC_BATCH, D)),
        'w_ada': nrm(ks[7], (DEPTH, D, 6 * D), 0.5 * D ** -0.5),
        'b_ada': nrm(ks[8], (DEPTH, 6 * D), 0.02),
        'w_in': nrm(ks[9], (DEPTH, D, IN_COLS), D ** -0.5),
        'lambda_qk': nrm(ks[10], (DEPTH, 4, HEAD_DIM), 0.1),
        'subln_g': 1.0 + nrm(ks[11], (DEPTH, V_DIM), 0.02),
        'conv_w': nrm(ks[12], (DEPTH, CONV_WIDTH, CONV_CH), CONV_WIDTH ** -0.5),
        'conv_b': nrm(ks[13], (DEPTH, CONV_CH), 0.02),
        'conv_ln_g': 1.0 + nrm(ks[14], (DEPTH, CONV_CH), 0.02),
        'conv_ln_b': nrm(ks[15], (DEPTH, CONV_CH), 0.02),
        'w_out': nrm(ks[16], (DEPTH, MIX_WIDTH, D), DEEPNORM_BETA * MIX_WIDTH ** -0.5),
        'ln1_g': 1.0 + nrm(ks[17], (DEPTH, D), 0.02),
        'ln1_b': nrm(ks[18], (DEPTH, D), 0.02),
        'ln2_g': 1.0 + nrm(ks[19], (DEPTH, D), 0.02),
        'ln2_b': nrm(ks[20], (DEPTH, D), 0.02),
        'w_router': nrm(ks[21], (D, N_EXPERTS), D ** -0.5),
        'b_router': nrm(ks[22], (N_EXPERTS,), 0.01),
        'w_gate': nrm(ks[23], (DEPTH, N_EXPERTS, D, D_EXPERT), D ** -0.5),
        'w_up': nrm(ks[24], (DEPTH, N_EXPERTS, D, D_EXPERT), D ** -0.5),
        'w_down': nrm(ks[25], (DEPTH, N_EXPERTS, D_EXPERT, D), DEEPNORM_BETA * D_EXPERT ** -0.5),
    }

def reference(x_prompt, x_sample, cache_k, cache_v, state_conv, c_prompt, c_sample,
              w_ada, b_ada, w_in, lambda_qk, subln_g, conv_w, conv_b, conv_ln_g, conv_ln_b,
              w_out, ln1_g, ln1_b, ln2_g, ln2_b, w_router, b_router, w_gate, w_up, w_down):
    pos_p = jnp.arange(x_prompt.shape[1], dtype=jnp.int32)
    pos_s = PAST_LEN + jnp.arange(x_sample.shape[1], dtype=jnp.int32)
    xp, xs = x_prompt, x_sample
    k_p, v_p, cv_p, k_s, v_s, cv_s = [], [], [], [], [], []
    for l in range(DEPTH):
        lw = (w_ada[l], b_ada[l], w_in[l], lambda_qk[l], subln_g[l], conv_w[l], conv_b[l],
              conv_ln_g[l], conv_ln_b[l], w_out[l], ln1_g[l], ln1_b[l], ln2_g[l], ln2_b[l],
              w_router, b_router, w_gate[l], w_up[l], w_down[l])
        xp, kn, vn, cn = _trunk_layer(xp, c_prompt, pos_p, l, None, None, None, *lw)
        k_p.append(kn)
        v_p.append(vn)
        cv_p.append(cn)
        xs, kn, vn, cn = _trunk_layer(xs, c_sample, pos_s, l, cache_k[l], cache_v[l], state_conv[l], *lw)
        k_s.append(kn)
        v_s.append(vn)
        cv_s.append(cn)
    return (xp, xs, jnp.stack(k_p), jnp.stack(v_p), jnp.stack(cv_p),
            jnp.stack(k_s), jnp.stack(v_s), jnp.stack(cv_s))


_drawn_inputs = setup_inputs


def setup_inputs(seed=0):
    import zlib

    import numpy as np

    out = dict(_drawn_inputs(seed))
    spreads = {}
    factors = {'lambda_qk': 5.628,
     'subln_g': 31.154,
     'conv_b': 7.762,
     'conv_ln_g': 32.095,
     'conv_ln_b': 30.224}
    for name, (base, spread) in spreads.items():
        noise = np.random.default_rng([zlib.crc32(name.encode()), seed]).standard_normal(out[name].shape)
        drawn = base * np.exp(spread * noise) if base else spread * noise
        out[name] = jnp.asarray(drawn.astype(out[name].dtype))
    for name, factor in factors.items():
        out[name] = (out[name] * factor).astype(out[name].dtype)
    return out
```

```python
import math
from contextlib import ExitStack

import concourse.bass as bass
import numpy as np
from concourse import mybir

ALU = mybir.AluOpType
ACT = mybir.ActivationFunctionType
F32 = mybir.dt.float32
I32 = mybir.dt.int32
AX_X = mybir.AxisListType.X

P = 128
D = 1024
DEPTH = 2
SEQ = 512
DEC = 64
PAST = 256
HEADS = 4
HD = 64
CONV = 512
TAPS = 31
STATE = TAPS - 1
EXPERTS = 16
GROUPS = 4
PER_GROUP = EXPERTS // GROUPS
TOP = 2
FE = 512
EPS = 1e-5
ALPHA = (2 * DEPTH) ** 0.25
SCALE = HD ** -0.5
NEG = -1e30
IN_COLS = 2560

KD = D // P
NTOK = SEQ + DEC
TILES = 5
ROWS = [P, P, P, P, DEC]
COL = [0, 128, 256, 384, 512]
GAP = SEQ + STATE
MCOL = [0, 128, 256, 384, GAP]
MW = 640
CW = GAP + DEC
HALF = CW // 2
GW = SEQ + DEC + 2 * STATE
KEYS_S = PAST + DEC
ADA_CHUNKS = 6 * D // 512
CHUNK_W = KD * 512
SLOTS = 6
TM = 64
MAX_TILES = EXPERTS + TOP * NTOK // TM
LANDED = 16


def lam_init(layer):
    return 0.8 - 0.6 * math.exp(-0.3 * layer)


def build(nc, a):
    with ExitStack() as ctx:
        def sb(name, shape, dt=F32):
            return ctx.enter_context(nc.sbuf_tensor(name, shape, dt))

        def sem(name):
            return ctx.enter_context(nc.semaphore(name))

        mod_dram = nc.dram_tensor("mod_scratch", (2, 6 * D), F32, kind="Internal").ap()
        h_dram = nc.dram_tensor("h_scratch", (NTOK, D), F32, kind="Internal").ap()
        slot_dram = nc.dram_tensor("slot_scratch", ((MAX_TILES + 1) * TM, 1), F32, kind="Internal").ap()
        y_dram = nc.dram_tensor("y_scratch", (MAX_TILES * TM, D), F32, kind="Internal").ap()

        ring = sb("ring", [P, SLOTS * CHUNK_W])
        x = sb("x", [P, TILES, D])
        reg_h = sb("reg_h", [P, KD * NTOK])
        reg_m = sb("reg_m", [P, KD * MW])
        reg_q = sb("reg_q", [P, HEADS * (NTOK + SEQ)])
        reg_v = sb("reg_v", [P, HEADS * KEYS_S + TILES * 512 + 2 * 512])

        def slot(s):
            return ring[:, s * CHUNK_W:(s + 1) * CHUNK_W]

        def by_k(s):
            return slot(s).rearrange("p (k c) -> p k c", k=KD)

        def by_f(s):
            return slot(s).rearrange("p (k c) -> p k c", k=FE // P)

        o = 4 * CHUNK_W
        glu = ring[:, o:o + 4 * GW].rearrange("p (j c) -> p j c", j=4)
        o += 4 * GW
        qk_row = ring[:, o:o + 1024].rearrange("p (b c) -> p b c", b=2)
        square = ring[:, o:o + 512]
        o += 1024
        prob = ring[:, o:o + 2048].rearrange("p (b m c) -> p b m c", b=2, m=2)
        cache_k_row = ring[:, o:o + 1024].rearrange("p (b c) -> p b c", b=2)
        sig = ring[:, o + 1024:o + 1024 + 2 * NTOK].rearrange("p (b c) -> p b c", b=2)
        new_conv = ring[:, o + 1024 + 2 * NTOK:o + 1024 + 2 * NTOK + 1024].rearrange("p (b c) -> p b c", b=2)
        o += 2048
        attn = ring[:, o:o + 1024].rearrange("p (b c) -> p b c", b=2)
        o += 1024
        attn_t = ring[:, o:o + 1024].rearrange("p (b c) -> p b c", b=2)
        o += 1024
        out_row = ring[:, o:o + 512]
        assert o + 512 <= SLOTS * CHUNK_W

        h_t = reg_h[:, :].rearrange("p (k t) -> p k t", k=KD)
        gate_bc = reg_h[:, 0:2 * D].rearrange("p (s c) -> p s c", s=2)
        ln_g_bc = reg_h[:, 2 * D:3 * D]
        ln_b_bc = reg_h[:, 3 * D:4 * D]
        route_t = [reg_h[:, 4096:4608].rearrange("p (k t) -> p k t", k=4),
                   reg_v[:, 4096:4608].rearrange("p (k t) -> p k t", k=4)]

        mix_t = reg_m[:, :].rearrange("p (k t) -> p k t", k=KD)
        b_ada = reg_m[:, 0:1536].rearrange("p (r c) -> p r c", r=3)
        mod_row = reg_m[:, 1536:3072].rearrange("p (r c) -> p r c", r=3)
        gathered_row = reg_m[0:TM, 0:1024]
        tok_t = reg_m[:, 1024:1536].rearrange("p (k t) -> p k t", k=KD)
        silu_g = reg_m[:, 1536:2048]
        act_row = reg_m[:, 2048:2560]
        act_t = reg_m[:, 2560:2816].rearrange("p (f t) -> p f t", f=4)
        y_row = reg_m[:, 2816:3328]
        mixed = reg_m[:, 0:2048].rearrange("p (b c) -> p b c", b=2)

        o = 3328
        lam_prod = reg_m[:, o:o + 128].rearrange("p (n c) -> p n c", n=2)
        sel = reg_m[:, o:o + 80].rearrange("p (t e) -> p t e", t=TILES)
        worse = reg_m[:, o + 80:o + 160].rearrange("p (t e) -> p t e", t=TILES)
        cmp_ge = reg_m[:, o + 160:o + 480].rearrange("p (g j i) -> p g j i", j=4, i=4)
        cmp_gt = reg_m[:, o + 480:o + 800].rearrange("p (g j i) -> p g j i", j=4, i=4)
        picks = reg_m[:, o + 800:o + 1120].rearrange("p (n t e) -> p n t e", n=4, t=TILES)

        q_t = reg_q[:, 0:HEADS * NTOK].rearrange("p (h t) -> p h t", h=HEADS)
        k_t = reg_q[:, HEADS * NTOK:].rearrange("p (h t) -> p h t", h=HEADS)
        scale_bc = reg_q[:, 0:2048].rearrange("p (s c) -> p s c", s=2)
        shift_bc = reg_q[:, 2048:4096].rearrange("p (s c) -> p s c", s=2)

        ks_t = reg_v[:, 0:HEADS * KEYS_S].rearrange("p (h t) -> p h t", h=HEADS)
        v_row = reg_v[:, HEADS * KEYS_S:HEADS * KEYS_S + TILES * 512].rearrange("p (t c) -> p t c", t=TILES)
        cache_v = reg_v[:, HEADS * KEYS_S + TILES * 512:].rearrange("p (t c) -> p t c", t=2)
        norm_row = reg_v[:, 0:2048].rearrange("p (b c) -> p b c", b=2)
        h_row = reg_v[:, 2048:4096].rearrange("p (b c) -> p b c", b=2)
        picked = reg_v[:, 0:4096].rearrange("p (b k c) -> p b k c", b=2, k=2)

        ident = sb("ident", [P, P])
        ones = sb("ones", [P, P])
        conv_mean = sb("conv_mean", [P, P])
        before = sb("before", [P, P])
        w_router = sb("w_router_sb", [P, KD, EXPERTS])
        b_router = sb("b_router_sb", [P, EXPERTS])
        rope = sb("rope_sb", [P, TILES, 32])
        c_row = sb("c_row", [16, P])
        c_silu = sb("c_silu", [16, P])
        c_t = sb("c_t", [P, KD, 32])
        conv_w_row = sb("conv_w_row", [TAPS, CONV])
        state_row = sb("state_row", [STATE, CONV])
        mod_cols_row = sb("mod_cols_row", [32, P])
        vec_row = sb("vec_row", [13, P])
        lam_qk = sb("lam_qk", [P, 4, HD])
        cols = sb("cols", [P, 320])
        eps = sb("eps", [P, 1])
        lam_e = sb("lam_e", [P, 6])
        rope_t = sb("rope_t", [P, 2, 8, 16])
        row_max = sb("row_max", [P, 2, 2])
        neg_max = sb("neg_max", [P, 2, 2])
        row_sum = sb("row_sum", [P, 2, 2])
        row_inv = sb("row_inv", [P, 2, 2])
        head_ss = sb("head_ss", [P, 3, 4])
        stats = sb("stats", [P, 2, 6])
        mean_var = sb("mean_var", [P, 2])
        std = sb("std", [P, 2])
        logits = sb("logits", [P, TILES, EXPERTS])
        score = sb("score", [P, TILES, EXPERTS])
        mask = sb("mask", [P, TILES, EXPERTS])
        lower = sb("lower", [P, 4, 4])
        upper = sb("upper", [P, 4, 4])
        reset = sb("reset", [P, TILES, EXPERTS])
        small = sb("small", [P, 8, TILES * GROUPS])
        pick = sb("pick", [P, 4, TILES])
        slot_of = sb("slot_of", [P, 2, TILES], I32)
        cnt = sb("cnt", [P, 6, EXPERTS])
        cnt_i = sb("cnt_i", [P, 2, EXPERTS], I32)
        total = sb("total", [P, 1])
        table = sb("table", [P, 40], I32)
        token_i = sb("token_i", [P, TILES], I32)
        token_f = sb("token_f", [P, TILES])
        zero_row = sb("zero_row", [MAX_TILES + 1, TM])
        slot_row = sb("slot_row", [MAX_TILES + 1, TM])
        slot_token = sb("slot_token", [TM, MAX_TILES + 1], I32)
        slot_now = sb("slot_now", [TM, 1], I32)

        pair = [ctx.enter_context(nc.psum_tensor(f"pair{i}", [P, 2, 512], F32)) for i in range(4)]

        def bank(b):
            return pair[b // 2][:, b % 2, :]

        const_ready = sem("const_ready")
        const_step = sem("const_step")
        setup_in = sem("setup_in")
        setup_dve = sem("setup_dve")
        c_silu_ready = sem("c_silu_ready")
        c_mm = sem("c_mm")
        c_ready = sem("c_ready")
        landed = [sem(f"landed{s}") for s in range(SLOTS)]
        ada_in = sem("ada_in")
        small_in = sem("small_in")
        cache_k_in = sem("cache_k_in")
        cache_v_in = sem("cache_v_in")
        ada_mm = sem("ada_mm")
        mod_ready = sem("mod_ready")
        mod_out = sem("mod_out")
        mod_cols_in = sem("mod_cols_in")
        cols_mm = sem("cols_mm")
        cols_ready = sem("cols_ready")
        lam_ready = sem("lam_ready")
        lam_exp = sem("lam_exp")
        xt_mm = sem("xt_mm")
        ht_dve = sem("ht_dve")
        ht_act = sem("ht_act")
        u_mm = sem("u_mm")
        sig_done = sem("sig_done")
        glu_done = sem("glu_done")
        conv_done = sem("conv_done")
        new_conv_mm = sem("new_conv_mm")
        new_conv_ready = sem("new_conv_ready")
        new_conv_out = sem("new_conv_out")
        proj_mm = sem("proj_mm")
        proj_act = sem("proj_act")
        proj_rope = sem("proj_rope")
        qk_t_mm = sem("qk_t_mm")
        qk_t_done = sem("qk_t_done")
        k_out = [sem("k_out0"), sem("k_out1")]
        v_out = sem("v_out")
        conv_stat_mm = sem("conv_stat_mm")
        centred = sem("centred")
        squared = sem("squared")
        conv_std = sem("conv_std")
        conv_normed = sem("conv_normed")
        conv_t_done = sem("conv_t_done")
        score_mm = sem("score_mm")
        max_done = sem("max_done")
        exp_done = sem("exp_done")
        attn_done = sem("attn_done")
        attn_t_mm = sem("attn_t_mm")
        attn_t_done = sem("attn_t_done")
        pv_mm = sem("pv_mm")
        out_row_done = sem("out_row_done")
        head_ss_done = sem("head_ss_done")
        head_std = sem("head_std")
        out_normed = sem("out_normed")
        out_t_mm = sem("out_t_mm")
        out_t_done = sem("out_t_done")
        bc1_in = sem("bc1_in")
        bcf_in = sem("bcf_in")
        bc2_in = sem("bc2_in")
        mixout_mm = sem("mixout_mm")
        mix_read = sem("mix_read")
        var_done = sem("var_done")
        std_done = sem("std_done")
        normed = sem("normed")
        h_ready = sem("h_ready")
        h_out = [sem("h_out0"), sem("h_out1")]
        route_t_mm = sem("route_t_mm")
        route_t_done = sem("route_t_done")
        logit_mm = sem("logit_mm")
        logit_max = sem("logit_max")
        logit_exp = sem("logit_exp")
        mask_ready = sem("mask_ready")
        rank_mm = sem("rank_mm")
        table_ready = sem("table_ready")
        slots_ready = sem("slots_ready")
        slot_zeroed = sem("slot_zeroed")
        slot_out = sem("slot_out")
        slot_in = sem("slot_in")
        slot_mm = sem("slot_mm")
        index_ready = sem("index_ready")
        index_now = sem("index_now")
        gathered = sem("gathered")
        tok_mm = sem("tok_mm")
        tok_done = sem("tok_done")
        up_mm = sem("up_mm")
        silu_done = sem("silu_done")
        act_done = sem("act_done")
        act_t_mm = sem("act_t_mm")
        act_t_done = sem("act_t_done")
        y_mm = sem("y_mm")
        y_done = sem("y_done")
        y_out = sem("y_out")
        expert_done = sem("expert_done")
        picked_in = [sem("picked_in0"), sem("picked_in1")]
        picked_read = sem("picked_read")
        var2_done = sem("var2_done")
        std2_done = sem("std2_done")
        normed2 = sem("normed2")
        x_done = sem("x_done")
        final_out = sem("final_out")
        dve_step = sem("dve_step")
        pool_step = sem("pool_step")
        act_step = sem("act_step")

        y_zeroed = sem("y_zeroed")
        pe_held = sem("pe_held")
        pool_held = sem("pool_held")

        n_setup = 8
        xt_per, pr_per, rope_per, qt_per, at_per = 2 * TILES, 3 * TILES, 2 * TILES, 2 * TILES + 2, TILES * HEADS

        block = ctx.enter_context(nc.Block())

        @block.sync
        def _(sp):
            for t in range(1):
                sp.dma_start(c_row[0:8, :], a["c_prompt"].rearrange("a (k p) -> (a k) p", p=P)).then_inc(setup_in, LANDED)
                sp.dma_start(c_row[8:16, :], a["c_sample"].rearrange("a (k p) -> (a k) p", p=P)).then_inc(setup_in, LANDED)
            fills = [0] * SLOTS

            def load(s, dst, src):
                fills[s] += 1
                sp.dma_start(dst, src).then_inc(landed[s], LANDED)

            for l in range(DEPTH):
                w_ada = a["w_ada"][l].rearrange("(k p) c -> p k c", p=P)
                for n in range(ADA_CHUNKS):
                    if n >= SLOTS:
                        sp.wait_ge(ada_mm, 3 * l + (n - SLOTS) // 4 + 1)
                    elif l and n % 3 == 0:
                        sp.wait_ge(expert_done, EXPERTS * l - 1 + n // 3)
                    load(n % SLOTS, by_k(n % SLOTS), w_ada[:, :, n * 512:(n + 1) * 512])
                    if l == 0 and n == 3:
                        sp.dma_start(x[:, 0:4, :], a["x_prompt"][0].rearrange("(t p) d -> p t d", p=P)).then_inc(setup_in, LANDED)
                        sp.dma_start(x[0:DEC, 4, :], a["x_sample"][0]).then_inc(setup_in, LANDED)
                        sp.dma_start(w_router[:, :, :], a["w_router"].rearrange("(k p) e -> p k e", p=P)).then_inc(setup_in, LANDED)
                        sp.dma_start(b_router[:, :], a["b_router"].partition_broadcast(P)).then_inc(setup_in, LANDED)
                        sp.dma_start(rope[:, :, :], a["rope"].rearrange("(t p) c -> p t c", p=P)).then_inc(setup_in, LANDED)
                        sp.dma_start(eps[:, :], a["eps"]).then_inc(setup_in, LANDED)
                w_in = a["w_in"][l].rearrange("(k p) c -> p k c", p=P)
                for n, c in enumerate((3, 4, 0, 1, 2)):
                    if n < 2:
                        sp.wait_ge(ada_mm, 3 * l + 2)
                    elif n < 4:
                        sp.wait_ge(ada_mm, 3 * l + 3)
                    else:
                        sp.wait_ge(u_mm, 4 * l + 4)
                    load(n % 4, by_k(n % 4), w_in[:, :, c * 512:(c + 1) * 512])
                w_out = a["w_out"][l].rearrange("(k p) c -> p k c", p=P)
                load(1, by_k(1), w_out[:, :, 0:512])
                sp.wait_ge(proj_mm, pr_per * l + TILES)
                load(2, by_k(2), w_out[:, :, 512:1024])
                for e in range(EXPERTS):
                    s = 3 * (e % 2)
                    if e == 0:
                        sp.wait_ge(proj_mm, pr_per * (l + 1))
                    elif e == 1:
                        sp.wait_ge(out_t_mm, TILES * (l + 1))
                        sp.wait_ge(out_t_done, TILES * (l + 1))
                        sp.wait_ge(conv_t_done, 4 * (l + 1))
                    else:
                        sp.wait_ge(expert_done, EXPERTS * l + e - 1)
                    load(s, by_k(s), a["w_gate"][l, e].rearrange("(k p) c -> p k c", p=P))
                    if e == 0:
                        sp.wait_ge(mixout_mm, TILES * (l + 1))
                    load(s + 1, by_k(s + 1), a["w_up"][l, e].rearrange("(k p) c -> p k c", p=P))
                    load(s + 2, by_f(s + 2), a["w_down"][l, e].rearrange("(k p) c -> p k c", p=P))
            sp.wait_ge(x_done, TILES * DEPTH)
            sp.dma_start(a["y_prompt"][0].rearrange("(t p) d -> p t d", p=P), x[:, 0:4, :]).then_inc(final_out, LANDED)
            sp.dma_start(a["y_sample"][0], x[0:DEC, 4, :]).then_inc(final_out, LANDED)
            sp.wait_ge(final_out, 2 * LANDED)

        @block.gpsimd
        def _(pool):
            steps = [0]

            def seq(ins):
                steps[0] += 1
                ins.then_inc(pool_step, 1)
                pool.wait_ge(pool_step, steps[0])

            seq(pool.memset(ident[:, :], 0.0))
            seq(pool.affine_select(out=ident[:, :], in_=ident[:, :], compare_op=ALU.not_equal, fill=1.0,
                                   base=0, pattern=[[-1, P]], channel_multiplier=1))
            seq(pool.memset(ones[:, :], 1.0))
            seq(pool.memset(conv_mean[:, :], 1.0 / CONV))
            seq(pool.affine_select(out=before[:, :], in_=ones[:, :], compare_op=ALU.is_gt, fill=0.0,
                                   base=0, pattern=[[1, P]], channel_multiplier=-1))
            four = ones[:, 0:16].rearrange("p (j i) -> p j i", j=4)
            seq(pool.affine_select(out=lower[:, :, :], in_=four, compare_op=ALU.is_gt, fill=0.0,
                                   base=0, pattern=[[1, 4], [-1, 4]], channel_multiplier=0))
            seq(pool.affine_select(out=upper[:, :, :], in_=four, compare_op=ALU.is_gt, fill=0.0,
                                   base=0, pattern=[[-1, 4], [1, 4]], channel_multiplier=0))
            seq(pool.memset(zero_row[:, :], 0.0))
            seq(pool.iota(token_i[:, :], pattern=[[P, TILES]], base=0, channel_multiplier=1))
            seq(pool.memset(reg_v[:, 0:D], 0.0))
            pool.memset(total[:, :], 0.0).then_inc(const_ready, 1)

            for l in range(DEPTH):
                if l:
                    pool.wait_ge(x_done, TILES * l)
                else:
                    pool.wait_ge(setup_dve, 1)
                for j in range(4):
                    src = a["b_ada"][l].rearrange("(r j c) -> j r c", j=4, c=512)[j].partition_broadcast(2)
                    pool.dma_start(b_ada[32 * j:32 * j + 2, :, :], src).then_inc(ada_in, LANDED)
                pool.dma_start(conv_w_row[:, :], a["conv_w"][l]).then_inc(small_in, LANDED)
                pool.dma_start(state_row[:, :], a["state_conv"][l, 0]).then_inc(small_in, LANDED)
                for n, name in enumerate(("conv_b", "conv_ln_g", "conv_ln_b")):
                    pool.dma_start(vec_row[4 * n:4 * n + 4, :], a[name][l].rearrange("(k p) -> k p", p=P)).then_inc(small_in, LANDED)
                pool.dma_start(vec_row[12:13, :], a["subln_g"][l].rearrange("(k p) -> k p", p=P)).then_inc(small_in, LANDED)
                pool.dma_start(lam_qk[:, :, :], a["lambda_qk"][l].partition_broadcast(P)).then_inc(small_in, LANDED)
                pool.dma_start(cache_v[:, :, :], a["cache_v"][l, 0].rearrange("(t p) h c -> p t (h c)", p=P)).then_inc(cache_v_in, LANDED)
                pool.dma_start(slot_dram.rearrange("(r c) a -> r (c a)", c=TM), zero_row[:, :]).then_inc(slot_zeroed, LANDED)
                if l == 0:
                    pool.dma_start(y_dram[EXPERTS * TM:, :].rearrange("(n p) d -> p n d", p=P),
                                   reg_v[:, 0:D].unsqueeze(1).to_broadcast([P, (MAX_TILES - EXPERTS) * TM // P, D])).then_inc(y_zeroed, LANDED)
                pool.wait_ge(mod_ready, 3 * (l + 1))
                for s in range(2):
                    dst = mod_dram[s].rearrange("(r j c) -> j r c", j=4, c=512)
                    pool.dma_start(dst, mod_row[s:s + 97:32, :, :]).then_inc(mod_out, LANDED)
                pool.wait_ge(mod_out, 2 * LANDED * (l + 1))
                for s in range(2):
                    pool.dma_start(mod_cols_row[16 * s:16 * s + 16, :],
                                   mod_dram[s, 0:2 * D].rearrange("(k p) -> k p", p=P)).then_inc(mod_cols_in, LANDED)
                pool.wait_ge(ada_mm, 3 * (l + 1))
                pool.dma_start(cache_k_row[:, :, :],
                               a["cache_k"][l, 0].rearrange("(t p) h m c -> p t (h m c)", p=P)).then_inc(cache_k_in, LANDED)
                pool.wait_ge(new_conv_ready, 2 * (l + 1))
                pool.dma_start(a["conv_prompt"][l, 0], new_conv[0:STATE, 0, :]).then_inc(new_conv_out, LANDED)
                pool.dma_start(a["conv_sample"][l, 0], new_conv[0:STATE, 1, :]).then_inc(new_conv_out, LANDED)
                for t in range(TILES):
                    i = TILES + t
                    pool.wait_ge(proj_act, pr_per * l + i + 1)
                    pool.wait_ge(proj_rope, rope_per * l + i + 1)
                    dst = a["k_sample"][l, 0] if t == 4 else a["k_prompt"][l, 0, t * P:(t + 1) * P]
                    pool.dma_start(dst.rearrange("t h m c -> t (h m c)"),
                                   qk_row[0:ROWS[t], i % 2, :]).then_inc(k_out[i % 2], LANDED)
                for t in range(TILES):
                    pool.wait_ge(proj_act, pr_per * l + 2 * TILES + t + 1)
                    dst = a["v_sample"][l, 0] if t == 4 else a["v_prompt"][l, 0, t * P:(t + 1) * P]
                    pool.dma_start(dst.rearrange("t h c -> t (h c)"), v_row[0:ROWS[t], t, :]).then_inc(v_out, LANDED)
                pool.wait_ge(proj_mm, pr_per * (l + 1))
                for s in range(2):
                    pool.dma_start(gate_bc[:, s, :], mod_dram[s, 2 * D:3 * D].partition_broadcast(P)).then_inc(bc1_in, LANDED)
                pool.dma_start(ln_g_bc, a["ln1_g"][l].partition_broadcast(P)).then_inc(bc1_in, LANDED)
                pool.dma_start(ln_b_bc, a["ln1_b"][l].partition_broadcast(P)).then_inc(bc1_in, LANDED)
                pool.wait_ge(score_mm, at_per * (l + 1))
                for s in range(2):
                    pool.dma_start(shift_bc[:, s, :], mod_dram[s, 3 * D:4 * D].partition_broadcast(P)).then_inc(bcf_in, LANDED)
                    pool.dma_start(scale_bc[:, s, :], mod_dram[s, 4 * D:5 * D].partition_broadcast(P)).then_inc(bcf_in, LANDED)
                pool.wait_ge(bcf_in, 4 * LANDED * (l + 1))
                seq(pool.tensor_scalar(scale_bc[:, :, :], scale_bc[:, :, :], 1.0, 0.0, ALU.add, ALU.add))
                pool.wait_ge(bc1_in, 4 * LANDED * (l + 1))
                for t in range(TILES):
                    r, b, s = ROWS[t], t % 2, t // 4
                    pool.wait_ge(normed, TILES * l + t + 1)
                    seq(pool.tensor_tensor(x[0:r, t, :], norm_row[0:r, b, :], ln_g_bc[0:r, :], ALU.mult))
                    seq(pool.tensor_tensor(x[0:r, t, :], x[0:r, t, :], ln_b_bc[0:r, :], ALU.add))
                    if t >= 2:
                        pool.wait_ge(route_t_mm, 2 * (TILES * l + t - 1))
                        pool.wait_ge(h_out[b], LANDED * (3 * l + t // 2 if b == 0 else 2 * l + t // 2))
                    seq(pool.tensor_tensor(h_row[0:r, b, :], x[0:r, t, :], scale_bc[0:r, s, :], ALU.mult))
                    pool.tensor_tensor(h_row[0:r, b, :], h_row[0:r, b, :], shift_bc[0:r, s, :], ALU.add).then_inc(h_ready, 1)
                    pool.wait_ge(h_ready, TILES * l + t + 1)
                    pool.dma_start(h_dram[t * P:t * P + r, :], h_row[0:r, b, :]).then_inc(h_out[b], LANDED)
                for s in range(2):
                    pool.dma_start(gate_bc[:, s, :], mod_dram[s, 5 * D:6 * D].partition_broadcast(P)).then_inc(bc2_in, LANDED)
                pool.dma_start(ln_g_bc, a["ln2_g"][l].partition_broadcast(P)).then_inc(bc2_in, LANDED)
                pool.dma_start(ln_b_bc, a["ln2_b"][l].partition_broadcast(P)).then_inc(bc2_in, LANDED)
                pool.wait_ge(slots_ready, l + 1)
                pool.wait_ge(slot_zeroed, LANDED * (l + 1))
                for k in range(TOP):
                    for t in range(TILES):
                        pool.indirect_dma_start(slot_dram, bass.IndirectOffsetOnAxis(slot_of[0:ROWS[t], k, t:t + 1], 0),
                                                token_f[0:ROWS[t], t:t + 1], None).then_inc(slot_out, LANDED)
                pool.wait_ge(slot_out, TOP * TILES * LANDED * (l + 1))
                pool.dma_start(slot_row[:, :], slot_dram.rearrange("(r c) a -> r (c a)", c=TM)).then_inc(slot_in, LANDED)
                pool.wait_ge(index_ready, l + 1)
                pool.wait_ge(h_out[0], 3 * LANDED * (l + 1))
                pool.wait_ge(h_out[1], 2 * LANDED * (l + 1))
                pool.wait_ge(table_ready, l + 1)
                tiles = pool.value_load(table[0:1, 32:33], min_val=EXPERTS, max_val=MAX_TILES)
                base = pool.value_load(table[0:1, 33:34], min_val=0, max_val=DEPTH * MAX_TILES)
                with pool.Fori(0, tiles + 1) as i:
                    pool.wait_ge(tok_mm, base + l + i + 1)
                    pool.sem_inc(pool_held, 1)
                    pool.tensor_copy(slot_now[:, :], slot_token[:, bass.ds(i, 1)]).then_inc(index_now, 1)
                    pool.wait_ge(index_now, base + l + i + 1)
                    pool.sem_inc(pool_held, 1)
                    pool.indirect_dma_start(gathered_row, None, h_dram,
                                            bass.IndirectOffsetOnAxis(slot_now[:, 0:1], 0)).then_inc(gathered, LANDED)
                pool.wait_ge(y_out, 2 * LANDED * (base + tiles + 1))
                pool.sem_inc(pool_held, 1)
                pool.wait_ge(bc2_in, 4 * LANDED * (l + 1))
                for t in range(TILES + 1):
                    if t < TILES:
                        r, b = ROWS[t], t % 2
                        if t >= 2:
                            pool.wait_ge(picked_read, TILES * l + t - 1)
                        for k in range(TOP):
                            pool.indirect_dma_start(picked[0:r, b, k, :], None, y_dram,
                                                    bass.IndirectOffsetOnAxis(slot_of[0:r, k, t:t + 1], 0)).then_inc(picked_in[b], LANDED)
                    if t:
                        r, b = ROWS[t - 1], (t - 1) % 2
                        pool.wait_ge(normed2, TILES * l + t)
                        seq(pool.tensor_tensor(x[0:r, t - 1, :], mixed[0:r, b, :], ln_g_bc[0:r, :], ALU.mult))
                        pool.tensor_tensor(x[0:r, t - 1, :], x[0:r, t - 1, :], ln_b_bc[0:r, :], ALU.add).then_inc(x_done, 1)
            for n, s in ((2 * DEPTH, new_conv_out), (2 * DEPTH, k_out[0]), (3 * DEPTH, k_out[1]), (TILES * DEPTH, v_out)):
                pool.wait_ge(s, n * LANDED)

        @block.scalar
        def _(act):
            A = nc.scalar.activation
            act.sem_inc(y_done, 1)
            act.sem_inc(y_out, 2 * LANDED)
            act.wait_ge(setup_in, n_setup * LANDED)
            A(c_silu[:, :], c_row[:, :], ACT.Silu).then_inc(c_silu_ready, 1)
            for l in range(DEPTH):
                act.wait_ge(lam_ready, 2 * l + 1)
                A(lam_e[:, 2:4], lam_e[:, 0:2], ACT.Exp).then_inc(lam_exp, 1)
                act.wait_ge(cols_ready, l + 1)
                for t in range(TILES):
                    r, s = ROWS[t], t // 4
                    act.wait_ge(xt_mm, xt_per * l + 2 * t + 2)
                    for k in range(4):
                        ins = A(h_t[:, 4 + k, COL[t]:COL[t] + r], bank(5)[:, k * P:k * P + r], ACT.Identity,
                                bias=cols[:, 16 * s + 4 + k:16 * s + 5 + k], scale=cols[:, 16 * s + 12 + k:16 * s + 13 + k])
                    ins.then_inc(ht_act, 1)
                for j in range(4):
                    act.wait_ge(u_mm, 4 * l + j + 1)
                    if j >= 2:
                        act.wait_ge(glu_done, 4 * l + j - 1)
                    A(sig[:, j % 2, 0:SEQ], bank(2 * (j % 2) + 1), ACT.Sigmoid)
                    A(sig[:, j % 2, SEQ:NTOK], bank(6 + j % 2)[:, DEC:2 * DEC], ACT.Sigmoid).then_inc(sig_done, 1)

                def leave_t(i):
                    act.wait_ge(qk_t_mm, qt_per * l + i + 1)
                    kind, t = i // TILES, i % TILES
                    r = ROWS[t] if kind < 2 else P
                    if kind == 0:
                        dst = q_t[:, :, COL[t]:COL[t] + r]
                    elif kind == 1 and t < 4:
                        dst = k_t[:, :, t * P:t * P + r]
                    elif kind == 1:
                        dst = ks_t[:, :, PAST:KEYS_S]
                    else:
                        dst = ks_t[:, :, t * P:t * P + P]
                    src = bank(4 + i % 2).rearrange("p (h t) -> p h t", h=HEADS)[:, :, 0:r]
                    A(dst, src, ACT.Copy).then_inc(qk_t_done, 1)

                act.wait_ge(y_zeroed, LANDED)
                for i in range(3 * TILES):
                    t, r = i % TILES, ROWS[i % TILES]
                    act.wait_ge(proj_mm, pr_per * l + i + 1)
                    if i < 2 * TILES:
                        if i >= 2:
                            act.wait_ge(qk_t_mm, qt_per * l + i - 1)
                        if i >= TILES + 2:
                            act.wait_ge(k_out[i % 2], LANDED * ((3 if i % 2 else 2) * l + (i - TILES) // 2))
                        A(qk_row[0:r, i % 2, :], bank(i % 4)[0:r, :], ACT.Copy).then_inc(proj_act, 1)
                    else:
                        A(v_row[0:r, t, :], bank(i % 4)[0:r, :], ACT.Copy).then_inc(proj_act, 1)
                    if 2 <= i < 2 * TILES + 4:
                        if i == 2 * TILES + 2:
                            pass
                        leave_t(i - 2)
                    if i == 2:
                        for b in range(2):
                            act.wait_ge(new_conv_mm, 2 * l + b + 1)
                            A(new_conv[0:STATE, b, :], bank(6 + b)[0:STATE, :], ACT.Copy).then_inc(new_conv_ready, 1)
                    if i == TILES:
                        for j in range(4):
                            act.wait_ge(centred, 4 * l + j + 1)
                            A(glu[:, j, 0:CW], mix_t[:, 4 + j, 0:CW], ACT.Square).then_inc(squared, 1)
                    if i == 2 * TILES:
                        act.wait_ge(conv_stat_mm, 2 * l + 2)
                        A(glu[:, 0, 0:CW].rearrange("p (b c) -> p b c", b=2), pair[3][:, :, 0:HALF], ACT.Sqrt,
                          bias=eps[:, :]).then_inc(conv_std, 1)
                    if i == 2 * TILES + 3:
                        for j in range(4):
                            act.wait_ge(conv_normed, 4 * l + j + 1)
                            A(mix_t[:, 4 + j, 0:CW], mix_t[:, 4 + j, 0:CW], ACT.Silu,
                              bias=cols[:, 40 + j:41 + j], scale=cols[:, 36 + j:37 + j]).then_inc(conv_t_done, 1)

                def exps(i):
                    r, keys, b = ROWS[i // 4], (KEYS_S if i // 4 == 4 else (i // 4 + 1) * P), i % 2
                    act.wait_ge(max_done, at_per * l + i + 1)
                    if i >= 2:
                        act.wait_ge(attn_done, at_per * l + i - 1)
                    for m in range(2):
                        ins = A(prob[0:r, b, m, 0:keys], pair[b][0:r, m, 0:keys], ACT.Exp,
                                bias=neg_max[0:r, b, m:m + 1], scale=SCALE, accum_out=row_sum[0:r, b, m:m + 1])
                    ins.then_inc(exp_done, 1)

                def leave_attn_t(i):
                    t = i // 4
                    act.wait_ge(attn_t_mm, at_per * l + i + 1)
                    if i >= 2:
                        act.wait_ge(pv_mm, at_per * l + i - 1)
                    if t < 4:
                        ins = A(attn_t[:, i % 2, 0:(t + 1) * P], bank(4 + i % 2)[:, 0:(t + 1) * P], ACT.Copy)
                    else:
                        A(attn_t[:, i % 2, 0:2 * P].rearrange("p (k t) -> p k t", k=2)[:, :, 0:DEC],
                          bank(4 + i % 2)[:, 0:2 * P].rearrange("p (k t) -> p k t", k=2)[:, :, 0:DEC], ACT.Copy)
                        ins = A(attn_t[0:DEC, i % 2, 2 * P:2 * P + DEC], bank(4 + i % 2)[0:DEC, 2 * P:2 * P + DEC], ACT.Copy)
                    ins.then_inc(attn_t_done, 1)

                def leave_out(t):
                    act.wait_ge(pv_mm, at_per * l + 4 * t + 4)
                    if t >= 1:
                        act.wait_ge(out_t_mm, TILES * l + t)
                    A(out_row[0:ROWS[t], :], bank(6 + t % 2)[0:ROWS[t], :], ACT.Copy).then_inc(out_row_done, 1)

                def head_sqrt(t):
                    act.wait_ge(head_ss_done, TILES * l + t + 1)
                    A(head_ss[0:ROWS[t], 1, :], head_ss[0:ROWS[t], 0, :], ACT.Sqrt, bias=eps[0:ROWS[t], :],
                      scale=1.0 / P).then_inc(head_std, 1)

                act.wait_ge(new_conv_out, 2 * LANDED * (l + 1))
                exps(0)
                for i in range(at_per + 2):
                    if i + 1 < at_per:
                        exps(i + 1)
                    if i < at_per:
                        leave_attn_t(i)
                    if i >= 4 and i % 4 == 0:
                        leave_out(i // 4 - 1)
                    if i >= 5 and i % 4 == 1:
                        head_sqrt(i // 4 - 1)

                for t in range(TILES + 2):
                    if t < TILES:
                        act.wait_ge(var_done, TILES * l + t + 1)
                        A(std[0:ROWS[t], 0:1], mean_var[0:ROWS[t], 1:2], ACT.Sqrt, bias=eps[0:ROWS[t], :]).then_inc(std_done, 1)
                    if t >= 2:
                        u = t - 2
                        for hf in range(2):
                            act.wait_ge(route_t_mm, 2 * (TILES * l + u) + hf + 1)
                            if u >= 1:
                                act.wait_ge(logit_mm, TILES * l + u)
                            A(route_t[hf][:, :, 0:ROWS[u]],
                              bank(4 + hf).rearrange("p (k t) -> p k t", k=4)[:, :, 0:ROWS[u]], ACT.Copy).then_inc(route_t_done, 1)
                act.wait_ge(logit_max, l + 1)
                A(score[:, :, :], logits[:, :, :], ACT.Exp).then_inc(logit_exp, 1)

                act.wait_ge(table_ready, l + 1)
                tiles = act.value_load(table[0:1, 32:33], min_val=EXPERTS, max_val=MAX_TILES)
                base = act.value_load(table[0:1, 33:34], min_val=0, max_val=DEPTH * MAX_TILES)
                act.wait_ge(tok_mm, base + l + 2)
                A(tok_t[:, :, :], bank(2).rearrange("p (k t) -> p k t", k=KD), ACT.Copy).then_inc(tok_done, 1)
                with act.Fori(0, tiles) as i:
                    for hf in range(2):
                        act.wait_ge(up_mm, (base + i) * 2 + hf + 1)
                        A(silu_g[TM:2 * TM, hf * 256:hf * 256 + 256], bank(hf)[0:TM, 0:256], ACT.Silu).then_inc(silu_done, 1)
                    act.wait_ge(tok_mm, base + l + i + 3)
                    A(tok_t[:, :, :], bank(2).rearrange("p (k t) -> p k t", k=KD), ACT.Copy).then_inc(tok_done, 1)
                    act.wait_ge(y_out, (base + i + 1) * (2 * LANDED))
                    act.wait_ge(y_mm, base + i + 1)
                    A(y_row, bank(4), ACT.Copy).then_inc(y_done, 1)
                    act.wait_ge(y_done, base + i + 2)
                    for n in range(2):
                        act.dma_start(y_dram[bass.ds(i * TM, TM), n * 512:(n + 1) * 512],
                                      y_row[n * TM:(n + 1) * TM, :]).then_inc(y_out, LANDED)
                for t in range(TILES):
                    act.wait_ge(var2_done, TILES * l + t + 1)
                    A(std[0:ROWS[t], 0:1], mean_var[0:ROWS[t], 1:2], ACT.Sqrt, bias=eps[0:ROWS[t], :]).then_inc(std2_done, 1)

        @block.vector
        def _(dve):
            V = nc.vector
            steps = [0]

            def seq(ins):
                steps[0] += 1
                ins.then_inc(dve_step, 1)
                dve.wait_ge(dve_step, steps[0])

            seq(V.memset(reg_m[:, 0:1536], 0.0))
            seq(V.memset(c_t[:, :, :], 0.0))
            seq(V.memset(reset[:, :, :], 1.0))
            seq(V.memset(reset[:, :, 0:1], 0.0))
            seq(V.memset(logits[:, :, :], 0.0))
            V.memset(cnt[:, 5, :], 1.0).then_inc(setup_dve, 1)
            dve.wait_ge(const_ready, 1)
            seq(V.tensor_copy(token_f[:, :], token_i[:, :]))
            dve.wait_ge(c_mm, 1)
            V.tensor_copy(c_t[:, :, 0:2], bank(7)[:, 0:16].rearrange("p (s k) -> p k s", s=2)).then_inc(c_ready, 1)

            def layer_norm_tail(out, src, r, ready, need):
                dve.wait_ge(ready, need)
                seq(V.reciprocal(std[0:r, 1:2], std[0:r, 0:1]))
                return V.tensor_scalar(out, src, mean_var[0:r, 0:1], std[0:r, 1:2], ALU.subtract, ALU.mult)

            def statistics(src, r):
                for hf in range(2):
                    seq(V.bn_stats(stats[0:r, hf, :], src[:, hf * 512:hf * 512 + 512]))
                return V.bn_aggr(mean_var[0:r, :], stats[0:r, :, :])

            for l in range(DEPTH):
                dve.wait_ge(ada_in, 4 * LANDED * (l + 1))
                for n in range(3):
                    dve.wait_ge(ada_mm, 3 * l + n + 1)
                    V.tensor_tensor(mod_row[:, n, :], bank(n), b_ada[:, n, :], ALU.add).then_inc(mod_ready, 1)
                dve.wait_ge(small_in, 7 * LANDED * (l + 1))
                seq(V.tensor_tensor(lam_prod[:, :, :], lam_qk[:, 0::2, :], lam_qk[:, 1::2, :], ALU.mult))
                V.reduce_sum(lam_e[:, 0:2], lam_prod[:, :, :], AX_X).then_inc(lam_ready, 1)
                dve.wait_ge(lam_exp, l + 1)
                seq(V.tensor_tensor(lam_e[:, 4:5], lam_e[:, 3:4], lam_e[:, 2:3], ALU.subtract))
                V.tensor_scalar(lam_e[:, 5:6], lam_e[:, 4:5], -lam_init(l), None, ALU.add).then_inc(lam_ready, 1)
                dve.wait_ge(cols_mm, l + 1)
                seq(V.tensor_copy(cols[:, 0:312], bank(4)[:, 0:312]))
                by_stream = cols[:, 0:32].rearrange("p (s k) -> p s k", s=2)
                seq(V.tensor_scalar(by_stream[:, :, 8:16], by_stream[:, :, 8:16], 1.0, None, ALU.add))
                seq(V.tensor_scalar(cols[:, 44:45], cols[:, 44:45], 1.0 - lam_init(l), None, ALU.mult))
                seq(V.memset(glu[:, :, 0:STATE], 0.0))
                V.tensor_copy(glu[:, :, STATE + SEQ:STATE + SEQ + STATE],
                              cols[:, 192:312].rearrange("p (j t) -> p j t", j=4)).then_inc(cols_ready, 1)
                for t in range(TILES):
                    r, s = ROWS[t], t // 4
                    dve.wait_ge(xt_mm, xt_per * l + 2 * t + 1)
                    if t == 0:
                        dve.wait_ge(cols_ready, l + 1)
                    for k in range(4):
                        ins = V.tensor_scalar(h_t[:, k, COL[t]:COL[t] + r], bank(4)[:, k * P:k * P + r],
                                              cols[:, 16 * s + 8 + k:16 * s + 9 + k], cols[:, 16 * s + k:16 * s + k + 1],
                                              ALU.mult, ALU.add)
                    ins.then_inc(ht_dve, 1)
                for j in range(4):
                    dve.wait_ge(sig_done, 4 * l + j + 1)
                    V.tensor_tensor(glu[:, j, STATE:STATE + SEQ], bank(2 * (j % 2)), sig[:, j % 2, 0:SEQ], ALU.mult)
                    V.tensor_tensor(glu[:, j, GW - DEC:GW], bank(6 + j % 2)[:, 0:DEC], sig[:, j % 2, SEQ:NTOK],
                                    ALU.mult).then_inc(glu_done, 1)
                    dve.wait_ge(glu_done, 4 * l + j + 1)
                    acc = mix_t[:, 4 + j, 0:CW]
                    tap = cols[:, 64 + TAPS * j:64 + TAPS * (j + 1)]
                    if j == 0:
                        dve.wait_ge(mod_out, 2 * LANDED * (l + 1))
                    seq(V.tensor_scalar(acc, glu[:, j, 0:CW], tap[:, 0:1], cols[:, 32 + j:33 + j], ALU.mult, ALU.add))
                    for w in range(1, TAPS):
                        ins = V.scalar_tensor_tensor(out=acc, in0=glu[:, j, w:w + CW], scalar=tap[:, w:w + 1], in1=acc,
                                                     op0=ALU.mult, op1=ALU.add)
                        if w < TAPS - 1:
                            seq(ins)
                    ins.then_inc(conv_done, 1)

                for i in range(2 * TILES):
                    t, r = i % TILES, ROWS[i % TILES]
                    dve.wait_ge(proj_act, pr_per * l + i + 1)
                    src = qk_row[0:r, i % 2, :].rearrange("p (g c) -> p g c", g=8)
                    cos = rope[0:r, t, 0:16].unsqueeze(1).to_broadcast([r, 8, 16])
                    sin = rope[0:r, t, 16:32].unsqueeze(1).to_broadcast([r, 8, 16])
                    V.tensor_tensor(rope_t[0:r, 0, :, :], src[:, :, 0:16], cos, ALU.mult)
                    V.tensor_tensor(rope_t[0:r, 1, :, 0:8], src[:, :, 8:16], sin[:, :, 0:8], ALU.mult)
                    seq(V.tensor_tensor(rope_t[0:r, 1, :, 8:16], src[:, :, 0:8], sin[:, :, 8:16], ALU.mult))
                    V.tensor_tensor(src[:, :, 0:16],
                                    rope_t[0:r, 0, :, :], rope_t[0:r, 1, :, :], ALU.add).then_inc(proj_rope, 1)
                    dve.wait_ge(proj_rope, rope_per * l + i + 1)
                    if i == TILES - 1:
                        dve.wait_ge(conv_stat_mm, 2 * l + 1)
                        for j in range(4):
                            view = mix_t[:, 4 + j, 0:CW].rearrange("p (b c) -> p b c", b=2)
                            V.tensor_tensor(view, view, pair[3][:, :, 0:HALF], ALU.subtract).then_inc(centred, 1)
                dve.wait_ge(conv_std, l + 1)
                seq(V.reciprocal(glu[:, 1, 0:CW], glu[:, 0, 0:CW]))
                for j in range(4):
                    V.tensor_tensor(mix_t[:, 4 + j, 0:CW], mix_t[:, 4 + j, 0:CW], glu[:, 1, 0:CW], ALU.mult).then_inc(conv_normed, 1)

                def maxima(i):
                    t, b = i // 4, i % 2
                    r, keys = ROWS[t], (KEYS_S if t == 4 else (t + 1) * P)
                    dve.wait_ge(score_mm, at_per * l + i + 1)
                    if t < 4:
                        seq(V.memset(pair[b][0:64, :, keys - 64:keys], NEG))
                    seq(V.reduce_max(row_max[0:r, b, :], pair[b][0:r, :, 0:keys], AX_X))
                    V.tensor_scalar(neg_max[0:r, b, :], row_max[0:r, b, :], -SCALE, None, ALU.mult).then_inc(max_done, 1)

                def combine(i):
                    t, b = i // 4, i % 2
                    r, keys = ROWS[t], (KEYS_S if t == 4 else (t + 1) * P)
                    dve.wait_ge(exp_done, at_per * l + i + 1)
                    seq(V.reciprocal(row_inv[0:r, b, :], row_sum[0:r, b, :]))
                    if i >= 2:
                        dve.wait_ge(attn_t_mm, at_per * l + i - 1)
                    V.tensor_scalar(attn[0:r, b, 0:keys], prob[0:r, b, 0, 0:keys], row_inv[0:r, b, 0:1], None, ALU.mult)
                    seq(V.tensor_scalar(row_inv[0:r, b, 1:2], row_inv[0:r, b, 1:2], lam_e[0:r, 5:6], None, ALU.mult))
                    V.scalar_tensor_tensor(out=attn[0:r, b, 0:keys], in0=prob[0:r, b, 1, 0:keys], scalar=row_inv[0:r, b, 1:2],
                                           in1=attn[0:r, b, 0:keys], op0=ALU.mult, op1=ALU.add).then_inc(attn_done, 1)

                def head_squares(t):
                    r = ROWS[t]
                    dve.wait_ge(out_row_done, TILES * l + t + 1)
                    seq(V.tensor_tensor(square[0:r, :], out_row[0:r, :], out_row[0:r, :], ALU.mult))
                    V.reduce_sum(head_ss[0:r, 0, :], square[0:r, :].rearrange("p (h c) -> p h c", h=4), AX_X).then_inc(head_ss_done, 1)

                def head_norm(t):
                    r = ROWS[t]
                    dve.wait_ge(head_std, TILES * l + t + 1)
                    seq(V.reciprocal(head_ss[0:r, 2, :], head_ss[0:r, 1, :]))
                    view = out_row[0:r, :].rearrange("p (h c) -> p h c", h=4)
                    V.tensor_tensor(view, view, head_ss[0:r, 2, :].unsqueeze(2).to_broadcast([r, 4, P]), ALU.mult).then_inc(out_normed, 1)

                def leave_out_t(t):
                    dve.wait_ge(out_t_mm, TILES * l + t + 1)
                    V.tensor_scalar(mix_t[:, 0:4, MCOL[t]:MCOL[t] + ROWS[t]],
                                    bank(6 + t % 2).rearrange("p (h t) -> p h t", h=4)[:, :, 0:ROWS[t]],
                                    cols[:, 44:45], None, ALU.mult).then_inc(out_t_done, 1)

                dve.wait_ge(k_out[0], 2 * LANDED * (l + 1))
                dve.wait_ge(k_out[1], 3 * LANDED * (l + 1))
                maxima(0)
                for i in range(at_per + 3):
                    if i + 1 < at_per:
                        maxima(i + 1)
                    if i < at_per:
                        combine(i)
                    if i >= 4 and i % 4 == 0:
                        head_squares(i // 4 - 1)
                    if i >= 5 and i % 4 == 1:
                        head_norm(i // 4 - 1)
                    if i >= 6 and i % 4 == 2:
                        leave_out_t(i // 4 - 1)

                dve.wait_ge(bc1_in, 4 * LANDED * (l + 1))
                dve.wait_ge(v_out, TILES * LANDED * (l + 1))
                for t in range(TILES):
                    r, b, s = ROWS[t], t % 2, t // 4
                    dve.wait_ge(mixout_mm, TILES * l + t + 1)
                    if t >= 2:
                        dve.wait_ge(h_ready, TILES * l + t - 1)
                    row = norm_row[0:r, b, :]
                    V.tensor_tensor(row.rearrange("p (n c) -> p n c", n=2), pair[b][0:r, :, :],
                                    gate_bc[0:r, s, :].rearrange("p (n c) -> p n c", n=2), ALU.mult).then_inc(mix_read, 1)
                    dve.wait_ge(mix_read, TILES * l + t + 1)
                    seq(V.scalar_tensor_tensor(out=row, in0=x[0:r, t, :], scalar=ALPHA, in1=row, op0=ALU.mult, op1=ALU.add))
                    statistics(row, r).then_inc(var_done, 1)
                    dve.wait_ge(var_done, TILES * l + t + 1)
                    layer_norm_tail(row, row, r, std_done, TILES * l + t + 1).then_inc(normed, 1)

                dve.wait_ge(logit_mm, TILES * (l + 1))
                V.tensor_copy(logits[:, 0:4, :], bank(6)[:, 0:64].rearrange("p (t e) -> p t e", t=4))
                seq(V.tensor_copy(logits[0:DEC, 4, :], bank(6)[0:DEC, 64:80]))
                t_max, t_sum, t_inv = small[:, 0, 0:TILES], small[:, 1, 0:TILES], small[:, 2, 0:TILES]

                def over_e(v):
                    return v.unsqueeze(2).to_broadcast([P, TILES, EXPERTS])

                seq(V.reduce_max(t_max, logits[:, :, :], AX_X))
                V.tensor_tensor(logits[:, :, :], logits[:, :, :], over_e(t_max), ALU.subtract).then_inc(logit_max, 1)
                dve.wait_ge(logit_exp, l + 1)
                seq(V.reduce_sum(t_sum, score[:, :, :], AX_X))
                seq(V.reciprocal(t_inv, t_sum))
                seq(V.tensor_tensor(score[:, :, :], score[:, :, :], over_e(t_inv), ALU.mult))
                seq(V.tensor_tensor(sel[:, :, :], score[:, :, :], b_router[:, :].unsqueeze(1).to_broadcast([P, TILES, EXPERTS]), ALU.add))

                def count_better(out, v, n):
                    shape = [P, n, 4, 4]
                    vi = v.unsqueeze(2).to_broadcast(shape)
                    vj = v.unsqueeze(3).to_broadcast(shape)
                    ge, gt = cmp_ge[:, 0:n, :, :], cmp_gt[:, 0:n, :, :]
                    V.tensor_tensor(ge, vi, vj, ALU.is_ge)
                    seq(V.tensor_tensor(gt, vi, vj, ALU.is_gt))
                    V.tensor_tensor(ge, ge, lower[:, :, :].unsqueeze(1).to_broadcast(shape), ALU.mult)
                    seq(V.tensor_tensor(gt, gt, upper[:, :, :].unsqueeze(1).to_broadcast(shape), ALU.mult))
                    seq(V.tensor_tensor(ge, ge, gt, ALU.add))
                    seq(V.reduce_sum(out, ge, AX_X))

                by_group = "p t (g i) -> p (t g) i"
                sel_g = sel[:, :, :].rearrange(by_group, g=GROUPS)
                worse_g = worse[:, :, :].rearrange(by_group, g=GROUPS)
                mask_g = mask[:, :, :].rearrange(by_group, g=GROUPS)
                count_better(worse_g, sel_g, TILES * GROUPS)
                seq(V.tensor_scalar(mask_g, worse_g, float(TOP), None, ALU.is_lt))
                seq(V.tensor_tensor(worse_g, mask_g, sel_g, ALU.mult))
                group_score, group_rank = small[:, 3, :], small[:, 4, :]
                seq(V.reduce_sum(group_score, worse_g, AX_X))
                count_better(group_rank.rearrange("p (t g) -> p t g", t=TILES), group_score.rearrange("p (t g) -> p t g", t=TILES), TILES)
                seq(V.tensor_scalar(group_rank, group_rank, 1.0, None, ALU.is_lt))
                seq(V.tensor_tensor(mask_g, mask_g, group_rank.unsqueeze(2).to_broadcast([P, TILES * GROUPS, PER_GROUP]), ALU.mult))
                V.memset(mask[DEC:P, 4, :], 0.0).then_inc(mask_ready, 1)
                dve.wait_ge(mask_ready, l + 1)
                seq(V.tensor_tensor_scan(worse[:, :, :].rearrange("p t e -> p (t e)"), reset[:, :, :].rearrange("p t e -> p (t e)"),
                                         mask[:, :, :].rearrange("p t e -> p (t e)"), 0.0, ALU.mult, ALU.add))
                for k in range(TOP):
                    ins = V.scalar_tensor_tensor(out=picks[:, 2 + k, :, :], in0=worse[:, :, :], scalar=float(k + 1), in1=mask[:, :, :],
                                                 op0=ALU.is_equal, op1=ALU.mult)
                seq(ins)
                dve.wait_ge(rank_mm, l + 1)
                seq(V.tensor_scalar(cnt[:, 0, :], bank(7)[:, 80:96], float(TM - 1), None, ALU.add))
                seq(V.tensor_copy(cnt_i[:, 0, :], cnt[:, 0, :]))
                seq(V.tensor_scalar(cnt_i[:, 1, :], cnt_i[:, 0, :], TM.bit_length() - 1, None, ALU.arith_shift_right))
                seq(V.tensor_copy(cnt[:, 1, :], cnt_i[:, 1, :]))
                seq(V.tensor_scalar(cnt[:, 1, :], cnt[:, 1, :], 1.0, None, ALU.max))
                seq(V.tensor_tensor_scan(cnt[:, 2, :], cnt[:, 5, :], cnt[:, 1, :], 0.0, ALU.mult, ALU.add))
                seq(V.tensor_tensor(cnt[:, 3, :], cnt[:, 2, :], cnt[:, 1, :], ALU.subtract))
                V.tensor_copy(table[:, 0:16], cnt[:, 1, :])
                V.tensor_copy(table[:, 16:32], cnt[:, 3, :])
                V.tensor_copy(table[:, 32:33], cnt[:, 2, 15:16])
                seq(V.tensor_copy(table[:, 33:34], total[:, :]))
                V.tensor_tensor(total[:, :], total[:, :], cnt[:, 2, 15:16], ALU.add).then_inc(table_ready, 1)
                seq(V.tensor_scalar(cnt[:, 4, :], cnt[:, 3, :], float(TM), None, ALU.mult))
                seq(V.tensor_tensor(sel[:, :, :], bank(7)[:, 0:80].rearrange("p (t e) -> p t e", t=TILES),
                                    cnt[:, 4, :].unsqueeze(1).to_broadcast([P, TILES, EXPERTS]), ALU.add))
                V.tensor_tensor(picks[:, 0, :, :], picks[:, 2, :, :], sel[:, :, :], ALU.mult)
                seq(V.tensor_tensor(picks[:, 1, :, :], picks[:, 3, :, :], sel[:, :, :], ALU.mult))
                V.tensor_tensor(picks[:, 2, :, :], picks[:, 2, :, :], score[:, :, :], ALU.mult)
                seq(V.tensor_tensor(picks[:, 3, :, :], picks[:, 3, :, :], score[:, :, :], ALU.mult))
                seq(V.reduce_sum(pick[:, :, :], picks[:, :, :, :], AX_X))
                V.tensor_copy(slot_of[:, :, :], pick[:, 0:2, :]).then_inc(slots_ready, 1)
                seq(V.tensor_tensor(t_sum, pick[:, 2, :], pick[:, 3, :], ALU.add))
                seq(V.tensor_scalar(t_sum[DEC:P, 4:5], t_sum[DEC:P, 4:5], 1.0, None, ALU.add))
                seq(V.reciprocal(t_inv, t_sum))
                for k in range(TOP):
                    seq(V.tensor_tensor(pick[:, 2 + k, :], pick[:, 2 + k, :], t_inv, ALU.mult))
                dve.wait_ge(slot_mm, l + 1)
                V.tensor_copy(slot_token[:, :], bank(5)[0:TM, 0:MAX_TILES + 1]).then_inc(index_ready, 1)

                tiles = dve.value_load(table[0:1, 32:33], min_val=EXPERTS, max_val=MAX_TILES)
                base = dve.value_load(table[0:1, 33:34], min_val=0, max_val=DEPTH * MAX_TILES)
                with dve.Fori(0, tiles) as i:
                    for hf in range(2):
                        c = slice(hf * 256, hf * 256 + 256)
                        dve.wait_ge(silu_done, (base + i) * 2 + hf + 1)
                        V.tensor_tensor(act_row[0:TM, c], silu_g[TM:2 * TM, c], bank(hf)[TM:2 * TM, 0:256], ALU.mult).then_inc(act_done, 1)
                    for hf in range(2):
                        dve.wait_ge(act_t_mm, (base + i) * 2 + hf + 1)
                        V.tensor_copy(act_t[:, 2 * hf:2 * hf + 2, :],
                                      bank((3, 5)[hf])[:, 0:2 * TM].rearrange("p (f t) -> p f t", f=2)).then_inc(act_t_done, 1)

                dve.wait_ge(bc2_in, 4 * LANDED * (l + 1))
                for t in range(TILES):
                    r, b, s = ROWS[t], t % 2, t // 4
                    dve.wait_ge(picked_in[b], 2 * LANDED * ((2 if b else 3) * l + t // 2 + 1))
                    if t >= 2:
                        dve.wait_ge(x_done, TILES * l + t - 1)
                    row = mixed[0:r, b, :]
                    seq(V.tensor_scalar(row, picked[0:r, b, 0, :], pick[0:r, 2, t:t + 1], None, ALU.mult))
                    V.scalar_tensor_tensor(out=row, in0=picked[0:r, b, 1, :], scalar=pick[0:r, 3, t:t + 1], in1=row,
                                           op0=ALU.mult, op1=ALU.add).then_inc(picked_read, 1)
                    dve.wait_ge(picked_read, TILES * l + t + 1)
                    seq(V.tensor_tensor(row, row, gate_bc[0:r, s, :], ALU.mult))
                    seq(V.scalar_tensor_tensor(out=row, in0=x[0:r, t, :], scalar=ALPHA, in1=row, op0=ALU.mult, op1=ALU.add))
                    statistics(row, r).then_inc(var2_done, 1)
                    dve.wait_ge(var2_done, TILES * l + t + 1)
                    layer_norm_tail(row, row, r, std2_done, TILES * l + t + 1).then_inc(normed2, 1)

        @block.tensor
        def _(pe):
            mm, tr = nc.tensor.matmul, nc.tensor.transpose
            fills = [0] * SLOTS

            def weights(s):
                fills[s] += 1
                pe.wait_ge(landed[s], LANDED * fills[s])

            pe.sem_inc(tok_mm, 1)
            pe.wait_ge(const_ready, 1)
            pe.wait_ge(c_silu_ready, 1)
            tr(bank(7)[:, 0:16], c_silu[:, :], ident[0:16, 0:16]).then_inc(c_mm, 1)
            pe.wait_ge(c_ready, 1)
            for l in range(DEPTH):
                for n in range(3):
                    s4 = [(4 * n + j) % SLOTS for j in range(4)]
                    for s in s4:
                        weights(s)
                    for k in range(KD):
                        for j in range(4):
                            ins = mm(bank(n)[32 * j:32 * j + 32, :], c_t[:, k, :], by_k(s4[j])[:, k, :],
                                     start=(k == 0), stop=(k == KD - 1))
                    ins.then_inc(ada_mm, 1)
                pe.wait_ge(mod_cols_in, 2 * LANDED * (l + 1))
                pe.wait_ge(small_in, 7 * LANDED * (l + 1))
                c = bank(4)
                tr(c[:, 0:32], mod_cols_row[:, :], ident[0:32, 0:32])
                tr(c[:, 32:45], vec_row[:, :], ident[0:13, 0:13])
                tr(c[:, 45:64], ident[0:19, :], ident[0:19, 0:19])
                for j in range(4):
                    tr(c[:, 64 + TAPS * j:64 + TAPS * (j + 1)], conv_w_row[:, j * P:(j + 1) * P], ident[0:TAPS, 0:TAPS])
                tr(c[:, 188:192], ident[0:4, :], ident[0:4, 0:4])
                for j in range(4):
                    ins = tr(c[:, 192 + STATE * j:192 + STATE * (j + 1)], state_row[:, j * P:(j + 1) * P], ident[0:STATE, 0:STATE])
                ins.then_inc(cols_mm, 1)
                if l == 0:
                    pe.wait_ge(setup_in, n_setup * LANDED)
                for t in range(TILES):
                    r = ROWS[t]
                    for hf in range(2):
                        if hf == 0 and t == 0:
                            pe.wait_ge(cols_ready, l + 1)
                        if t:
                            pe.wait_ge((ht_dve, ht_act)[hf], TILES * l + t)
                        for k in range(4):
                            c0 = (4 * hf + k) * P
                            ins = tr(bank(4 + hf)[:, k * P:k * P + r], x[0:r, t, c0:c0 + P], ident[0:r, 0:r])
                        ins.then_inc(xt_mm, 1)
                pe.wait_ge(ht_dve, TILES * (l + 1))
                pe.wait_ge(ht_act, TILES * (l + 1))
                weights(0)
                weights(1)
                for j in range(4):
                    if j >= 2:
                        pe.wait_ge(glu_done, 4 * l + j - 1)
                    for part, s in ((1, 1), (0, 0)):
                        for k in range(KD):
                            mm(bank(2 * (j % 2) + part), by_k(s)[:, k, j * P:(j + 1) * P], h_t[:, k, 0:SEQ],
                               start=(k == 0), stop=(k == KD - 1))
                        for k in range(KD):
                            ins = mm(bank(6 + j % 2)[:, part * DEC:(part + 1) * DEC], by_k(s)[:, k, j * P:(j + 1) * P],
                                     h_t[:, k, SEQ:NTOK], start=(k == 0), stop=(k == KD - 1))
                    ins.then_inc(u_mm, 1)

                def project(i):
                    t, r, s = i % TILES, ROWS[i % TILES], (2, 3, 0)[i // TILES]
                    if t == 0:
                        weights(s)
                    if i < 4:
                        pe.wait_ge(glu_done, 4 * l + 4)
                    else:
                        pe.wait_ge(proj_act, pr_per * l + i - 3)
                    for k in range(KD):
                        ins = mm(bank(i % 4)[0:r, :], h_t[:, k, COL[t]:COL[t] + r], by_k(s)[:, k, :],
                                 start=(k == 0), stop=(k == KD - 1))
                    ins.then_inc(proj_mm, 1)

                def turn(i):
                    if i >= 2:
                        pe.wait_ge(qk_t_done, qt_per * l + i - 1)
                    if i < 2 * TILES:
                        r = ROWS[i % TILES]
                        pe.wait_ge(proj_act, pr_per * l + i + 1)
                        pe.wait_ge(proj_rope, rope_per * l + i + 1)
                        src = qk_row[0:r, i % 2, :]
                    else:
                        r = P
                        pe.wait_ge(cache_k_in, LANDED * (l + 1))
                        src = cache_k_row[:, i - 2 * TILES, :]
                    for h in range(HEADS):
                        ins = tr(bank(4 + i % 2)[:, h * P:h * P + r], src[:, h * P:(h + 1) * P], ident[0:r, 0:r])
                    ins.then_inc(qk_t_mm, 1)

                for i in range(3 * TILES):
                    project(i)
                    if 2 <= i < qt_per + 2:
                        turn(i - 2)
                    if i == 2:
                        for b, c0 in enumerate((SEQ, GW - STATE)):
                            for j in range(4):
                                ins = tr(bank(6 + b)[0:STATE, j * P:(j + 1) * P], glu[:, j, c0:c0 + STATE], ident[:, :])
                            ins.then_inc(new_conv_mm, 1)
                    if i == TILES - 1:
                        pe.wait_ge(conv_done, 4 * (l + 1))
                        pe.wait_ge(new_conv_ready, 2 * (l + 1))
                        for b in range(2):
                            for j in range(4):
                                ins = mm(pair[3][:, b, 0:HALF], conv_mean[:, :], mix_t[:, 4 + j, b * HALF:(b + 1) * HALF],
                                         start=(j == 0), stop=(j == 3))
                        ins.then_inc(conv_stat_mm, 1)
                    if i == 2 * TILES - 1:
                        pe.wait_ge(squared, 4 * (l + 1))
                        for b in range(2):
                            for j in range(4):
                                ins = mm(pair[3][:, b, 0:HALF], conv_mean[:, :], glu[:, j, b * HALF:(b + 1) * HALF],
                                         start=(j == 0), stop=(j == 3))
                        ins.then_inc(conv_stat_mm, 1)

                def scores(i):
                    t, h, b = i // 4, i % 4, i % 2
                    r, keys = ROWS[t], (KEYS_S if t == 4 else (t + 1) * P)
                    kt = ks_t if t == 4 else k_t
                    if i >= 2:
                        pe.wait_ge(exp_done, at_per * l + i - 1)
                    for m in range(2):
                        ins = mm(pair[b][0:r, m, 0:keys], q_t[64 * m:64 * m + 64, h, COL[t]:COL[t] + r],
                                 kt[64 * m:64 * m + 64, h, 0:keys], start=True, stop=True)
                    ins.then_inc(score_mm, 1)

                def key_blocks(t):
                    if t < 4:
                        return [(n * P, P, v_row[:, n, :]) for n in range(t + 1)]
                    return [(0, P, cache_v[:, 0, :]), (P, P, cache_v[:, 1, :]), (2 * P, DEC, v_row[0:DEC, 4, :])]

                def turn_attn(i):
                    t, b = i // 4, i % 2
                    r = ROWS[t]
                    pe.wait_ge(attn_done, at_per * l + i + 1)
                    if i >= 2:
                        pe.wait_ge(attn_t_done, at_per * l + i - 1)
                    for c0, w, _ in key_blocks(t):
                        ins = tr(bank(4 + b)[0:w, c0:c0 + r], attn[0:r, b, c0:c0 + w], ident[0:r, 0:r])
                    ins.then_inc(attn_t_mm, 1)

                def values(i):
                    t, h = i // 4, i % 4
                    r = ROWS[t]
                    pe.wait_ge(attn_t_done, at_per * l + i + 1)
                    if t == 4 and h == 0:
                        pe.wait_ge(cache_v_in, LANDED * (l + 1))
                    if h == 0 and t >= 2:
                        pe.wait_ge(out_t_done, TILES * l + t - 1)
                    blocks = key_blocks(t)
                    for n, (c0, w, v) in enumerate(blocks):
                        ins = mm(bank(6 + t % 2)[0:r, h * P:(h + 1) * P], attn_t[0:w, i % 2, c0:c0 + r], v[:, h * P:(h + 1) * P],
                                 start=(n == 0), stop=(n == len(blocks) - 1))
                    ins.then_inc(pv_mm, 1)

                def turn_out(t):
                    r = ROWS[t]
                    pe.wait_ge(out_normed, TILES * l + t + 1)
                    for h in range(HEADS):
                        ins = tr(bank(6 + t % 2)[:, h * P:h * P + r], out_row[0:r, h * P:(h + 1) * P], ident[0:r, 0:r])
                    ins.then_inc(out_t_mm, 1)

                pe.wait_ge(qk_t_done, qt_per * (l + 1))
                pe.wait_ge(proj_act, pr_per * (l + 1))
                pe.wait_ge(conv_std, l + 1)
                scores(0)
                for i in range(at_per + 3):
                    if i + 1 < at_per:
                        scores(i + 1)
                    if i < at_per:
                        turn_attn(i)
                    if 1 <= i <= at_per:
                        values(i - 1)
                    if i >= 6 and i % 4 == 2:
                        turn_out(i // 4 - 1)

                weights(1)
                weights(2)
                pe.wait_ge(conv_t_done, 4 * (l + 1))
                for t in range(TILES + 3):
                    if t < TILES:
                        r, b = ROWS[t], t % 2
                        pe.wait_ge(out_t_done, TILES * l + t + 1)
                        if t >= 2:
                            pe.wait_ge(mix_read, TILES * l + t - 1)
                        for n in range(2):
                            for k in range(KD):
                                ins = mm(pair[b][0:r, n, :], mix_t[:, k, MCOL[t]:MCOL[t] + r], by_k(1 + n)[:, k, :],
                                         start=(k == 0), stop=(k == KD - 1))
                        ins.then_inc(mixout_mm, 1)
                    if t >= 3:
                        u = t - 3
                        pe.wait_ge(route_t_done, 2 * (TILES * l + u + 1))
                        for k in range(KD):
                            ins = mm(bank(6)[0:ROWS[u], u * EXPERTS:(u + 1) * EXPERTS], route_t[k // 4][:, k % 4, 0:ROWS[u]],
                                     w_router[:, k, :], start=(k == 0), stop=(k == KD - 1))
                        ins.then_inc(logit_mm, 1)
                    if 2 <= t < TILES + 2:
                        u = t - 2
                        pe.wait_ge(h_ready, TILES * l + u + 1)
                        for hf in range(2):
                            if u >= 1:
                                pe.wait_ge(route_t_done, 2 * (TILES * l + u - 1) + hf + 1)
                            for k in range(4):
                                c0 = (4 * hf + k) * P
                                ins = tr(bank(4 + hf)[:, k * P:k * P + ROWS[u]], h_row[0:ROWS[u], u % 2, c0:c0 + P],
                                         ident[0:ROWS[u], 0:ROWS[u]])
                            ins.then_inc(route_t_mm, 1)
                pe.wait_ge(mask_ready, l + 1)
                for t in range(TILES):
                    for u in range(t + 1):
                        mm(bank(7)[:, t * EXPERTS:(t + 1) * EXPERTS], (ones if u < t else before)[:, :], mask[:, u, :],
                           start=(u == 0), stop=(u == t))
                for u in range(TILES):
                    ins = mm(bank(7)[:, 80:96], ones[:, :], mask[:, u, :], start=(u == 0), stop=(u == TILES - 1))
                ins.then_inc(rank_mm, 1)
                pe.wait_ge(slot_in, LANDED * (l + 1))
                tr(bank(5)[0:TM, 0:MAX_TILES + 1], slot_row[:, :], ident[0:MAX_TILES + 1, 0:MAX_TILES + 1]).then_inc(slot_mm, 1)

                pe.wait_ge(table_ready, l + 1)
                base = pe.value_load(table[0:1, 33:34], min_val=0, max_val=DEPTH * MAX_TILES)

                def turn_tokens():
                    for k in range(KD):
                        ins = tr(bank(2)[:, k * TM:(k + 1) * TM], gathered_row[:, k * P:(k + 1) * P], ident[0:TM, 0:TM])
                    ins.then_inc(tok_mm, 1)

                pe.wait_ge(index_ready, l + 1)
                pe.wait_ge(gathered, (base + l + 1) * LANDED)
                pe.sem_inc(pe_held, 1)
                turn_tokens()
                for e in range(EXPERTS):
                    s = 3 * (e % 2)
                    for n in range(3):
                        weights(s + n)
                    n_tiles = pe.value_load(table[0:1, e:e + 1], min_val=1, max_val=NTOK // TM)
                    start = pe.value_load(table[0:1, 16 + e:17 + e], min_val=0, max_val=MAX_TILES - 1)
                    with pe.Fori(0, n_tiles) as g:
                        i = base + start + g
                        pe.wait_ge(tok_done, i + l + 1)
                        for hf in range(2):
                            for k in range(KD):
                                for n in range(2):
                                    ins = mm(bank(hf)[n * TM:(n + 1) * TM, 0:256], tok_t[:, k, :],
                                             by_k(s + n)[:, k, hf * 256:hf * 256 + 256], start=(k == 0), stop=(k == KD - 1))
                            ins.then_inc(up_mm, 1)
                        pe.wait_ge(gathered, (i + l + 2) * LANDED)
                        pe.sem_inc(pe_held, 1)
                        turn_tokens()

                        def turn_act(hf):
                            pe.wait_ge(act_done, i * 2 + hf + 1)
                            pe.sem_inc(pe_held, 1)
                            for f in range(2):
                                c0 = (2 * hf + f) * P
                                ins = tr(bank((3, 5)[hf])[:, f * TM:(f + 1) * TM], act_row[0:TM, c0:c0 + P], ident[0:TM, 0:TM])
                            ins.then_inc(act_t_mm, 1)

                        def down(hf):
                            pe.wait_ge(act_t_done, i * 2 + hf + 1)
                            for f in range(2 * hf, 2 * hf + 2):
                                for n in range(2):
                                    ins = mm(bank(4)[n * TM:(n + 1) * TM, :], act_t[:, f, :], by_f(s + 2)[:, f, n * 512:(n + 1) * 512],
                                             start=(f == 0), stop=(f == 3))
                            return ins

                        turn_act(0)
                        pe.wait_ge(y_done, i + 1)
                        down(0)
                        turn_act(1)
                        down(1).then_inc(y_mm, 1)
                    pe.drain().then_inc(expert_done, 1)
                tiles = pe.value_load(table[0:1, 32:33], min_val=EXPERTS, max_val=MAX_TILES)
                pe.wait_ge(tok_done, base + tiles + l + 1)
                pe.wait_ge(y_done, base + tiles + 1)
                pe.sem_inc(pe_held, 1)


_INS = ["x_prompt", "x_sample", "cache_k", "cache_v", "state_conv", "c_prompt", "c_sample", "w_ada", "b_ada", "w_in",
        "lambda_qk", "subln_g", "conv_w", "conv_b", "conv_ln_g", "conv_ln_b", "w_out", "ln1_g", "ln1_b", "ln2_g", "ln2_b",
        "w_router", "b_router", "w_gate", "w_up", "w_down"]
_OUTS = [("y_prompt", (1, SEQ, D)), ("y_sample", (1, DEC, D)),
         ("k_prompt", (DEPTH, 1, SEQ, HEADS, 2, HD)), ("v_prompt", (DEPTH, 1, SEQ, HEADS, 2 * HD)),
         ("conv_prompt", (DEPTH, 1, STATE, CONV)),
         ("k_sample", (DEPTH, 1, DEC, HEADS, 2, HD)), ("v_sample", (DEPTH, 1, DEC, HEADS, 2 * HD)),
         ("conv_sample", (DEPTH, 1, STATE, CONV))]


def rope_table():
    half = 8
    inv = np.power(np.float32(500000.0), -np.arange(half, dtype=np.float32) * np.float32(2.0) / np.float32(16))
    pos = np.concatenate([np.arange(SEQ), PAST + np.arange(DEC), np.zeros(TILES * P - NTOK)]).astype(np.float32)
    ang = pos[:, None] * inv[None, :].astype(np.float32)
    cos, sin = np.cos(ang), np.sin(ang)
    return np.concatenate([cos, cos, -sin, sin], 1).astype(np.float32)


def kernel(**inputs):
    import concourse.bacc as bacc
    from concourse.bass_utils import run_bass_kernel_spmd

    nc = bacc.Bacc("TRN2", target_bir_lowering=False, num_devices=1)
    arrays, aps = {}, {}
    constants = {"rope": rope_table(), "eps": np.full((P, 1), EPS, np.float32)}
    for name in _INS + list(constants):
        v = np.ascontiguousarray(constants[name] if name in constants else inputs[name])
        arrays[f"in_{name}"] = v
        aps[name] = nc.dram_tensor(f"in_{name}", v.shape, F32, kind="ExternalInput").ap()
    for name, shape in _OUTS:
        aps[name] = nc.dram_tensor(f"out_{name}", shape, F32, kind="ExternalOutput").ap()
    build(nc, aps)
    r = run_bass_kernel_spmd(nc, [arrays], core_ids=[0])
    return tuple(r.results[0][f"out_{name}"] for name, _ in _OUTS)
```

```python
import math
from contextlib import ExitStack

import concourse.bass as bass
import numpy as np
from concourse import mybir

ALU = mybir.AluOpType
ACT = mybir.ActivationFunctionType
F32 = mybir.dt.float32
I32 = mybir.dt.int32
AX_X = mybir.AxisListType.X

P = 128
D = 1024
DEPTH = 2
SEQ = 512
DEC = 64
PAST = 256
HEADS = 4
HD = 64
CONV = 512
TAPS = 31
STATE = TAPS - 1
DVE_TAPS = TAPS - 9
POOL_TAPS = TAPS - DVE_TAPS
EXPERTS = 16
GROUPS = 4
PER_GROUP = EXPERTS // GROUPS
TOP = 2
FE = 512
EPS = 1e-5
ALPHA = (2 * DEPTH) ** 0.25
SCALE = HD ** -0.5
NEG = -1e30
IN_COLS = 2560

KD = D // P
NTOK = SEQ + DEC
TILES = 5
ROWS = [P, P, P, P, DEC]
COL = [0, 128, 256, 384, 512]
GAP = SEQ + STATE
MCOL = [0, 128, 256, 384, GAP]
MW = 640
CW = GAP + DEC
HALF = CW // 2
GW = SEQ + DEC + 2 * STATE
KEYS_S = PAST + DEC
ADA_CHUNKS = 6 * D // 512
CHUNK_W = KD * 512
SLOTS = 6
ALL_SLOTS = SLOTS + 3
ADA_SLOTS = [[2, 3, 6, 8] * 3,
             [0, 1, 2, 6, 2, 6, 3, 8, 2, 6, 3, 8]]
ADA_BANK = [6, 4, 5]
EXPERT_SLOTS = [(3, 4, 5), (0, 1, 2), (6, 7, 8)]
TM = 64
MAX_TILES = EXPERTS + TOP * NTOK // TM
LANDED = 16


def lam_init(layer):
    return 0.8 - 0.6 * math.exp(-0.3 * layer)


def build(nc, a):
    with ExitStack() as ctx:
        def sb(name, shape, dt=F32):
            return ctx.enter_context(nc.sbuf_tensor(name, shape, dt))

        def sem(name):
            return ctx.enter_context(nc.semaphore(name))

        mod_dram = nc.dram_tensor("mod_scratch", (2, 6 * D), F32, kind="Internal").ap()
        h_dram = nc.dram_tensor("h_scratch", (NTOK, D), F32, kind="Internal").ap()
        slot_dram = nc.dram_tensor("slot_scratch", ((MAX_TILES + 1) * TM, 1), F32, kind="Internal").ap()
        y_dram = nc.dram_tensor("y_scratch", (MAX_TILES * TM, D), F32, kind="Internal").ap()

        ring = sb("ring", [P, SLOTS * CHUNK_W])
        x = sb("x", [P, TILES, D])
        reg_h = sb("reg_h", [P, KD * NTOK])
        reg_m = sb("reg_m", [P, KD * MW])
        reg_q = sb("reg_q", [P, HEADS * (NTOK + SEQ)])
        reg_v = sb("reg_v", [P, HEADS * KEYS_S + TILES * 512 + 2 * 512])

        def slot(s):
            if s < SLOTS:
                return ring[:, s * CHUNK_W:(s + 1) * CHUNK_W]
            return (reg_q, reg_h, reg_v)[s - SLOTS][:, 0:CHUNK_W]

        def by_k(s):
            return slot(s).rearrange("p (k c) -> p k c", k=KD)

        def by_f(s):
            return slot(s).rearrange("p (k c) -> p k c", k=FE // P)

        o = 4 * CHUNK_W
        glu = ring[:, o:o + 4 * GW].rearrange("p (j c) -> p j c", j=4)
        o += 4 * GW
        q_pad = ring[:, o - 4 * GW:o - 4 * GW + 1024].rearrange("p (b m t) -> p b m t", b=4, m=2)
        qk_row = ring[:, o:o + 1024].rearrange("p (b c) -> p b c", b=2)
        square = ring[:, o:o + 512]
        o += 1024
        prob = ring[:, o:o + 2048].rearrange("p (b m c) -> p b m c", b=2, m=2)
        cache_k_row = ring[:, o:o + 1024].rearrange("p (b c) -> p b c", b=2)
        sig = ring[:, o + 1024:o + 1024 + 2 * NTOK].rearrange("p (b c) -> p b c", b=2)
        new_conv = ring[:, o + 1024 + 2 * NTOK:o + 1024 + 2 * NTOK + 1024].rearrange("p (b c) -> p b c", b=2)
        o += 2048
        attn = ring[:, o:o + 1024].rearrange("p (b c) -> p b c", b=2)
        o += 1024
        attn_t = ring[:, o:o + 1024].rearrange("p (b c) -> p b c", b=2)
        o += 1024
        out_row = ring[:, o:o + 512]
        scaled = [ring[:, at:at + CW] for at in (o - 4096 - 1024 + n * CW for n in range(3))]
        pool_sum = scaled[2]
        odd_sum = ring[:, o - 600:o - 600 + CW]
        assert o + 512 <= SLOTS * CHUNK_W

        h_t = reg_h[:, :].rearrange("p (k t) -> p k t", k=KD)
        gate_bc = reg_h[:, 0:2 * D].rearrange("p (s c) -> p s c", s=2)
        ln_g_bc = reg_h[:, 2 * D:3 * D]
        ln_b_bc = reg_h[:, 3 * D:4 * D]
        route_t = [reg_h[:, 4096:4608].rearrange("p (k t) -> p k t", k=4),
                   reg_v[:, 4096:4608].rearrange("p (k t) -> p k t", k=4)]

        mix_t = reg_m[:, :].rearrange("p (k t) -> p k t", k=KD)
        mod_row = reg_m[:, 0:1536].rearrange("p (r c) -> p r c", r=3)
        zeros = reg_m[:, 4096:4096 + D]
        gathered_row = reg_m[0:TM, 1536:2560]
        tok_t = reg_m[:, 2560:3072].rearrange("p (k t) -> p k t", k=KD)
        silu_g = reg_m[:, 3072:3584]
        act_row = reg_m[:, 3584:4096]
        act_t = reg_m[:, 4096:4352].rearrange("p (f t) -> p f t", f=4)
        y_row = reg_m[:, 4352:4864]
        mixed = reg_m[:, 1536:3584].rearrange("p (b c) -> p b c", b=2)

        o = 1536
        sel = reg_m[:, o:o + 80].rearrange("p (t e) -> p t e", t=TILES)
        worse = reg_m[:, o + 80:o + 160].rearrange("p (t e) -> p t e", t=TILES)
        cmp_ge = reg_m[:, o + 160:o + 480].rearrange("p (g j i) -> p g j i", j=4, i=4)
        cmp_gt = reg_m[:, o + 480:o + 800].rearrange("p (g j i) -> p g j i", j=4, i=4)
        picks = reg_m[:, o + 800:o + 1120].rearrange("p (n t e) -> p n t e", n=4, t=TILES)

        q_t = reg_q[:, 0:HEADS * NTOK].rearrange("p (h t) -> p h t", h=HEADS)
        k_t = reg_q[:, HEADS * NTOK:].rearrange("p (h t) -> p h t", h=HEADS)
        scale_bc = reg_q[:, 0:2048].rearrange("p (s c) -> p s c", s=2)
        shift_bc = reg_q[:, 2048:4096].rearrange("p (s c) -> p s c", s=2)

        ks_t = reg_v[:, 0:HEADS * KEYS_S].rearrange("p (h t) -> p h t", h=HEADS)
        v_row = reg_v[:, HEADS * KEYS_S:HEADS * KEYS_S + TILES * 512].rearrange("p (t c) -> p t c", t=TILES)
        cache_v = reg_v[:, HEADS * KEYS_S + TILES * 512:].rearrange("p (t c) -> p t c", t=2)
        norm_row = reg_v[:, 0:2048].rearrange("p (b c) -> p b c", b=2)
        h_row = reg_v[:, 2048:4096].rearrange("p (b c) -> p b c", b=2)
        picked = [at.rearrange("p (k c) -> p k c", k=TOP) for at in
                  (reg_v[:, 0:2048], reg_v[:, 2048:4096], slot(5)[:, 0:2048], slot(5)[:, 2048:4096])]

        ident = sb("ident", [P, P])
        ones = sb("ones", [P, P])
        conv_mean = sb("conv_mean", [P, P])
        before = sb("before", [P, P])
        w_router = sb("w_router_sb", [P, KD, EXPERTS])
        b_router = sb("b_router_sb", [P, EXPERTS])
        rope = sb("rope_sb", [P, TILES, 32])
        c_row = sb("c_row", [16, P])
        c_silu = sb("c_silu", [16, P])
        c_t = sb("c_t", [P, KD, 32])
        conv_w_row = sb("conv_w_row", [TAPS, CONV])
        state_row = sb("state_row", [STATE, CONV])
        lam_prod = sb("lam_prod", [P, 2, HD])
        vec_row = sb("vec_row", [13, P])
        lam_qk = sb("lam_qk", [P, 4, HD])
        cols = sb("cols", [P, 320])
        eps = sb("eps", [P, 1])
        lam_e = sb("lam_e", [P, 6])
        rope_t = sb("rope_t", [P, 2, 8, 16])
        row_max = sb("row_max", [P, 2, 2])
        neg_max = sb("neg_max", [P, 2, 2])
        row_sum = sb("row_sum", [P, 2, 2])
        row_inv = sb("row_inv", [P, 2, 2])
        head_ss = sb("head_ss", [P, 3, 4])
        stats = sb("stats", [P, 2, 6])
        mean_var = sb("mean_var", [P, 2])
        std = sb("std", [P, 2])
        logits = sb("logits", [P, TILES, EXPERTS])
        score = sb("score", [P, TILES, EXPERTS])
        mask = sb("mask", [P, TILES, EXPERTS])
        lower = sb("lower", [P, 4, 4])
        upper = sb("upper", [P, 4, 4])
        reset = sb("reset", [P, TILES, EXPERTS])
        small = sb("small", [P, 8, TILES * GROUPS])
        pick = sb("pick", [P, 4, TILES])
        slot_of = sb("slot_of", [P, 2, TILES], I32)
        cnt = sb("cnt", [P, 6, EXPERTS])
        cnt_i = sb("cnt_i", [P, 2, EXPERTS], I32)
        total = sb("total", [P, 1])
        table = sb("table", [P, 40], I32)
        token_i = sb("token_i", [P, TILES], I32)
        token_f = sb("token_f", [P, TILES])
        zero_row = sb("zero_row", [MAX_TILES + 1, TM])
        slot_row = sb("slot_row", [MAX_TILES + 1, TM])
        slot_token = sb("slot_token", [TM, MAX_TILES + 1], I32)
        slot_now = sb("slot_now", [TM, 1], I32)

        pair = [ctx.enter_context(nc.psum_tensor(f"pair{i}", [P, 2, 512], F32)) for i in range(4)]

        def bank(b):
            return pair[b // 2][:, b % 2, :]

        const_ready = sem("const_ready")
        const_step = sem("const_step")
        setup_in = sem("setup_in")
        setup_dve = sem("setup_dve")
        c_silu_ready = sem("c_silu_ready")
        c_mm = sem("c_mm")
        c_ready = sem("c_ready")
        landed = [sem(f"landed{s}") for s in range(ALL_SLOTS)]
        ada_in = sem("ada_in")
        small_in = sem("small_in")
        cache_k_in = sem("cache_k_in")
        cache_v_in = sem("cache_v_in")
        ada_mm = sem("ada_mm")
        mod_ready = sem("mod_ready")
        mod_out = sem("mod_out")
        c_in = sem("c_in")
        x_in = sem("x_in")
        cols_mm = sem("cols_mm")
        cols_ready = sem("cols_ready")
        lam_ready = sem("lam_ready")
        lam_exp = sem("lam_exp")
        xt_mm = sem("xt_mm")
        ht_dve = sem("ht_dve")
        ht_act = sem("ht_act")
        u_mm = sem("u_mm")
        sig_done = sem("sig_done")
        glu_done = sem("glu_done")
        conv_step = sem("conv_step")
        tap_scaled = sem("tap_scaled")
        tap_added = sem("tap_added")
        conv_done = sem("conv_done")
        new_conv_mm = sem("new_conv_mm")
        new_conv_ready = sem("new_conv_ready")
        new_conv_out = sem("new_conv_out")
        proj_mm = sem("proj_mm")
        proj_act = sem("proj_act")
        proj_rope = sem("proj_rope")
        qk_t_mm = sem("qk_t_mm")
        qk_t_done = sem("qk_t_done")
        k_out = [sem("k_out0"), sem("k_out1")]
        v_out = sem("v_out")
        conv_stat_mm = sem("conv_stat_mm")
        centred = sem("centred")
        squared = sem("squared")
        conv_std = sem("conv_std")
        conv_normed = sem("conv_normed")
        conv_t_done = sem("conv_t_done")
        q_padded = sem("q_padded")
        score_mm = sem("score_mm")
        max_done = sem("max_done")
        exp_done = sem("exp_done")
        attn_done = sem("attn_done")
        attn_t_mm = sem("attn_t_mm")
        attn_t_done = sem("attn_t_done")
        pv_mm = sem("pv_mm")
        out_row_done = sem("out_row_done")
        head_ss_done = sem("head_ss_done")
        head_std = sem("head_std")
        out_normed = sem("out_normed")
        out_t_mm = sem("out_t_mm")
        out_t_done = sem("out_t_done")
        bc1_in = sem("bc1_in")
        bcf_in = sem("bcf_in")
        bc2_in = sem("bc2_in")
        mixout_mm = sem("mixout_mm")
        mix_read = sem("mix_read")
        var_done = sem("var_done")
        std_done = sem("std_done")
        normed = sem("normed")
        h_ready = sem("h_ready")
        h_out = [sem("h_out0"), sem("h_out1")]
        route_t_mm = sem("route_t_mm")
        route_t_done = sem("route_t_done")
        logit_mm = sem("logit_mm")
        logit_max = sem("logit_max")
        logit_exp = sem("logit_exp")
        mask_ready = sem("mask_ready")
        rank_mm = sem("rank_mm")
        table_ready = sem("table_ready")
        slots_ready = sem("slots_ready")
        slot_zeroed = sem("slot_zeroed")
        slot_out = sem("slot_out")
        slot_in = sem("slot_in")
        slot_mm = sem("slot_mm")
        index_ready = sem("index_ready")
        index_now = sem("index_now")
        gathered = sem("gathered")
        tok_mm = sem("tok_mm")
        tok_done = sem("tok_done")
        up_mm = sem("up_mm")
        silu_done = sem("silu_done")
        act_done = sem("act_done")
        act_t_mm = sem("act_t_mm")
        act_t_done = sem("act_t_done")
        y_mm = sem("y_mm")
        y_done = sem("y_done")
        y_out = sem("y_out")
        expert_done = sem("expert_done")
        picked_in = [sem(f"picked_in{b}") for b in range(4)]
        picked_read = sem("picked_read")
        pick_scaled = sem("pick_scaled")
        var2_done = sem("var2_done")
        std2_done = sem("std2_done")
        normed2 = sem("normed2")
        x_done = sem("x_done")
        final_out = sem("final_out")
        dve_step = sem("dve_step")
        pool_step = sem("pool_step")
        act_step = sem("act_step")

        y_zeroed = sem("y_zeroed")
        pe_held = sem("pe_held")
        pool_held = sem("pool_held")

        n_setup = 4
        xt_per, pr_per, rope_per, qt_per, at_per = 2 * TILES, 3 * TILES, 2 * TILES, 2 * TILES + 2, TILES * HEADS

        block = ctx.enter_context(nc.Block())

        def picks_landed(eng, l, t):
            eng.wait_ge(picked_in[t % 4], TOP * LANDED * ((1 if t % 4 else 2) * l + t // 4 + 1))

        def load_small(sp, l):
            sp.dma_start(conv_w_row[:, :], a["conv_w"][l]).then_inc(small_in, LANDED)
            sp.dma_start(state_row[:, :], a["state_conv"][l, 0]).then_inc(small_in, LANDED)
            for n, name in enumerate(("conv_b", "conv_ln_g", "conv_ln_b")):
                sp.dma_start(vec_row[4 * n:4 * n + 4, :], a[name][l].rearrange("(k p) -> k p", p=P)).then_inc(small_in, LANDED)
            sp.dma_start(vec_row[12:13, :], a["subln_g"][l].rearrange("(k p) -> k p", p=P)).then_inc(small_in, LANDED)
            sp.dma_start(lam_qk[:, :, :], a["lambda_qk"][l].partition_broadcast(P)).then_inc(small_in, LANDED)

        @block.sync
        def _(sp):
            sp.dma_start(c_row[0:8, :], a["c_prompt"].rearrange("a (k p) -> (a k) p", p=P)).then_inc(c_in, LANDED)
            sp.dma_start(c_row[8:16, :], a["c_sample"].rearrange("a (k p) -> (a k) p", p=P)).then_inc(c_in, LANDED)
            fills = [0] * ALL_SLOTS

            def load(s, dst, src):
                fills[s] += 1
                sp.dma_start(dst, src).then_inc(landed[s], LANDED)

            def load_ada(l, n):
                w_ada = a["w_ada"][l].rearrange("(k p) c -> p k c", p=P)
                load(ADA_SLOTS[l][n], by_k(ADA_SLOTS[l][n]), w_ada[:, :, n * 512:(n + 1) * 512])

            def load_in(l, s, c):
                w_in = a["w_in"][l].rearrange("(k p) c -> p k c", p=P)
                load(s, by_k(s), w_in[:, :, c * 512:(c + 1) * 512])

            def load_b_ada(l):
                for j in range(4):
                    sp.dma_start(mod_row[32 * j:32 * j + 2, :, :],
                                 a["b_ada"][l].rearrange("(r j c) -> j r c", j=4, c=512)[j].partition_broadcast(2)).then_inc(ada_in, LANDED)

            for l in range(DEPTH):
                if l == 0:
                    for n in range(4):
                        load_ada(0, n)
                    sp.wait_ge(setup_dve, 1)
                    load_b_ada(0)
                    load_small(sp, 0)
                    sp.dma_start(x[:, 0:4, :], a["x_prompt"][0].rearrange("(t p) d -> p t d", p=P)).then_inc(x_in, LANDED)
                    sp.dma_start(x[0:DEC, 4, :], a["x_sample"][0]).then_inc(x_in, LANDED)
                    sp.dma_start(eps[:, :], a["eps"]).then_inc(setup_in, LANDED)
                    load_in(l, 0, 3)
                    load_in(l, 1, 4)
                    sp.dma_start(w_router[:, :, :], a["w_router"].rearrange("(k p) e -> p k e", p=P)).then_inc(setup_in, LANDED)
                    sp.dma_start(b_router[:, :], a["b_router"].partition_broadcast(P)).then_inc(setup_in, LANDED)
                    sp.dma_start(rope[:, :, :], a["rope"].rearrange("(t p) c -> p t c", p=P)).then_inc(setup_in, LANDED)
                    for n in range(4, 8):
                        if n == 4:
                            sp.wait_ge(ada_mm, 1)
                        load_ada(0, n)
                else:
                    sp.wait_ge(expert_done, EXPERTS * l)
                    load_ada(l, 6)
                    sp.wait_ge(picked_read, TILES * l)
                    load_ada(l, 7)
                sp.wait_ge(ada_mm, 3 * l + 2)
                for n in range(8, ADA_CHUNKS):
                    load_ada(l, n)
                sp.wait_ge(ada_mm, 3 * l + 3)
                load_in(l, 2, 0)
                load_in(l, 3, 1)
                sp.wait_ge(u_mm, 4 * l + 4)
                load_in(l, 0, 2)
                w_out = a["w_out"][l].rearrange("(k p) c -> p k c", p=P)
                load(1, by_k(1), w_out[:, :, 0:512])
                sp.wait_ge(proj_mm, pr_per * l + TILES)
                load(2, by_k(2), w_out[:, :, 512:1024])
                for e in range(EXPERTS):
                    s_gate, s_up, s_down = EXPERT_SLOTS[e % 3]
                    if e == 0:
                        sp.wait_ge(proj_mm, pr_per * l + 2 * TILES)
                    elif e == 1:
                        sp.wait_ge(proj_mm, pr_per * (l + 1))
                    elif e == 2:
                        sp.wait_ge(h_ready, TILES * (l + 1))
                    else:
                        sp.wait_ge(expert_done, EXPERTS * l + e - 2)
                    load(s_gate, by_k(s_gate), a["w_gate"][l, e].rearrange("(p k) c -> p k c", p=P))
                    if e == 0:
                        sp.wait_ge(out_t_mm, TILES * (l + 1))
                        sp.wait_ge(out_t_done, TILES * (l + 1))
                        sp.wait_ge(conv_t_done, 4 * (l + 1))
                    elif e == 1:
                        sp.wait_ge(mixout_mm, TILES * (l + 1))
                    load(s_up, by_k(s_up), a["w_up"][l, e].rearrange("(p k) c -> p k c", p=P))
                    if e == 2:
                        sp.wait_ge(h_out[0], 3 * LANDED * (l + 1))
                        sp.wait_ge(h_out[1], 2 * LANDED * (l + 1))
                        sp.wait_ge(route_t_mm, 2 * TILES * (l + 1))
                    load(s_down, slot(s_down).rearrange("p (h k c) -> p h k c", h=2, k=2),
                         a["w_down"][l, e].rearrange("(h p k) c -> p h k c", h=2, k=2))
                    if e == 3 and l + 1 < DEPTH:
                        load_b_ada(l + 1)
                        load_small(sp, l + 1)
                if l + 1 < DEPTH:
                    sp.wait_ge(expert_done, EXPERTS * l + 14)
                    for n in range(3):
                        load_ada(l + 1, n)
                    sp.wait_ge(expert_done, EXPERTS * l + 15)
                    load_ada(l + 1, 3)
                sp.wait_ge(expert_done, EXPERTS * l + 15)
                for s in range(2):
                    sp.dma_start(gate_bc[:, s, :], mod_dram[s, 5 * D:6 * D].partition_broadcast(P)).then_inc(bc2_in, LANDED)
                sp.dma_start(ln_g_bc, a["ln2_g"][l].partition_broadcast(P)).then_inc(bc2_in, LANDED)
                sp.dma_start(ln_b_bc, a["ln2_b"][l].partition_broadcast(P)).then_inc(bc2_in, LANDED)
                if l + 1 < DEPTH:
                    sp.wait_ge(ada_mm, 3 * (l + 1) + 1)
                    for t in range(4):
                        picks_landed(sp, l, t)
                    load_in(l + 1, 0, 3)
                    load_in(l + 1, 1, 4)
                    load_ada(l + 1, 4)
                    load_ada(l + 1, 5)
            sp.wait_ge(x_done, TILES * DEPTH)
            sp.dma_start(a["y_prompt"][0].rearrange("(t p) d -> p t d", p=P), x[:, 0:4, :]).then_inc(final_out, LANDED)
            sp.dma_start(a["y_sample"][0], x[0:DEC, 4, :]).then_inc(final_out, LANDED)
            sp.wait_ge(final_out, 2 * LANDED)

        @block.gpsimd
        def _(pool):
            steps = [0]

            def seq(ins):
                steps[0] += 1
                ins.then_inc(pool_step, 1)
                pool.wait_ge(pool_step, steps[0])

            seq(pool.memset(ident[:, :], 0.0))
            seq(pool.affine_select(out=ident[:, :], in_=ident[:, :], compare_op=ALU.not_equal, fill=1.0,
                                   base=0, pattern=[[-1, P]], channel_multiplier=1))
            seq(pool.memset(ones[:, :], 1.0))
            seq(pool.memset(conv_mean[:, :], 1.0 / CONV))
            seq(pool.affine_select(out=before[:, :], in_=ones[:, :], compare_op=ALU.is_gt, fill=0.0,
                                   base=0, pattern=[[1, P]], channel_multiplier=-1))
            four = ones[:, 0:16].rearrange("p (j i) -> p j i", j=4)
            seq(pool.affine_select(out=lower[:, :, :], in_=four, compare_op=ALU.is_gt, fill=0.0,
                                   base=0, pattern=[[1, 4], [-1, 4]], channel_multiplier=0))
            seq(pool.affine_select(out=upper[:, :, :], in_=four, compare_op=ALU.is_gt, fill=0.0,
                                   base=0, pattern=[[-1, 4], [1, 4]], channel_multiplier=0))
            seq(pool.memset(zero_row[:, :], 0.0))
            seq(pool.iota(token_i[:, :], pattern=[[P, TILES]], base=0, channel_multiplier=1))
            seq(pool.memset(zeros, 0.0))
            pool.memset(total[:, :], 0.0).then_inc(const_ready, 1)

            for l in range(DEPTH):
                pool.dma_start(slot_dram.rearrange("(r c) a -> r (c a)", c=TM), zero_row[:, :]).then_inc(slot_zeroed, LANDED)
                if l == 0:
                    pool.dma_start(y_dram[EXPERTS * TM:, :].rearrange("(n p) d -> p n d", p=P),
                                   zeros.unsqueeze(1).to_broadcast([P, (MAX_TILES - EXPERTS) * TM // P, D])).then_inc(y_zeroed, LANDED)
                for n in range(4 * l * POOL_TAPS, 4 * (l + 1) * POOL_TAPS):
                    w = n % POOL_TAPS
                    pool.wait_ge(tap_scaled, n + 1)
                    if w:
                        ins = pool.tensor_tensor(pool_sum, pool_sum, scaled[n % 2], ALU.add)
                    else:
                        if n > 4 * l * POOL_TAPS:
                            pool.wait_ge(conv_done, n // POOL_TAPS)
                        ins = pool.tensor_copy(pool_sum, scaled[n % 2])
                    ins.then_inc(tap_added, 1)
                    pool.wait_ge(tap_added, n + 1)
                pool.wait_ge(mod_ready, 3 * (l + 1))
                for s in range(2):
                    dst = mod_dram[s].rearrange("(r j c) -> j r c", j=4, c=512)
                    pool.dma_start(dst[:, 1:3, :], mod_row[s:s + 97:32, 1:3, :]).then_inc(mod_out, LANDED)
                pool.wait_ge(ada_mm, 3 * (l + 1))
                pool.wait_ge(conv_done, 4 * (l + 1))
                pool.dma_start(cache_k_row[:, :, :],
                               a["cache_k"][l, 0].rearrange("(t p) h m c -> p t (h m c)", p=P)).then_inc(cache_k_in, LANDED)
                if l:
                    pool.wait_ge(picked_read, TILES * l)
                pool.dma_start(cache_v[:, :, :], a["cache_v"][l, 0].rearrange("(t p) h c -> p t (h c)", p=P)).then_inc(cache_v_in, LANDED)
                pool.wait_ge(new_conv_ready, 2 * (l + 1))
                pool.dma_start(a["conv_prompt"][l, 0], new_conv[0:STATE, 0, :]).then_inc(new_conv_out, LANDED)
                pool.dma_start(a["conv_sample"][l, 0], new_conv[0:STATE, 1, :]).then_inc(new_conv_out, LANDED)
                for t in range(TILES):
                    i = TILES + t
                    pool.wait_ge(proj_act, pr_per * l + i + 1)
                    pool.wait_ge(proj_rope, rope_per * l + i + 1)
                    dst = a["k_sample"][l, 0] if t == 4 else a["k_prompt"][l, 0, t * P:(t + 1) * P]
                    pool.dma_start(dst.rearrange("t h m c -> t (h m c)"),
                                   qk_row[0:ROWS[t], i % 2, :]).then_inc(k_out[i % 2], LANDED)
                pool.wait_ge(conv_normed, 4 * (l + 1))
                seq(pool.memset(q_pad[:, :, :, :], 0.0))

                def pad_q(i):
                    t, h, b = i // 4, i % 4, i % 4
                    r = ROWS[t]
                    pool.wait_ge(qk_t_done, qt_per * l + t + 1)
                    if i >= 4:
                        pool.wait_ge(score_mm, at_per * l + i - 3)
                    for m in range(2):
                        half = slice(HD * m, HD * m + HD)
                        ins = pool.tensor_copy(q_pad[half, b, m, 0:r], q_t[half, h, COL[t]:COL[t] + r])
                    ins.then_inc(q_padded, 1)

                for i in range(4):
                    pad_q(i)
                def store_v(t):
                    pool.wait_ge(proj_act, pr_per * l + 2 * TILES + t + 1)
                    dst = a["v_sample"][l, 0] if t == 4 else a["v_prompt"][l, 0, t * P:(t + 1) * P]
                    pool.dma_start(dst.rearrange("t h c -> t (h c)"), v_row[0:ROWS[t], t, :]).then_inc(v_out, LANDED)

                for i in range(4, at_per):
                    pad_q(i)
                    if i % 4 == 2 and i > 4:
                        store_v(i // 4)
                    if i == 4:
                        store_v(0)
                pool.wait_ge(mod_out, 2 * LANDED * (l + 1))
                pool.wait_ge(proj_mm, pr_per * (l + 1))
                for s in range(2):
                    pool.dma_start(gate_bc[:, s, :], mod_dram[s, 2 * D:3 * D].partition_broadcast(P)).then_inc(bc1_in, LANDED)
                pool.dma_start(ln_g_bc, a["ln1_g"][l].partition_broadcast(P)).then_inc(bc1_in, LANDED)
                pool.dma_start(ln_b_bc, a["ln1_b"][l].partition_broadcast(P)).then_inc(bc1_in, LANDED)
                pool.wait_ge(score_mm, at_per * (l + 1))
                for s in range(2):
                    pool.dma_start(shift_bc[:, s, :], mod_dram[s, 3 * D:4 * D].partition_broadcast(P)).then_inc(bcf_in, LANDED)
                    pool.dma_start(scale_bc[:, s, :], mod_dram[s, 4 * D:5 * D].partition_broadcast(P)).then_inc(bcf_in, LANDED)
                pool.wait_ge(bcf_in, 4 * LANDED * (l + 1))
                seq(pool.tensor_scalar(scale_bc[:, :, :], scale_bc[:, :, :], 1.0, 0.0, ALU.add, ALU.add))
                pool.wait_ge(bc1_in, 4 * LANDED * (l + 1))
                for t in range(TILES):
                    r, b, s = ROWS[t], t % 2, t // 4
                    pool.wait_ge(normed, TILES * l + t + 1)
                    seq(pool.tensor_tensor(x[0:r, t, :], norm_row[0:r, b, :], ln_g_bc[0:r, :], ALU.mult))
                    seq(pool.tensor_tensor(x[0:r, t, :], x[0:r, t, :], ln_b_bc[0:r, :], ALU.add))
                    if t >= 2:
                        pool.wait_ge(route_t_mm, 2 * (TILES * l + t - 1))
                        pool.wait_ge(h_out[b], LANDED * (3 * l + t // 2 if b == 0 else 2 * l + t // 2))
                    seq(pool.tensor_tensor(h_row[0:r, b, :], x[0:r, t, :], scale_bc[0:r, s, :], ALU.mult))
                    pool.tensor_tensor(h_row[0:r, b, :], h_row[0:r, b, :], shift_bc[0:r, s, :], ALU.add).then_inc(h_ready, 1)
                    pool.wait_ge(h_ready, TILES * l + t + 1)
                    pool.dma_start(h_dram[t * P:t * P + r, :], h_row[0:r, b, :]).then_inc(h_out[b], LANDED)
                pool.wait_ge(slots_ready, l + 1)
                pool.wait_ge(slot_zeroed, LANDED * (l + 1))
                for k in range(TOP):
                    for t in range(TILES):
                        pool.indirect_dma_start(slot_dram, bass.IndirectOffsetOnAxis(slot_of[0:ROWS[t], k, t:t + 1], 0),
                                                token_f[0:ROWS[t], t:t + 1], None).then_inc(slot_out, LANDED)
                pool.wait_ge(slot_out, TOP * TILES * LANDED * (l + 1))
                pool.dma_start(slot_row[:, :], slot_dram.rearrange("(r c) a -> r (c a)", c=TM)).then_inc(slot_in, LANDED)
                pool.wait_ge(index_ready, l + 1)
                pool.wait_ge(h_out[0], 3 * LANDED * (l + 1))
                pool.wait_ge(h_out[1], 2 * LANDED * (l + 1))
                pool.wait_ge(table_ready, l + 1)
                tiles = pool.value_load(table[0:1, 32:33], min_val=EXPERTS, max_val=MAX_TILES)
                base = pool.value_load(table[0:1, 33:34], min_val=0, max_val=DEPTH * MAX_TILES)
                with pool.Fori(0, tiles + 1) as i:
                    pool.wait_ge(tok_mm, base + l + i + 1)
                    pool.sem_inc(pool_held, 1)
                    pool.tensor_copy(slot_now[:, :], slot_token[:, bass.ds(i, 1)]).then_inc(index_now, 1)
                    pool.wait_ge(index_now, base + l + i + 1)
                    pool.sem_inc(pool_held, 1)
                    pool.indirect_dma_start(gathered_row, None, h_dram,
                                            bass.IndirectOffsetOnAxis(slot_now[:, 0:1], 0)).then_inc(gathered, LANDED)
                pool.wait_ge(y_out, 2 * LANDED * (base + tiles + 1))
                pool.sem_inc(pool_held, 1)
                pool.wait_ge(bc2_in, 4 * LANDED * (l + 1))
                def pick_rows(t):
                    r, b = ROWS[t], t % 4
                    for k in range(TOP):
                        pool.indirect_dma_start(picked[b][0:r, k, :], None, y_dram,
                                                bass.IndirectOffsetOnAxis(slot_of[0:r, k, t:t + 1], 0)).then_inc(picked_in[b], LANDED)

                for t in range(4):
                    pick_rows(t)
                pool.wait_ge(picked_read, TILES * l + 1)
                pick_rows(4)
                for t in range(TILES):
                    r, b = ROWS[t], t % 2
                    pool.wait_ge(normed2, TILES * l + t + 1)
                    seq(pool.tensor_tensor(x[0:r, t, :], mixed[0:r, b, :], ln_g_bc[0:r, :], ALU.mult))
                    pool.tensor_tensor(x[0:r, t, :], x[0:r, t, :], ln_b_bc[0:r, :], ALU.add).then_inc(x_done, 1)
            for n, s in ((2 * DEPTH, new_conv_out), (2 * DEPTH, k_out[0]), (3 * DEPTH, k_out[1]), (TILES * DEPTH, v_out)):
                pool.wait_ge(s, n * LANDED)

        @block.scalar
        def _(act):
            A = nc.scalar.activation
            act.sem_inc(y_done, 1)
            act.sem_inc(y_out, 2 * LANDED)
            act.wait_ge(c_in, 2 * LANDED)
            A(c_silu[:, :], c_row[:, :], ACT.Silu).then_inc(c_silu_ready, 1)

            def lambda_exp(l):
                act.wait_ge(lam_ready, 2 * l + 1)
                A(lam_e[:, 2:4], lam_e[:, 0:2], ACT.Exp).then_inc(lam_exp, 1)

            lambda_exp(0)
            for l in range(DEPTH):
                act.wait_ge(cols_ready, l + 1)
                for t in range(TILES):
                    r, s = ROWS[t], t // 4
                    act.wait_ge(xt_mm, xt_per * l + 2 * t + 2)
                    for k in range(4):
                        ins = A(h_t[:, 4 + k, COL[t]:COL[t] + r], bank(5)[:, k * P:k * P + r], ACT.Identity,
                                bias=cols[:, 16 * s + 4 + k:16 * s + 5 + k], scale=cols[:, 16 * s + 12 + k:16 * s + 13 + k])
                    ins.then_inc(ht_act, 1)
                for j in range(4):
                    act.wait_ge(u_mm, 4 * l + j + 1)
                    if j >= 2:
                        act.wait_ge(glu_done, 4 * l + j - 1)
                    A(sig[:, j % 2, 0:SEQ], bank(2 * (j % 2) + 1), ACT.Sigmoid)
                    A(sig[:, j % 2, SEQ:NTOK], bank(6 + j % 2)[:, DEC:2 * DEC], ACT.Sigmoid).then_inc(sig_done, 1)
                    act.wait_ge(glu_done, 4 * l + j + 1)
                    for w in range(POOL_TAPS):
                        n = (4 * l + j) * POOL_TAPS + w
                        if n >= 2:
                            act.wait_ge(tap_added, n - 1)
                        c = DVE_TAPS + w
                        A(scaled[n % 2], glu[:, j, c:c + CW], ACT.Copy,
                          scale=cols[:, 64 + TAPS * j + c:65 + TAPS * j + c]).then_inc(tap_scaled, 1)
                act.wait_ge(conv_done, 4 * (l + 1))

                def leave_t(i):
                    act.wait_ge(qk_t_mm, qt_per * l + i + 1)
                    kind, t = i // TILES, i % TILES
                    r = ROWS[t] if kind < 2 else P
                    if kind == 0:
                        dst = q_t[:, :, COL[t]:COL[t] + r]
                    elif kind == 1 and t < 4:
                        dst = k_t[:, :, t * P:t * P + r]
                    elif kind == 1:
                        dst = ks_t[:, :, PAST:KEYS_S]
                    else:
                        dst = ks_t[:, :, t * P:t * P + P]
                    src = bank(4 + i % 2).rearrange("p (h t) -> p h t", h=HEADS)[:, :, 0:r]
                    A(dst, src, ACT.Copy).then_inc(qk_t_done, 1)

                if l:
                    act.wait_ge(picked_read, TILES * l)
                for i in range(3 * TILES):
                    t, r = i % TILES, ROWS[i % TILES]
                    if i <= 2 * TILES:
                        act.wait_ge(proj_mm, pr_per * l + i + 1)
                    if i < 2 * TILES:
                        if i >= 2:
                            act.wait_ge(qk_t_mm, qt_per * l + i - 1)
                        if i >= TILES + 2:
                            act.wait_ge(k_out[i % 2], LANDED * ((3 if i % 2 else 2) * l + (i - TILES) // 2))
                        A(qk_row[0:r, i % 2, :], bank(i % 4)[0:r, :], ACT.Copy).then_inc(proj_act, 1)
                    elif i == 2 * TILES:
                        A(v_row[0:r, t, :], bank(i % 4)[0:r, :], ACT.Copy).then_inc(proj_act, 1)
                    if 2 <= i < 2 * TILES + 4:
                        leave_t(i - 2)
                    if i == 2:
                        for b in range(2):
                            act.wait_ge(new_conv_mm, 2 * l + b + 1)
                            A(new_conv[0:STATE, b, :], bank(6 + b)[0:STATE, :], ACT.Copy).then_inc(new_conv_ready, 1)
                    if i == TILES - 1:
                        for j in range(4):
                            act.wait_ge(centred, 4 * l + j + 1)
                            A(glu[:, j, 0:CW], mix_t[:, 4 + j, 0:CW], ACT.Square).then_inc(squared, 1)
                    if i == TILES + 2:
                        act.wait_ge(conv_stat_mm, 2 * l + 2)
                        A(glu[:, 0, 0:CW].rearrange("p (b c) -> p b c", b=2), pair[3][:, :, 0:HALF], ACT.Sqrt,
                          bias=eps[:, :]).then_inc(conv_std, 1)
                    if i == 2 * TILES + 2:
                        for j in range(4):
                            act.wait_ge(conv_normed, 4 * l + j + 1)
                            A(mix_t[:, 4 + j, 0:CW], mix_t[:, 4 + j, 0:CW], ACT.Silu,
                              bias=cols[:, 40 + j:41 + j], scale=cols[:, 36 + j:37 + j]).then_inc(conv_t_done, 1)

                def exps(i):
                    r, keys, b = ROWS[i // 4], (KEYS_S if i // 4 == 4 else (i // 4 + 1) * P), i % 2
                    act.wait_ge(max_done, at_per * l + i + 1)
                    if i >= 2:
                        act.wait_ge(attn_done, at_per * l + i - 1)
                    for m in range(2):
                        ins = A(prob[0:r, b, m, 0:keys], pair[b][0:r, m, 0:keys], ACT.Exp,
                                bias=neg_max[0:r, b, m:m + 1], scale=SCALE, accum_out=row_sum[0:r, b, m:m + 1])
                    ins.then_inc(exp_done, 1)

                def leave_attn_t(i):
                    t = i // 4
                    act.wait_ge(attn_t_mm, at_per * l + i + 1)
                    if i >= 2:
                        act.wait_ge(pv_mm, at_per * l + i - 1)
                    if t < 4:
                        ins = A(attn_t[:, i % 2, 0:(t + 1) * P], bank(4)[:, 0:(t + 1) * P], ACT.Copy)
                    else:
                        A(attn_t[:, i % 2, 0:2 * P].rearrange("p (k t) -> p k t", k=2)[:, :, 0:DEC],
                          bank(4)[:, 0:2 * P].rearrange("p (k t) -> p k t", k=2)[:, :, 0:DEC], ACT.Copy)
                        ins = A(attn_t[0:DEC, i % 2, 2 * P:2 * P + DEC], bank(4)[0:DEC, 2 * P:2 * P + DEC], ACT.Copy)
                    ins.then_inc(attn_t_done, 1)

                def leave_out(t):
                    act.wait_ge(pv_mm, at_per * l + 4 * t + 4)
                    if t >= 1:
                        act.wait_ge(out_t_mm, TILES * l + t)
                    A(out_row[0:ROWS[t], :], bank(6 + t % 2)[0:ROWS[t], :], ACT.Copy).then_inc(out_row_done, 1)

                def head_sqrt(t):
                    act.wait_ge(head_ss_done, TILES * l + t + 1)
                    A(head_ss[0:ROWS[t], 1, :], head_ss[0:ROWS[t], 0, :], ACT.Sqrt, bias=eps[0:ROWS[t], :],
                      scale=1.0 / P).then_inc(head_std, 1)

                act.wait_ge(new_conv_out, 2 * LANDED * (l + 1))
                exps(0)
                for i in range(at_per + 2):
                    if i + 1 < at_per:
                        exps(i + 1)
                    if i < at_per:
                        leave_attn_t(i)
                    if i % 4 == 3 and i < at_per - 4:
                        t = i // 4 + 1
                        act.wait_ge(proj_mm, pr_per * l + 2 * TILES + t + 1)
                        A(v_row[0:ROWS[t], t, :], bank(5)[0:ROWS[t], :], ACT.Copy).then_inc(proj_act, 1)
                    if i >= 4 and i % 4 == 0:
                        leave_out(i // 4 - 1)
                    if i >= 5 and i % 4 == 1:
                        head_sqrt(i // 4 - 1)

                for t in range(TILES + 2):
                    if t < TILES:
                        act.wait_ge(var_done, TILES * l + t + 1)
                        A(std[0:ROWS[t], 0:1], mean_var[0:ROWS[t], 1:2], ACT.Sqrt, bias=eps[0:ROWS[t], :]).then_inc(std_done, 1)
                    if t >= 2:
                        u = t - 2
                        for hf in range(2):
                            act.wait_ge(route_t_mm, 2 * (TILES * l + u) + hf + 1)
                            if u >= 1:
                                act.wait_ge(logit_mm, TILES * l + u)
                            A(route_t[hf][:, :, 0:ROWS[u]],
                              bank(4 + hf).rearrange("p (k t) -> p k t", k=4)[:, :, 0:ROWS[u]], ACT.Copy).then_inc(route_t_done, 1)
                act.wait_ge(logit_max, l + 1)
                A(score[:, :, :], logits[:, :, :], ACT.Exp).then_inc(logit_exp, 1)

                act.wait_ge(table_ready, l + 1)
                tiles = act.value_load(table[0:1, 32:33], min_val=EXPERTS, max_val=MAX_TILES)
                base = act.value_load(table[0:1, 33:34], min_val=0, max_val=DEPTH * MAX_TILES)
                act.wait_ge(tok_mm, base + l + 2)
                A(tok_t[:, :, :], bank(2).rearrange("p (k t) -> p k t", k=KD), ACT.Copy).then_inc(tok_done, 1)
                with act.Fori(0, tiles) as i:
                    for hf in range(2):
                        act.wait_ge(up_mm, (base + i) * 2 + hf + 1)
                        A(silu_g[TM:2 * TM, hf * 256:hf * 256 + 256], bank(hf)[0:TM, 0:256], ACT.Silu).then_inc(silu_done, 1)
                    act.wait_ge(tok_mm, base + l + i + 3)
                    A(tok_t[:, :, :], bank(2).rearrange("p (k t) -> p k t", k=KD), ACT.Copy).then_inc(tok_done, 1)
                    act.wait_ge(y_out, (base + i + 1) * (2 * LANDED))
                    act.wait_ge(y_mm, base + i + 1)
                    A(y_row, bank(4), ACT.Copy).then_inc(y_done, 1)
                    act.wait_ge(y_done, base + i + 2)
                    for n in range(2):
                        act.dma_start(y_dram[bass.ds(i * TM, TM), n * 512:(n + 1) * 512],
                                      y_row[n * TM:(n + 1) * TM, :]).then_inc(y_out, LANDED)
                for t in range(TILES):
                    r, b = ROWS[t], t % 2
                    picks_landed(act, l, t)
                    if t >= 2:
                        act.wait_ge(x_done, TILES * l + t - 1)
                    A(mixed[0:r, b, :], picked[t % 4][0:r, 0, :], ACT.Copy, scale=pick[0:r, 2, t:t + 1]).then_inc(pick_scaled, 1)
                    act.wait_ge(var2_done, TILES * l + t + 1)
                    A(std[0:r, 0:1], mean_var[0:r, 1:2], ACT.Sqrt, bias=eps[0:r, :]).then_inc(std2_done, 1)
                    if l + 1 < DEPTH and t == 0:
                        lambda_exp(l + 1)

        @block.vector
        def _(dve):
            V = nc.vector
            steps = [0]

            def seq(ins):
                steps[0] += 1
                ins.then_inc(dve_step, 1)
                dve.wait_ge(dve_step, steps[0])

            seq(V.memset(mod_row[:, :, :], 0.0))
            seq(V.memset(c_t[:, :, :], 0.0))
            seq(V.memset(reset[:, :, :], 1.0))
            seq(V.memset(reset[:, :, 0:1], 0.0))
            seq(V.memset(logits[:, :, :], 0.0))
            V.memset(cnt[:, 5, :], 1.0).then_inc(setup_dve, 1)
            dve.wait_ge(const_ready, 1)
            seq(V.tensor_copy(token_f[:, :], token_i[:, :]))
            dve.wait_ge(c_mm, 1)
            V.tensor_copy(c_t[:, :, 0:2], bank(7)[:, 0:16].rearrange("p (s k) -> p k s", s=2)).then_inc(c_ready, 1)

            def layer_norm_tail(out, src, r, ready, need):
                dve.wait_ge(ready, need)
                seq(V.reciprocal(std[0:r, 1:2], std[0:r, 0:1]))
                return V.tensor_scalar(out, src, mean_var[0:r, 0:1], std[0:r, 1:2], ALU.subtract, ALU.mult)

            def statistics(src, r):
                for hf in range(2):
                    seq(V.bn_stats(stats[0:r, hf, :], src[:, hf * 512:hf * 512 + 512]))
                return V.bn_aggr(mean_var[0:r, :], stats[0:r, :, :])

            def add_bias(l, n):
                dve.wait_ge(ada_in, 4 * LANDED * (l + 1))
                dve.wait_ge(ada_mm, 3 * l + n + 1)
                V.tensor_tensor(mod_row[:, n, :], bank(ADA_BANK[n]), mod_row[:, n, :], ALU.add).then_inc(mod_ready, 1)

            def prepare_lambda(l):
                add_bias(l, 0)
                dve.wait_ge(small_in, 7 * LANDED * (l + 1))
                seq(V.tensor_tensor(lam_prod[:, :, :], lam_qk[:, 0::2, :], lam_qk[:, 1::2, :], ALU.mult))
                V.reduce_sum(lam_e[:, 0:2], lam_prod[:, :, :], AX_X).then_inc(lam_ready, 1)

            def prepare_columns(l):
                dve.wait_ge(lam_exp, l + 1)
                seq(V.tensor_tensor(lam_e[:, 4:5], lam_e[:, 3:4], lam_e[:, 2:3], ALU.subtract))
                V.tensor_scalar(lam_e[:, 5:6], lam_e[:, 4:5], -lam_init(l), None, ALU.add).then_inc(lam_ready, 1)
                dve.wait_ge(cols_mm, l + 1)
                V.tensor_copy(cols[:, 32:312], bank(4)[:, 32:312])
                seq(V.tensor_copy(cols[:, 0:32].rearrange("p (s j b) -> p s j b", s=2, j=4),
                                  bank(5).rearrange("p (b j x) -> p x j b", b=4, j=4)[:, 0:2, :, :]))
                by_stream = cols[:, 0:32].rearrange("p (s k) -> p s k", s=2)
                seq(V.tensor_scalar(by_stream[:, :, 8:16], by_stream[:, :, 8:16], 1.0, None, ALU.add))
                seq(V.tensor_scalar(cols[:, 44:45], cols[:, 44:45], 1.0 - lam_init(l), None, ALU.mult))
                seq(V.memset(glu[:, :, 0:STATE], 0.0))
                V.tensor_copy(glu[:, :, STATE + SEQ:STATE + SEQ + STATE],
                              cols[:, 192:312].rearrange("p (j t) -> p j t", j=4)).then_inc(cols_ready, 1)

            prepare_lambda(0)
            prepare_columns(0)
            for l in range(DEPTH):
                for t in range(TILES):
                    r, s = ROWS[t], t // 4
                    dve.wait_ge(xt_mm, xt_per * l + 2 * t + 1)
                    if t == 0:
                        dve.wait_ge(cols_ready, l + 1)
                    for k in range(4):
                        ins = V.tensor_scalar(h_t[:, k, COL[t]:COL[t] + r], bank(4)[:, k * P:k * P + r],
                                              cols[:, 16 * s + 8 + k:16 * s + 9 + k], cols[:, 16 * s + k:16 * s + k + 1],
                                              ALU.mult, ALU.add)
                    ins.then_inc(ht_dve, 1)
                for j in range(4):
                    dve.wait_ge(sig_done, 4 * l + j + 1)
                    V.tensor_tensor(glu[:, j, STATE:STATE + SEQ], bank(2 * (j % 2)), sig[:, j % 2, 0:SEQ], ALU.mult)
                    V.tensor_tensor(glu[:, j, GW - DEC:GW], bank(6 + j % 2)[:, 0:DEC], sig[:, j % 2, SEQ:NTOK],
                                    ALU.mult).then_inc(glu_done, 1)
                    dve.wait_ge(glu_done, 4 * l + j + 1)
                    acc = mix_t[:, 4 + j, 0:CW]
                    tap = cols[:, 64 + TAPS * j:64 + TAPS * (j + 1)]
                    if j == 2 and l == 0:
                        dve.wait_ge(y_zeroed, LANDED)
                    V.tensor_scalar(acc, glu[:, j, 0:CW], tap[:, 0:1], cols[:, 32 + j:33 + j], ALU.mult, ALU.add).then_inc(conv_step, 1)
                    V.tensor_scalar(odd_sum, glu[:, j, 1:1 + CW], tap[:, 1:2], None, ALU.mult).then_inc(conv_step, 1)
                    for w in range(2, DVE_TAPS):
                        dve.wait_ge(conv_step, DVE_TAPS * (4 * l + j) + w - 1)
                        out = odd_sum if w % 2 else acc
                        V.scalar_tensor_tensor(out=out, in0=glu[:, j, w:w + CW], scalar=tap[:, w:w + 1], in1=out,
                                               op0=ALU.mult, op1=ALU.add).then_inc(conv_step, 1)
                    dve.wait_ge(conv_step, DVE_TAPS * (4 * l + j + 1))
                    seq(V.tensor_tensor(acc, acc, odd_sum, ALU.add))
                    dve.wait_ge(tap_added, POOL_TAPS * (4 * l + j + 1))
                    V.tensor_tensor(acc, acc, pool_sum, ALU.add).then_inc(conv_done, 1)
                    if j in (0, 2):
                        add_bias(l, 1 + j // 2)

                for i in range(2 * TILES):
                    t, r = i % TILES, ROWS[i % TILES]
                    dve.wait_ge(proj_act, pr_per * l + i + 1)
                    src = qk_row[0:r, i % 2, :].rearrange("p (g c) -> p g c", g=8)
                    cos = rope[0:r, t, 0:16].unsqueeze(1).to_broadcast([r, 8, 16])
                    sin = rope[0:r, t, 16:32].unsqueeze(1).to_broadcast([r, 8, 16])
                    V.tensor_tensor(rope_t[0:r, 0, :, :], src[:, :, 0:16], cos, ALU.mult)
                    V.tensor_tensor(rope_t[0:r, 1, :, 0:8], src[:, :, 8:16], sin[:, :, 0:8], ALU.mult)
                    seq(V.tensor_tensor(rope_t[0:r, 1, :, 8:16], src[:, :, 0:8], sin[:, :, 8:16], ALU.mult))
                    V.tensor_tensor(src[:, :, 0:16],
                                    rope_t[0:r, 0, :, :], rope_t[0:r, 1, :, :], ALU.add).then_inc(proj_rope, 1)
                    dve.wait_ge(proj_rope, rope_per * l + i + 1)
                    if i == TILES - 2:
                        dve.wait_ge(conv_stat_mm, 2 * l + 1)
                        for j in range(4):
                            view = mix_t[:, 4 + j, 0:CW].rearrange("p (b c) -> p b c", b=2)
                            V.tensor_tensor(view, view, pair[3][:, :, 0:HALF], ALU.subtract).then_inc(centred, 1)
                    if i == TILES + 3:
                        dve.wait_ge(conv_std, l + 1)
                        seq(V.reciprocal(glu[:, 1, 0:CW], glu[:, 0, 0:CW]))
                        for j in range(4):
                            V.tensor_tensor(mix_t[:, 4 + j, 0:CW], mix_t[:, 4 + j, 0:CW], glu[:, 1, 0:CW], ALU.mult).then_inc(conv_normed, 1)
                def maxima(i):
                    t, b = i // 4, i % 2
                    r, keys = ROWS[t], (KEYS_S if t == 4 else (t + 1) * P)
                    dve.wait_ge(score_mm, at_per * l + i + 1)
                    if t < 4:
                        seq(V.memset(pair[b][0:64, :, keys - 64:keys], NEG))
                    seq(V.reduce_max(row_max[0:r, b, :], pair[b][0:r, :, 0:keys], AX_X))
                    V.tensor_scalar(neg_max[0:r, b, :], row_max[0:r, b, :], -SCALE, None, ALU.mult).then_inc(max_done, 1)

                def combine(i):
                    t, b = i // 4, i % 2
                    r, keys = ROWS[t], (KEYS_S if t == 4 else (t + 1) * P)
                    dve.wait_ge(exp_done, at_per * l + i + 1)
                    seq(V.reciprocal(row_inv[0:r, b, :], row_sum[0:r, b, :]))
                    if i >= 2:
                        dve.wait_ge(attn_t_mm, at_per * l + i - 1)
                    V.tensor_scalar(attn[0:r, b, 0:keys], prob[0:r, b, 0, 0:keys], row_inv[0:r, b, 0:1], None, ALU.mult)
                    seq(V.tensor_scalar(row_inv[0:r, b, 1:2], row_inv[0:r, b, 1:2], lam_e[0:r, 5:6], None, ALU.mult))
                    V.scalar_tensor_tensor(out=attn[0:r, b, 0:keys], in0=prob[0:r, b, 1, 0:keys], scalar=row_inv[0:r, b, 1:2],
                                           in1=attn[0:r, b, 0:keys], op0=ALU.mult, op1=ALU.add).then_inc(attn_done, 1)

                def head_squares(t):
                    r = ROWS[t]
                    dve.wait_ge(out_row_done, TILES * l + t + 1)
                    seq(V.tensor_tensor(square[0:r, :], out_row[0:r, :], out_row[0:r, :], ALU.mult))
                    V.reduce_sum(head_ss[0:r, 0, :], square[0:r, :].rearrange("p (h c) -> p h c", h=4), AX_X).then_inc(head_ss_done, 1)

                def head_norm(t):
                    r = ROWS[t]
                    dve.wait_ge(head_std, TILES * l + t + 1)
                    seq(V.reciprocal(head_ss[0:r, 2, :], head_ss[0:r, 1, :]))
                    view = out_row[0:r, :].rearrange("p (h c) -> p h c", h=4)
                    V.tensor_tensor(view, view, head_ss[0:r, 2, :].unsqueeze(2).to_broadcast([r, 4, P]), ALU.mult).then_inc(out_normed, 1)

                def leave_out_t(t):
                    dve.wait_ge(out_t_mm, TILES * l + t + 1)
                    V.tensor_scalar(mix_t[:, 0:4, MCOL[t]:MCOL[t] + ROWS[t]],
                                    bank(6 + t % 2).rearrange("p (h t) -> p h t", h=4)[:, :, 0:ROWS[t]],
                                    cols[:, 44:45], None, ALU.mult).then_inc(out_t_done, 1)

                dve.wait_ge(mod_out, 2 * LANDED * (l + 1))
                dve.wait_ge(k_out[0], 2 * LANDED * (l + 1))
                dve.wait_ge(k_out[1], 3 * LANDED * (l + 1))
                maxima(0)
                for i in range(at_per + 3):
                    if i + 1 < at_per:
                        maxima(i + 1)
                    if i < at_per:
                        combine(i)
                    if i >= 4 and i % 4 == 0:
                        head_squares(i // 4 - 1)
                    if i >= 5 and i % 4 == 1:
                        head_norm(i // 4 - 1)
                    if i >= 6 and i % 4 == 2:
                        leave_out_t(i // 4 - 1)

                dve.wait_ge(bc1_in, 4 * LANDED * (l + 1))
                dve.wait_ge(v_out, TILES * LANDED * (l + 1))
                for t in range(TILES):
                    r, b, s = ROWS[t], t % 2, t // 4
                    dve.wait_ge(mixout_mm, TILES * l + t + 1)
                    if t >= 2:
                        dve.wait_ge(h_ready, TILES * l + t - 1)
                    row = norm_row[0:r, b, :]
                    V.tensor_tensor(row.rearrange("p (n c) -> p n c", n=2), pair[b][0:r, :, :],
                                    gate_bc[0:r, s, :].rearrange("p (n c) -> p n c", n=2), ALU.mult).then_inc(mix_read, 1)
                    dve.wait_ge(mix_read, TILES * l + t + 1)
                    seq(V.scalar_tensor_tensor(out=row, in0=x[0:r, t, :], scalar=ALPHA, in1=row, op0=ALU.mult, op1=ALU.add))
                    statistics(row, r).then_inc(var_done, 1)
                    dve.wait_ge(var_done, TILES * l + t + 1)
                    layer_norm_tail(row, row, r, std_done, TILES * l + t + 1).then_inc(normed, 1)

                dve.wait_ge(logit_mm, TILES * (l + 1))
                V.tensor_copy(logits[:, 0:4, :], bank(6)[:, 0:64].rearrange("p (t e) -> p t e", t=4))
                seq(V.tensor_copy(logits[0:DEC, 4, :], bank(6)[0:DEC, 64:80]))
                t_max, t_sum, t_inv = small[:, 0, 0:TILES], small[:, 1, 0:TILES], small[:, 2, 0:TILES]

                def over_e(v):
                    return v.unsqueeze(2).to_broadcast([P, TILES, EXPERTS])

                seq(V.reduce_max(t_max, logits[:, :, :], AX_X))
                V.tensor_tensor(logits[:, :, :], logits[:, :, :], over_e(t_max), ALU.subtract).then_inc(logit_max, 1)
                dve.wait_ge(logit_exp, l + 1)
                seq(V.reduce_sum(t_sum, score[:, :, :], AX_X))
                seq(V.reciprocal(t_inv, t_sum))
                seq(V.tensor_tensor(score[:, :, :], score[:, :, :], over_e(t_inv), ALU.mult))
                seq(V.tensor_tensor(sel[:, :, :], score[:, :, :], b_router[:, :].unsqueeze(1).to_broadcast([P, TILES, EXPERTS]), ALU.add))

                def count_better(out, v, n):
                    shape = [P, n, 4, 4]
                    vi = v.unsqueeze(2).to_broadcast(shape)
                    vj = v.unsqueeze(3).to_broadcast(shape)
                    ge, gt = cmp_ge[:, 0:n, :, :], cmp_gt[:, 0:n, :, :]
                    V.tensor_tensor(ge, vi, vj, ALU.is_ge)
                    seq(V.tensor_tensor(gt, vi, vj, ALU.is_gt))
                    V.tensor_tensor(ge, ge, lower[:, :, :].unsqueeze(1).to_broadcast(shape), ALU.mult)
                    seq(V.tensor_tensor(gt, gt, upper[:, :, :].unsqueeze(1).to_broadcast(shape), ALU.mult))
                    seq(V.tensor_tensor(ge, ge, gt, ALU.add))
                    seq(V.reduce_sum(out, ge, AX_X))

                by_group = "p t (g i) -> p (t g) i"
                sel_g = sel[:, :, :].rearrange(by_group, g=GROUPS)
                worse_g = worse[:, :, :].rearrange(by_group, g=GROUPS)
                mask_g = mask[:, :, :].rearrange(by_group, g=GROUPS)
                count_better(worse_g, sel_g, TILES * GROUPS)
                seq(V.tensor_scalar(mask_g, worse_g, float(TOP), None, ALU.is_lt))
                seq(V.tensor_tensor(worse_g, mask_g, sel_g, ALU.mult))
                group_score, group_rank = small[:, 3, :], small[:, 4, :]
                seq(V.reduce_sum(group_score, worse_g, AX_X))
                count_better(group_rank.rearrange("p (t g) -> p t g", t=TILES), group_score.rearrange("p (t g) -> p t g", t=TILES), TILES)
                seq(V.tensor_scalar(group_rank, group_rank, 1.0, None, ALU.is_lt))
                seq(V.tensor_tensor(mask_g, mask_g, group_rank.unsqueeze(2).to_broadcast([P, TILES * GROUPS, PER_GROUP]), ALU.mult))
                V.memset(mask[DEC:P, 4, :], 0.0).then_inc(mask_ready, 1)
                dve.wait_ge(mask_ready, l + 1)
                seq(V.tensor_tensor_scan(worse[:, :, :].rearrange("p t e -> p (t e)"), reset[:, :, :].rearrange("p t e -> p (t e)"),
                                         mask[:, :, :].rearrange("p t e -> p (t e)"), 0.0, ALU.mult, ALU.add))
                for k in range(TOP):
                    ins = V.scalar_tensor_tensor(out=picks[:, 2 + k, :, :], in0=worse[:, :, :], scalar=float(k + 1), in1=mask[:, :, :],
                                                 op0=ALU.is_equal, op1=ALU.mult)
                seq(ins)
                dve.wait_ge(rank_mm, l + 1)
                seq(V.tensor_scalar(cnt[:, 0, :], bank(7)[:, 80:96], float(TM - 1), None, ALU.add))
                seq(V.tensor_copy(cnt_i[:, 0, :], cnt[:, 0, :]))
                seq(V.tensor_scalar(cnt_i[:, 1, :], cnt_i[:, 0, :], TM.bit_length() - 1, None, ALU.arith_shift_right))
                seq(V.tensor_copy(cnt[:, 1, :], cnt_i[:, 1, :]))
                seq(V.tensor_scalar(cnt[:, 1, :], cnt[:, 1, :], 1.0, None, ALU.max))
                seq(V.tensor_tensor_scan(cnt[:, 2, :], cnt[:, 5, :], cnt[:, 1, :], 0.0, ALU.mult, ALU.add))
                seq(V.tensor_tensor(cnt[:, 3, :], cnt[:, 2, :], cnt[:, 1, :], ALU.subtract))
                V.tensor_copy(table[:, 0:16], cnt[:, 1, :])
                V.tensor_copy(table[:, 16:32], cnt[:, 3, :])
                V.tensor_copy(table[:, 32:33], cnt[:, 2, 15:16])
                seq(V.tensor_copy(table[:, 33:34], total[:, :]))
                V.tensor_tensor(total[:, :], total[:, :], cnt[:, 2, 15:16], ALU.add).then_inc(table_ready, 1)
                seq(V.tensor_scalar(cnt[:, 4, :], cnt[:, 3, :], float(TM), None, ALU.mult))
                seq(V.tensor_tensor(sel[:, :, :], bank(7)[:, 0:80].rearrange("p (t e) -> p t e", t=TILES),
                                    cnt[:, 4, :].unsqueeze(1).to_broadcast([P, TILES, EXPERTS]), ALU.add))
                V.tensor_tensor(picks[:, 0, :, :], picks[:, 2, :, :], sel[:, :, :], ALU.mult)
                seq(V.tensor_tensor(picks[:, 1, :, :], picks[:, 3, :, :], sel[:, :, :], ALU.mult))
                V.tensor_tensor(picks[:, 2, :, :], picks[:, 2, :, :], score[:, :, :], ALU.mult)
                seq(V.tensor_tensor(picks[:, 3, :, :], picks[:, 3, :, :], score[:, :, :], ALU.mult))
                seq(V.reduce_sum(pick[:, :, :], picks[:, :, :, :], AX_X))
                V.tensor_copy(slot_of[:, :, :], pick[:, 0:2, :]).then_inc(slots_ready, 1)
                seq(V.tensor_tensor(t_sum, pick[:, 2, :], pick[:, 3, :], ALU.add))
                seq(V.tensor_scalar(t_sum[DEC:P, 4:5], t_sum[DEC:P, 4:5], 1.0, None, ALU.add))
                seq(V.reciprocal(t_inv, t_sum))
                for k in range(TOP):
                    seq(V.tensor_tensor(pick[:, 2 + k, :], pick[:, 2 + k, :], t_inv, ALU.mult))
                dve.wait_ge(slot_mm, l + 1)
                V.tensor_copy(slot_token[:, :], bank(5)[0:TM, 0:MAX_TILES + 1]).then_inc(index_ready, 1)

                tiles = dve.value_load(table[0:1, 32:33], min_val=EXPERTS, max_val=MAX_TILES)
                base = dve.value_load(table[0:1, 33:34], min_val=0, max_val=DEPTH * MAX_TILES)
                with dve.Fori(0, tiles) as i:
                    for hf in range(2):
                        c = slice(hf * 256, hf * 256 + 256)
                        dve.wait_ge(silu_done, (base + i) * 2 + hf + 1)
                        V.tensor_tensor(act_row[0:TM, c], silu_g[TM:2 * TM, c], bank(hf)[TM:2 * TM, 0:256], ALU.mult).then_inc(act_done, 1)
                        dve.wait_ge(act_t_mm, (base + i) * 2 + hf + 1)
                        V.tensor_copy(act_t[:, 2 * hf:2 * hf + 2, :],
                                      bank((3, 5)[hf])[:, 0:2 * TM].rearrange("p (f t) -> p f t", f=2)).then_inc(act_t_done, 1)

                dve.wait_ge(bc2_in, 4 * LANDED * (l + 1))
                for t in range(TILES):
                    r, b, s = ROWS[t], t % 2, t // 4
                    picks_landed(dve, l, t)
                    dve.wait_ge(pick_scaled, TILES * l + t + 1)
                    row = mixed[0:r, b, :]
                    V.scalar_tensor_tensor(out=row, in0=picked[t % 4][0:r, 1, :], scalar=pick[0:r, 3, t:t + 1], in1=row,
                                           op0=ALU.mult, op1=ALU.add).then_inc(picked_read, 1)
                    dve.wait_ge(picked_read, TILES * l + t + 1)
                    seq(V.tensor_tensor(row, row, gate_bc[0:r, s, :], ALU.mult))
                    seq(V.scalar_tensor_tensor(out=row, in0=x[0:r, t, :], scalar=ALPHA, in1=row, op0=ALU.mult, op1=ALU.add))
                    statistics(row, r).then_inc(var2_done, 1)
                    dve.wait_ge(var2_done, TILES * l + t + 1)
                    layer_norm_tail(row, row, r, std2_done, TILES * l + t + 1).then_inc(normed2, 1)
                    if l + 1 < DEPTH and t == 0:
                        prepare_lambda(l + 1)
                    if l + 1 < DEPTH and t == 3:
                        prepare_columns(l + 1)

        @block.tensor
        def _(pe):
            mm, tr = nc.tensor.matmul, nc.tensor.transpose
            fills = [0] * ALL_SLOTS

            def weights(s):
                fills[s] += 1
                pe.wait_ge(landed[s], LANDED * fills[s])

            pe.sem_inc(tok_mm, 1)
            pe.wait_ge(const_ready, 1)
            pe.wait_ge(c_silu_ready, 1)
            tr(bank(7)[:, 0:16], c_silu[:, :], ident[0:16, 0:16]).then_inc(c_mm, 1)
            pe.wait_ge(c_ready, 1)

            def modulation(l, n):
                s4 = ADA_SLOTS[l][4 * n:4 * n + 4]
                for s in s4:
                    weights(s)
                for k in range(KD):
                    for j in range(4):
                        ins = mm(bank(ADA_BANK[n])[32 * j:32 * j + 32, :], c_t[:, k, :], by_k(s4[j])[:, k, :],
                                 start=(k == 0), stop=(k == KD - 1))
                ins.then_inc(ada_mm, 1)

            def columns(l):
                pe.wait_ge(mod_ready, 3 * l + 1)
                for b in range(4):
                    tr(bank(5)[:, b * P:(b + 1) * P], mod_row[:, 0, b * P:(b + 1) * P], ident[:, :])
                pe.wait_ge(small_in, 7 * LANDED * (l + 1))
                c = bank(4)
                tr(c[:, 32:45], vec_row[:, :], ident[0:13, 0:13])
                tr(c[:, 45:64], ident[0:19, :], ident[0:19, 0:19])
                for j in range(4):
                    tr(c[:, 64 + TAPS * j:64 + TAPS * (j + 1)], conv_w_row[:, j * P:(j + 1) * P], ident[0:TAPS, 0:TAPS])
                tr(c[:, 188:192], ident[0:4, :], ident[0:4, 0:4])
                for j in range(4):
                    ins = tr(c[:, 192 + STATE * j:192 + STATE * (j + 1)], state_row[:, j * P:(j + 1) * P], ident[0:STATE, 0:STATE])
                ins.then_inc(cols_mm, 1)

            modulation(0, 0)
            columns(0)
            for l in range(DEPTH):
                if l == 0:
                    pe.wait_ge(x_in, 2 * LANDED)
                else:
                    pe.wait_ge(x_done, TILES * l)
                for t in range(TILES):
                    r = ROWS[t]
                    for hf in range(2):
                        if hf == 0 and t == 0:
                            pe.wait_ge(cols_ready, l + 1)
                        if t:
                            pe.wait_ge((ht_dve, ht_act)[hf], TILES * l + t)
                        for k in range(4):
                            c0 = (4 * hf + k) * P
                            ins = tr(bank(4 + hf)[:, k * P:k * P + r], x[0:r, t, c0:c0 + P], ident[0:r, 0:r])
                        ins.then_inc(xt_mm, 1)
                pe.wait_ge(ht_dve, TILES * (l + 1))
                pe.wait_ge(ht_act, TILES * (l + 1))
                weights(0)
                weights(1)
                for j in range(4):
                    if j >= 2:
                        pe.wait_ge(glu_done, 4 * l + j - 1)
                    for part, s in ((1, 1), (0, 0)):
                        for k in range(KD):
                            mm(bank(2 * (j % 2) + part), by_k(s)[:, k, j * P:(j + 1) * P], h_t[:, k, 0:SEQ],
                               start=(k == 0), stop=(k == KD - 1))
                        for k in range(KD):
                            ins = mm(bank(6 + j % 2)[:, part * DEC:(part + 1) * DEC], by_k(s)[:, k, j * P:(j + 1) * P],
                                     h_t[:, k, SEQ:NTOK], start=(k == 0), stop=(k == KD - 1))
                    ins.then_inc(u_mm, 1)
                    if j in (0, 2):
                        modulation(l, 1 + j // 2)

                def project(i):
                    t, r, s = i % TILES, ROWS[i % TILES], (2, 3, 0)[i // TILES]
                    if t == 0:
                        weights(s)
                    if i < 4:
                        pe.wait_ge(glu_done, 4 * l + 4)
                    else:
                        pe.wait_ge(proj_act, pr_per * l + i - 3)
                    for k in range(KD):
                        ins = mm(bank(i % 4)[0:r, :], h_t[:, k, COL[t]:COL[t] + r], by_k(s)[:, k, :],
                                 start=(k == 0), stop=(k == KD - 1))
                    ins.then_inc(proj_mm, 1)

                def turn(i):
                    if i == 0:
                        pe.wait_ge(mod_ready, 3 * (l + 1))
                    if i >= 2:
                        pe.wait_ge(qk_t_done, qt_per * l + i - 1)
                    if i < 2 * TILES:
                        r = ROWS[i % TILES]
                        pe.wait_ge(proj_act, pr_per * l + i + 1)
                        pe.wait_ge(proj_rope, rope_per * l + i + 1)
                        src = qk_row[0:r, i % 2, :]
                    else:
                        r = P
                        pe.wait_ge(cache_k_in, LANDED * (l + 1))
                        src = cache_k_row[:, i - 2 * TILES, :]
                    for h in range(HEADS):
                        ins = tr(bank(4 + i % 2)[:, h * P:h * P + r], src[:, h * P:(h + 1) * P], ident[0:r, 0:r])
                    ins.then_inc(qk_t_mm, 1)

                if l == 0:
                    pe.wait_ge(setup_in, n_setup * LANDED)
                for i in range(3 * TILES):
                    if i <= 2 * TILES:
                        project(i)
                    if 2 <= i < qt_per + 2:
                        turn(i - 2)
                    if i == 2:
                        for b, c0 in enumerate((SEQ, GW - STATE)):
                            for j in range(4):
                                ins = tr(bank(6 + b)[0:STATE, j * P:(j + 1) * P], glu[:, j, c0:c0 + STATE], ident[:, :])
                            ins.then_inc(new_conv_mm, 1)
                    if i == TILES - 2:
                        pe.wait_ge(conv_done, 4 * (l + 1))
                        pe.wait_ge(new_conv_ready, 2 * (l + 1))
                        for b in range(2):
                            for j in range(4):
                                ins = mm(pair[3][:, b, 0:HALF], conv_mean[:, :], mix_t[:, 4 + j, b * HALF:(b + 1) * HALF],
                                         start=(j == 0), stop=(j == 3))
                        ins.then_inc(conv_stat_mm, 1)
                    if i == TILES + 1:
                        pe.wait_ge(squared, 4 * (l + 1))
                        for b in range(2):
                            for j in range(4):
                                ins = mm(pair[3][:, b, 0:HALF], conv_mean[:, :], glu[:, j, b * HALF:(b + 1) * HALF],
                                         start=(j == 0), stop=(j == 3))
                        ins.then_inc(conv_stat_mm, 1)

                def scores(i):
                    t, h, b = i // 4, i % 4, i % 2
                    r, keys = ROWS[t], (KEYS_S if t == 4 else (t + 1) * P)
                    kt = ks_t if t == 4 else k_t
                    if i >= 2:
                        pe.wait_ge(exp_done, at_per * l + i - 1)
                    pe.wait_ge(q_padded, at_per * l + i + 1)
                    for m in range(2):
                        ins = mm(pair[b][0:r, m, 0:keys], q_pad[:, i % 4, m, 0:r], kt[:, h, 0:keys], start=True, stop=True)
                    ins.then_inc(score_mm, 1)

                def key_blocks(t):
                    if t < 4:
                        return [(n * P, P, v_row[:, n, :]) for n in range(t + 1)]
                    return [(0, P, cache_v[:, 0, :]), (P, P, cache_v[:, 1, :]), (2 * P, DEC, v_row[0:DEC, 4, :])]

                def turn_attn(i):
                    t, b = i // 4, i % 2
                    r = ROWS[t]
                    pe.wait_ge(attn_done, at_per * l + i + 1)
                    if i >= 1:
                        pe.wait_ge(attn_t_done, at_per * l + i)
                    for c0, w, _ in key_blocks(t):
                        ins = tr(bank(4)[0:w, c0:c0 + r], attn[0:r, b, c0:c0 + w], ident[0:r, 0:r])
                    ins.then_inc(attn_t_mm, 1)

                def values(i):
                    t, h = i // 4, i % 4
                    r = ROWS[t]
                    pe.wait_ge(attn_t_done, at_per * l + i + 1)
                    if h == 0:
                        pe.wait_ge(proj_act, pr_per * l + 2 * TILES + t + 1)
                    if t == 4 and h == 0:
                        pe.wait_ge(cache_v_in, LANDED * (l + 1))
                    if h == 0 and t >= 2:
                        pe.wait_ge(out_t_done, TILES * l + t - 1)
                    blocks = key_blocks(t)
                    for n, (c0, w, v) in enumerate(blocks):
                        ins = mm(bank(6 + t % 2)[0:r, h * P:(h + 1) * P], attn_t[0:w, i % 2, c0:c0 + r], v[:, h * P:(h + 1) * P],
                                 start=(n == 0), stop=(n == len(blocks) - 1))
                    ins.then_inc(pv_mm, 1)

                def project_v_part(t, quarter):
                    if quarter == 0 and t >= 2:
                        pe.wait_ge(proj_act, pr_per * l + 2 * TILES + t)
                    for k in (2 * quarter, 2 * quarter + 1):
                        ins = mm(bank(5)[0:ROWS[t], :], h_t[:, k, COL[t]:COL[t] + ROWS[t]], by_k(0)[:, k, :],
                                 start=(k == 0), stop=(k == KD - 1))
                    if quarter == 3:
                        ins.then_inc(proj_mm, 1)

                def turn_out(t):
                    r = ROWS[t]
                    pe.wait_ge(out_normed, TILES * l + t + 1)
                    for h in range(HEADS):
                        ins = tr(bank(6 + t % 2)[:, h * P:h * P + r], out_row[0:r, h * P:(h + 1) * P], ident[0:r, 0:r])
                    ins.then_inc(out_t_mm, 1)

                pe.wait_ge(qk_t_done, qt_per * (l + 1))
                pe.wait_ge(proj_act, pr_per * l + 2 * TILES + 1)
                pe.wait_ge(conv_std, l + 1)
                scores(0)
                scores(1)
                for i in range(at_per + 3):
                    if i + 2 < at_per:
                        scores(i + 2)
                    if i < at_per - 4:
                        project_v_part(i // 4 + 1, i % 4)
                    if i < at_per:
                        turn_attn(i)
                    if 1 <= i <= at_per:
                        values(i - 1)
                    if i >= 6 and i % 4 == 2:
                        turn_out(i // 4 - 1)

                weights(1)
                weights(2)
                pe.wait_ge(conv_t_done, 4 * (l + 1))
                for t in range(TILES + 3):
                    if t < TILES:
                        r, b = ROWS[t], t % 2
                        pe.wait_ge(out_t_done, TILES * l + t + 1)
                        if t >= 2:
                            pe.wait_ge(mix_read, TILES * l + t - 1)
                        for n in range(2):
                            for k in range(KD):
                                ins = mm(pair[b][0:r, n, :], mix_t[:, k, MCOL[t]:MCOL[t] + r], by_k(1 + n)[:, k, :],
                                         start=(k == 0), stop=(k == KD - 1))
                        ins.then_inc(mixout_mm, 1)
                    if t >= 3:
                        u = t - 3
                        pe.wait_ge(route_t_done, 2 * (TILES * l + u + 1))
                        for k in range(KD):
                            ins = mm(bank(6)[0:ROWS[u], u * EXPERTS:(u + 1) * EXPERTS], route_t[k // 4][:, k % 4, 0:ROWS[u]],
                                     w_router[:, k, :], start=(k == 0), stop=(k == KD - 1))
                        ins.then_inc(logit_mm, 1)
                    if 2 <= t < TILES + 2:
                        u = t - 2
                        pe.wait_ge(h_ready, TILES * l + u + 1)
                        for hf in range(2):
                            if u >= 1:
                                pe.wait_ge(route_t_done, 2 * (TILES * l + u - 1) + hf + 1)
                            for k in range(4):
                                c0 = (4 * hf + k) * P
                                ins = tr(bank(4 + hf)[:, k * P:k * P + ROWS[u]], h_row[0:ROWS[u], u % 2, c0:c0 + P],
                                         ident[0:ROWS[u], 0:ROWS[u]])
                            ins.then_inc(route_t_mm, 1)
                pe.wait_ge(mask_ready, l + 1)
                for t in range(TILES):
                    for u in range(t + 1):
                        mm(bank(7)[:, t * EXPERTS:(t + 1) * EXPERTS], (ones if u < t else before)[:, :], mask[:, u, :],
                           start=(u == 0), stop=(u == t))
                for u in range(TILES):
                    ins = mm(bank(7)[:, 80:96], ones[:, :], mask[:, u, :], start=(u == 0), stop=(u == TILES - 1))
                ins.then_inc(rank_mm, 1)
                pe.wait_ge(slot_in, LANDED * (l + 1))
                tr(bank(5)[0:TM, 0:MAX_TILES + 1], slot_row[:, :], ident[0:MAX_TILES + 1, 0:MAX_TILES + 1]).then_inc(slot_mm, 1)

                pe.wait_ge(table_ready, l + 1)
                base = pe.value_load(table[0:1, 33:34], min_val=0, max_val=DEPTH * MAX_TILES)

                def turn_tokens():
                    for k in range(KD):
                        ins = tr(bank(2)[:, k * TM:(k + 1) * TM], gathered_row[:, k::KD], ident[0:TM, 0:TM])
                    ins.then_inc(tok_mm, 1)

                pe.wait_ge(index_ready, l + 1)
                pe.wait_ge(gathered, (base + l + 1) * LANDED)
                pe.sem_inc(pe_held, 1)
                turn_tokens()
                for e in range(EXPERTS):
                    for s in EXPERT_SLOTS[e % 3]:
                        weights(s)
                    s_down = EXPERT_SLOTS[e % 3][2]
                    n_tiles = pe.value_load(table[0:1, e:e + 1], min_val=1, max_val=NTOK // TM)
                    start = pe.value_load(table[0:1, 16 + e:17 + e], min_val=0, max_val=MAX_TILES - 1)
                    with pe.Fori(0, n_tiles) as g:
                        i = base + start + g
                        pe.wait_ge(tok_done, i + l + 1)

                        def up(hf, ks):
                            for k in ks:
                                for n in range(2):
                                    ins = mm(bank(hf)[n * TM:(n + 1) * TM, 0:256], tok_t[:, k, :],
                                             by_k(EXPERT_SLOTS[e % 3][n])[:, k, hf * 256:hf * 256 + 256], start=(k == 0), stop=(k == KD - 1))
                            return ins

                        def turn_act(hf):
                            pe.wait_ge(act_done, i * 2 + hf + 1)
                            pe.sem_inc(pe_held, 1)
                            for f in range(2):
                                ins = tr(bank((3, 5)[hf])[:, f * TM:(f + 1) * TM], act_row[0:TM, 256 * hf + f:256 * (hf + 1):2], ident[0:TM, 0:TM])
                            ins.then_inc(act_t_mm, 1)

                        def down(hf):
                            pe.wait_ge(act_t_done, i * 2 + hf + 1)
                            for f in range(2 * hf, 2 * hf + 2):
                                for n in range(2):
                                    ins = mm(bank(4)[n * TM:(n + 1) * TM, :], act_t[:, f, :], by_f(s_down)[:, f, n * 512:(n + 1) * 512],
                                             start=(f == 0), stop=(f == 3))
                            return ins

                        up(0, range(KD)).then_inc(up_mm, 1)
                        up(1, range(KD // 2))
                        turn_act(0)
                        up(1, range(KD // 2, KD)).then_inc(up_mm, 1)
                        pe.wait_ge(y_done, i + 1)
                        down(0)
                        turn_act(1)
                        pe.wait_ge(gathered, (i + l + 2) * LANDED)
                        pe.sem_inc(pe_held, 1)
                        turn_tokens()
                        down(1).then_inc(y_mm, 1)
                    pe.drain().then_inc(expert_done, 1)
                tiles = pe.value_load(table[0:1, 32:33], min_val=EXPERTS, max_val=MAX_TILES)
                pe.wait_ge(tok_done, base + tiles + l + 1)
                pe.wait_ge(y_done, base + tiles + 1)
                pe.sem_inc(pe_held, 1)
                if l + 1 < DEPTH:
                    modulation(l + 1, 0)
                    columns(l + 1)


_INS = ["x_prompt", "x_sample", "cache_k", "cache_v", "state_conv", "c_prompt", "c_sample", "w_ada", "b_ada", "w_in",
        "lambda_qk", "subln_g", "conv_w", "conv_b", "conv_ln_g", "conv_ln_b", "w_out", "ln1_g", "ln1_b", "ln2_g", "ln2_b",
        "w_router", "b_router", "w_gate", "w_up", "w_down"]
_OUTS = [("y_prompt", (1, SEQ, D)), ("y_sample", (1, DEC, D)),
         ("k_prompt", (DEPTH, 1, SEQ, HEADS, 2, HD)), ("v_prompt", (DEPTH, 1, SEQ, HEADS, 2 * HD)),
         ("conv_prompt", (DEPTH, 1, STATE, CONV)),
         ("k_sample", (DEPTH, 1, DEC, HEADS, 2, HD)), ("v_sample", (DEPTH, 1, DEC, HEADS, 2 * HD)),
         ("conv_sample", (DEPTH, 1, STATE, CONV))]


def rope_table():
    half = 8
    inv = np.power(np.float32(500000.0), -np.arange(half, dtype=np.float32) * np.float32(2.0) / np.float32(16))
    pos = np.concatenate([np.arange(SEQ), PAST + np.arange(DEC), np.zeros(TILES * P - NTOK)]).astype(np.float32)
    ang = pos[:, None] * inv[None, :].astype(np.float32)
    cos, sin = np.cos(ang), np.sin(ang)
    return np.concatenate([cos, cos, -sin, sin], 1).astype(np.float32)


def kernel(**inputs):
    import concourse.bacc as bacc
    from concourse.bass_utils import run_bass_kernel_spmd

    nc = bacc.Bacc("TRN2", target_bir_lowering=False, num_devices=1)
    arrays, aps = {}, {}
    constants = {"rope": rope_table(), "eps": np.full((P, 1), EPS, np.float32)}
    for name in _INS + list(constants):
        v = np.ascontiguousarray(constants[name] if name in constants else inputs[name])
        arrays[f"in_{name}"] = v
        aps[name] = nc.dram_tensor(f"in_{name}", v.shape, F32, kind="ExternalInput").ap()
    for name, shape in _OUTS:
        aps[name] = nc.dram_tensor(f"out_{name}", shape, F32, kind="ExternalOutput").ap()
    build(nc, aps)
    r = run_bass_kernel_spmd(nc, [arrays], core_ids=[0])
    return tuple(r.results[0][f"out_{name}"] for name, _ in _OUTS)
```

```python
import math
from contextlib import ExitStack

import concourse.bass as bass
import numpy as np
from concourse import mybir

ALU = mybir.AluOpType
ACT = mybir.ActivationFunctionType
F32 = mybir.dt.float32
I32 = mybir.dt.int32
AX_X = mybir.AxisListType.X

P = 128
D = 1024
DEPTH = 2
SEQ = 512
DEC = 64
PAST = 256
HEADS = 4
HD = 64
CONV = 512
TAPS = 31
STATE = TAPS - 1
DVE_TAPS = TAPS - 9
POOL_TAPS = TAPS - DVE_TAPS
EXPERTS = 16
GROUPS = 4
PER_GROUP = EXPERTS // GROUPS
TOP = 2
FE = 512
EPS = 1e-5
ALPHA = (2 * DEPTH) ** 0.25
SCALE = HD ** -0.5
NEG = -1e30

KD = D // P
NTOK = SEQ + DEC
TILES = 5
ROWS = [P, P, P, P, DEC]
COL = [0, 128, 256, 384, 512]
GAP = SEQ + STATE
MCOL = [0, 128, 256, 384, GAP]
MW = 640
CW = GAP + DEC
HALF = CW // 2
GW = SEQ + DEC + 2 * STATE
KEYS_S = PAST + DEC
ADA_CHUNKS = 6 * D // 512
CHUNK_W = KD * 512
SLOTS = 6
ALL_SLOTS = SLOTS + 3
ADA_SLOTS = [[2, 3, 6, 8] * 3,
             [0, 1, 3, 4, 6, 3, 8, 2, 6, 3, 8, 2]]
ADA_BANK = [6, 4, 5]
BUF_A, BUF_B, BUF_C = (0, 1, 2), (3, 4, 5), (6, 7, 8)
STREAMED = EXPERTS - 2
FIXED = 2
PARTS = 3
BLOCKS = [kind for g in range(2 * PARTS) for kind in (("s", 2 * g), ("s", 2 * g + 1), ("r", g))] + [("s", 12), ("s", 13)]
N_BLOCKS = len(BLOCKS)
T_COUNT, T_START, T_STREAM, T_RESIDENT, T_TILES, T_BASE = 0, 20, 40, 54, 56, 57
TM = 64
MAX_TILES = EXPERTS + TOP * NTOK // TM + 4
LANDED = 16


def lam_init(layer):
    return 0.8 - 0.6 * math.exp(-0.3 * layer)


def build(nc, a):
    with ExitStack() as ctx:
        def sb(name, shape, dt=F32):
            return ctx.enter_context(nc.sbuf_tensor(name, shape, dt))

        def sem(name):
            return ctx.enter_context(nc.semaphore(name))

        mod_dram = nc.dram_tensor("mod_scratch", (2, 6 * D), F32, kind="Internal").ap()
        h_dram = nc.dram_tensor("h_scratch", (NTOK, D), F32, kind="Internal").ap()
        y_dram = nc.dram_tensor("y_scratch", (MAX_TILES * TM, D), F32, kind="Internal").ap()

        ring = sb("ring", [P, SLOTS * CHUNK_W])
        x = sb("x", [P, TILES, D])
        reg_h = sb("reg_h", [P, KD * NTOK])
        reg_m = sb("reg_m", [P, KD * MW])
        reg_q = sb("reg_q", [P, HEADS * (NTOK + SEQ)])
        reg_v = sb("reg_v", [P, HEADS * KEYS_S + TILES * 512 + 2 * 512])

        def slot(s):
            if s < SLOTS:
                return ring[:, s * CHUNK_W:(s + 1) * CHUNK_W]
            return (reg_q, reg_h, reg_v)[s - SLOTS][:, 0:CHUNK_W]

        def by_k(s):
            return slot(s).rearrange("p (k c) -> p k c", k=KD)

        def by_f(s):
            return slot(s).rearrange("p (k c) -> p k c", k=FE // P)

        o = 4 * CHUNK_W
        glu = ring[:, o:o + 4 * GW].rearrange("p (j c) -> p j c", j=4)
        o += 4 * GW
        q_pad = ring[:, o - 4 * GW:o - 4 * GW + 1024].rearrange("p (b m t) -> p b m t", b=4, m=2)
        qk_row = ring[:, o:o + 1024].rearrange("p (b c) -> p b c", b=2)
        square = ring[:, o:o + 512]
        o += 1024
        prob = ring[:, o:o + 2048].rearrange("p (b m c) -> p b m c", b=2, m=2)
        cache_k_row = ring[:, o:o + 1024].rearrange("p (b c) -> p b c", b=2)
        sig = ring[:, o + 1024:o + 1024 + 2 * NTOK].rearrange("p (b c) -> p b c", b=2)
        new_conv = ring[:, o + 1024 + 2 * NTOK:o + 1024 + 2 * NTOK + 1024].rearrange("p (b c) -> p b c", b=2)
        o += 2048
        attn = ring[:, o:o + 1024].rearrange("p (b c) -> p b c", b=2)
        o += 1024
        attn_t = ring[:, o:o + 1024].rearrange("p (b c) -> p b c", b=2)
        o += 1024
        out_row = ring[:, o:o + 512]
        scaled = [ring[:, at:at + CW] for at in (o - 4096 - 1024 + n * CW for n in range(3))]
        pool_sum = scaled[2]
        odd_sum = ring[:, o - 600:o - 600 + CW]
        assert o + 512 <= SLOTS * CHUNK_W

        h_t = reg_h[:, :].rearrange("p (k t) -> p k t", k=KD)
        gate_bc = reg_h[:, 0:2 * D].rearrange("p (s c) -> p s c", s=2)
        ln_g_bc = reg_h[:, 2 * D:3 * D]
        ln_b_bc = reg_h[:, 3 * D:4 * D]
        gate2_bc = slot(2)[:, 0:2 * D].rearrange("p (s c) -> p s c", s=2)
        ln2_g_bc = slot(2)[:, 2 * D:3 * D]
        ln2_b_bc = slot(2)[:, 3 * D:4 * D]
        route_t = [reg_h[:, 4096:4608].rearrange("p (k t) -> p k t", k=4),
                   reg_v[:, 4096:4608].rearrange("p (k t) -> p k t", k=4)]

        mix_t = reg_m[:, :].rearrange("p (k t) -> p k t", k=KD)
        mod_row = reg_m[:, 0:1536].rearrange("p (r c) -> p r c", r=3)
        zeros = reg_m[:, 4096:4096 + D]
        gathered_row = reg_m[0:TM, 1536:2560]
        landing_row = reg_m[TM:2 * TM, 1536:2560]
        tok_t = reg_m[:, 2560:3072].rearrange("p (k t) -> p k t", k=KD)
        silu_g = reg_m[:, 3072:3584]
        act_row = reg_m[:, 3072:3584]
        act_t = reg_m[:, 3584:3840].rearrange("p (f t) -> p f t", f=4)
        y_row = reg_m[0:TM, 3840:4864]
        mixed = reg_m[:, 1536:3584].rearrange("p (b c) -> p b c", b=2)

        o = 1536
        sel = reg_m[:, o:o + 80].rearrange("p (t e) -> p t e", t=TILES)
        worse = reg_m[:, o + 80:o + 160].rearrange("p (t e) -> p t e", t=TILES)
        cmp_ge = reg_m[:, o + 160:o + 480].rearrange("p (g j i) -> p g j i", j=4, i=4)
        cmp_gt = reg_m[:, o + 480:o + 800].rearrange("p (g j i) -> p g j i", j=4, i=4)
        picks = reg_m[:, o + 800:o + 1120].rearrange("p (n t e) -> p n t e", n=4, t=TILES)

        o += 1120
        onehot = reg_m[:, o:o + 224].rearrange("p (s e) -> p s e", s=STREAMED)
        stream_pick = reg_m[:, o + 224:o + 672].rearrange("p (n s e) -> p n s e", n=2, s=STREAMED)
        stream_at = reg_m[:, o + 672:o + 896].rearrange("p (e s) -> p e s", s=STREAMED)
        o += 896
        stream_n = reg_m[:, o:o + 28].rearrange("p (n s) -> p n s", n=2)
        stream_start = reg_m[:, o + 28:o + 42]
        resident = reg_m[:, o + 42:o + 74].rearrange("p (r e) -> p r e", r=2)
        res_pick = reg_m[:, o + 74:o + 138].rearrange("p (n r e) -> p n r e", n=2, r=2)
        res_n = reg_m[:, o + 138:o + 142].rearrange("p (n r) -> p n r", n=2)
        part_n = reg_m[:, o + 142:o + 148].rearrange("p (r q) -> p r q", r=2)
        res_vals = reg_m[:, o + 148:o + 158].rearrange("p (v r) -> p v r", r=2)
        res_wide = reg_m[:, o + 158:o + 318].rearrange("p (v r e) -> p v r e", v=5, r=2)
        res_by_e = reg_m[:, o + 318:o + 398].rearrange("p (v e) -> p v e", v=5)
        block_n = reg_m[:, o + 398:o + 478].rearrange("p (n k) -> p n k", n=4)
        keys_e = reg_m[:, o + 478:o + 542].rearrange("p (n e) -> p n e", n=4)
        past = reg_m[:, o + 542:o + 702].rearrange("p (n t e) -> p n t e", n=2, t=TILES)
        offset_hot = reg_m[:, o + 702:o + 1342].rearrange("p (n b) -> p n b", b=TM)
        assert o + 1342 <= KD * MW
        tile_hot = stream_pick.rearrange("p n s e -> p (n s e)")[:, 0:TOP * TILES * (MAX_TILES + 2)].rearrange("p (n a) -> p n a", n=TOP * TILES)

        q_t = reg_q[:, 0:HEADS * NTOK].rearrange("p (h t) -> p h t", h=HEADS)
        k_t = reg_q[:, HEADS * NTOK:].rearrange("p (h t) -> p h t", h=HEADS)
        scale_bc = reg_q[:, 0:2048].rearrange("p (s c) -> p s c", s=2)
        shift_bc = reg_q[:, 2048:4096].rearrange("p (s c) -> p s c", s=2)

        ks_t = reg_v[:, 0:HEADS * KEYS_S].rearrange("p (h t) -> p h t", h=HEADS)
        v_row = reg_v[:, HEADS * KEYS_S:HEADS * KEYS_S + TILES * 512].rearrange("p (t c) -> p t c", t=TILES)
        cache_v = reg_v[:, HEADS * KEYS_S + TILES * 512:].rearrange("p (t c) -> p t c", t=2)
        norm_row = reg_v[:, 0:2048].rearrange("p (b c) -> p b c", b=2)
        h_row = reg_v[:, 2048:4096].rearrange("p (b c) -> p b c", b=2)
        picked = [at.rearrange("p (k c) -> p k c", k=TOP) for at in
                  (reg_v[:, 0:2048], reg_v[:, 2048:4096], slot(5)[:, 0:2048], slot(5)[:, 2048:4096])]

        ident = sb("ident", [P, P])
        ones = sb("ones", [P, P])
        conv_mean = sb("conv_mean", [P, P])
        before = sb("before", [P, P])
        w_router = sb("w_router_sb", [P, KD, EXPERTS])
        b_router = sb("b_router_sb", [P, EXPERTS])
        rope = sb("rope_sb", [P, TILES, 32])
        c_row = sb("c_row", [16, P])
        c_silu = sb("c_silu", [16, P])
        c_t = sb("c_t", [P, KD, 32])
        conv_w_row = sb("conv_w_row", [TAPS, CONV])
        state_row = sb("state_row", [STATE, CONV])
        lam_prod = sb("lam_prod", [P, 2, HD])
        vec_row = sb("vec_row", [13, P])
        lam_qk = sb("lam_qk", [P, 4, HD])
        cols = sb("cols", [P, 320])
        eps = sb("eps", [P, 1])
        lam_e = sb("lam_e", [P, 6])
        rope_t = sb("rope_t", [P, 2, 8, 16])
        row_max = sb("row_max", [P, 2, 2])
        neg_max = sb("neg_max", [P, 2, 2])
        row_sum = sb("row_sum", [P, 2, 2])
        row_inv = sb("row_inv", [P, 2, 2])
        head_ss = sb("head_ss", [P, 3, 4])
        stats = sb("stats", [P, 2, 6])
        mean_var = sb("mean_var", [P, 2])
        std = sb("std", [P, 2])
        logits = sb("logits", [P, TILES, EXPERTS])
        score = sb("score", [P, TILES, EXPERTS])
        mask = sb("mask", [P, TILES, EXPERTS])
        lower = sb("lower", [P, 4, 4])
        upper = sb("upper", [P, 4, 4])
        reset = sb("reset", [P, TILES, EXPERTS])
        small = sb("small", [P, 8, TILES * GROUPS])
        pick = sb("pick", [P, 4, TILES])
        slot_of = sb("slot_of", [P, 2, TILES], I32)
        cnt = sb("cnt", [P, 6, EXPERTS])
        cnt_i = sb("cnt_i", [P, 2, EXPERTS], I32)
        total = sb("total", [P, 1])
        table = sb("table", [P, 58], I32)
        plan = sb("plan", [P, 65 + TM])
        token_i = sb("token_i", [P, TILES], I32)
        token_f = sb("token_f", [P, TILES])
        slot_token = sb("slot_token", [TM, MAX_TILES + 2], I32)
        slot_now = sb("slot_now", [TM, 1], I32)

        pair = [ctx.enter_context(nc.psum_tensor(f"pair{i}", [P, 2, 512], F32)) for i in range(4)]

        def bank(b):
            return pair[b // 2][:, b % 2, :]

        const_ready = sem("const_ready")
        setup_in = sem("setup_in")
        setup_dve = sem("setup_dve")
        c_silu_ready = sem("c_silu_ready")
        c_mm = sem("c_mm")
        c_ready = sem("c_ready")
        landed = [sem(f"landed{s}") for s in range(ALL_SLOTS)]
        ada_in = sem("ada_in")
        small_in = sem("small_in")
        cache_k_in = sem("cache_k_in")
        cache_v_in = sem("cache_v_in")
        ada_mm = sem("ada_mm")
        mod_ready = sem("mod_ready")
        mod_out = sem("mod_out")
        c_in = sem("c_in")
        x_in = sem("x_in")
        cols_mm = sem("cols_mm")
        cols_ready = sem("cols_ready")
        lam_ready = sem("lam_ready")
        lam_exp = sem("lam_exp")
        xt_mm = sem("xt_mm")
        ht_dve = sem("ht_dve")
        ht_act = sem("ht_act")
        u_mm = sem("u_mm")
        sig_done = sem("sig_done")
        glu_done = sem("glu_done")
        conv_step = sem("conv_step")
        tap_scaled = sem("tap_scaled")
        tap_added = sem("tap_added")
        conv_done = sem("conv_done")
        new_conv_mm = sem("new_conv_mm")
        new_conv_ready = sem("new_conv_ready")
        new_conv_out = sem("new_conv_out")
        proj_mm = sem("proj_mm")
        proj_act = sem("proj_act")
        proj_rope = sem("proj_rope")
        qk_t_mm = sem("qk_t_mm")
        qk_t_done = sem("qk_t_done")
        k_out = [sem("k_out0"), sem("k_out1")]
        v_out = sem("v_out")
        conv_stat_mm = sem("conv_stat_mm")
        centred = sem("centred")
        squared = sem("squared")
        conv_std = sem("conv_std")
        conv_normed = sem("conv_normed")
        conv_t_done = sem("conv_t_done")
        q_padded = sem("q_padded")
        score_mm = sem("score_mm")
        max_done = sem("max_done")
        exp_done = sem("exp_done")
        attn_done = sem("attn_done")
        attn_t_mm = sem("attn_t_mm")
        attn_t_done = sem("attn_t_done")
        pv_mm = sem("pv_mm")
        out_row_done = sem("out_row_done")
        head_ss_done = sem("head_ss_done")
        head_std = sem("head_std")
        out_normed = sem("out_normed")
        out_t_mm = sem("out_t_mm")
        out_t_done = sem("out_t_done")
        bc1_in = sem("bc1_in")
        bcf_in = sem("bcf_in")
        bc2_in = sem("bc2_in")
        mixout_mm = sem("mixout_mm")
        mix_read = sem("mix_read")
        var_done = sem("var_done")
        std_done = sem("std_done")
        normed = sem("normed")
        h_ready = sem("h_ready")
        h_out = [sem("h_out0"), sem("h_out1")]
        route_t_mm = sem("route_t_mm")
        route_t_done = sem("route_t_done")
        logit_mm = sem("logit_mm")
        logit_max = sem("logit_max")
        logit_exp = sem("logit_exp")
        mask_ready = sem("mask_ready")
        rank_mm = sem("rank_mm")
        table_ready = sem("table_ready")
        slots_ready = sem("slots_ready")
        hot_ready = sem("hot_ready")
        slot_mm = sem("slot_mm")
        index_ready = sem("index_ready")
        index_now = sem("index_now")
        gathered = sem("gathered")
        rows_ready = sem("rows_ready")
        tok_mm = sem("tok_mm")
        tok_done = sem("tok_done")
        up_mm = sem("up_mm")
        silu_done = sem("silu_done")
        act_done = sem("act_done")
        act_t_mm = sem("act_t_mm")
        act_t_done = sem("act_t_done")
        y_mm = sem("y_mm")
        y_done = sem("y_done")
        y_out = sem("y_out")
        block_done = sem("block_done")
        picked_in = [sem(f"picked_in{b}") for b in range(4)]
        picked_read = sem("picked_read")
        pick_scaled = sem("pick_scaled")
        var2_done = sem("var2_done")
        std2_done = sem("std2_done")
        normed2 = sem("normed2")
        x_done = sem("x_done")
        final_out = sem("final_out")
        dve_step = sem("dve_step")
        pool_step = sem("pool_step")

        y_zeroed = sem("y_zeroed")
        pe_held = sem("pe_held")
        pool_held = sem("pool_held")

        n_setup = 5
        xt_per, pr_per, rope_per, qt_per, at_per = 2 * TILES, 3 * TILES, 2 * TILES, 2 * TILES + 2, TILES * HEADS

        block = ctx.enter_context(nc.Block())

        def picks_landed(eng, l, t):
            eng.wait_ge(picked_in[t % 4], TOP * LANDED * ((1 if t % 4 else 2) * l + t // 4 + 1))

        def load_small(sp, l):
            sp.dma_start(conv_w_row[:, :], a["conv_w"][l]).then_inc(small_in, LANDED)
            sp.dma_start(state_row[:, :], a["state_conv"][l, 0]).then_inc(small_in, LANDED)
            for n, name in enumerate(("conv_b", "conv_ln_g", "conv_ln_b")):
                sp.dma_start(vec_row[4 * n:4 * n + 4, :], a[name][l].rearrange("(k p) -> k p", p=P)).then_inc(small_in, LANDED)
            sp.dma_start(vec_row[12:13, :], a["subln_g"][l].rearrange("(k p) -> k p", p=P)).then_inc(small_in, LANDED)
            sp.dma_start(lam_qk[:, :, :], a["lambda_qk"][l].partition_broadcast(P)).then_inc(small_in, LANDED)

        @block.sync
        def _(sp):
            sp.dma_start(c_row[0:8, :], a["c_prompt"].rearrange("a (k p) -> (a k) p", p=P)).then_inc(c_in, LANDED)
            sp.dma_start(c_row[8:16, :], a["c_sample"].rearrange("a (k p) -> (a k) p", p=P)).then_inc(c_in, LANDED)
            fills = [0] * ALL_SLOTS
            in_flight = []
            in_layers = []

            def load(s, dst, src):
                while len(in_flight) >= (2 if in_layers else ALL_SLOTS):
                    before, count = in_flight.pop(0)
                    sp.wait_ge(landed[before], count)
                fills[s] += 1
                sp.dma_start(dst, src).then_inc(landed[s], LANDED)
                in_flight.append((s, LANDED * fills[s]))

            def load_ada(l, n):
                w_ada = a["w_ada"][l].rearrange("(k p) c -> p k c", p=P)
                load(ADA_SLOTS[l][n], by_k(ADA_SLOTS[l][n]), w_ada[:, :, n * 512:(n + 1) * 512])

            def load_in(l, s, c):
                w_in = a["w_in"][l].rearrange("(k p) c -> p k c", p=P)
                load(s, by_k(s), w_in[:, :, c * 512:(c + 1) * 512])

            def load_b_ada(l):
                for j in range(4):
                    sp.dma_start(mod_row[32 * j:32 * j + 2, :, :],
                                 a["b_ada"][l].rearrange("(r j c) -> j r c", j=4, c=512)[j].partition_broadcast(2)).then_inc(ada_in, LANDED)

            for l in range(DEPTH):
                if l == 0:
                    for n in range(4):
                        load_ada(0, n)
                    sp.wait_ge(setup_dve, 1)
                    load_b_ada(0)
                    load_small(sp, 0)
                    sp.dma_start(x[:, 0:4, :], a["x_prompt"][0].rearrange("(t p) d -> p t d", p=P)).then_inc(x_in, LANDED)
                    sp.dma_start(x[0:DEC, 4, :], a["x_sample"][0]).then_inc(x_in, LANDED)
                    sp.dma_start(eps[:, :], a["eps"]).then_inc(setup_in, LANDED)
                    sp.dma_start(plan[:, :], a["plan"].rearrange("a c -> (a c)").partition_broadcast(P)).then_inc(setup_in, LANDED)
                    load_in(l, 0, 3)
                    load_in(l, 1, 4)
                    sp.dma_start(w_router[:, :, :], a["w_router"].rearrange("(k p) e -> p k e", p=P)).then_inc(setup_in, LANDED)
                    sp.dma_start(b_router[:, :], a["b_router"].partition_broadcast(P)).then_inc(setup_in, LANDED)
                    sp.dma_start(rope[:, :, :], a["rope"].rearrange("(t p) c -> p t c", p=P)).then_inc(setup_in, LANDED)
                    for n in range(4, 8):
                        if n == 4:
                            sp.wait_ge(ada_mm, 1)
                        load_ada(0, n)
                else:
                    sp.wait_ge(picked_read, TILES * l)
                    load_ada(l, 6)
                    sp.wait_ge(x_done, TILES * l)
                    load_ada(l, 7)
                in_layers.append(l)
                sp.wait_ge(ada_mm, 3 * l + 2)
                for n in range(8, ADA_CHUNKS):
                    load_ada(l, n)
                sp.wait_ge(ada_mm, 3 * l + 3)
                load_in(l, 2, 0)
                load_in(l, 3, 1)
                sp.wait_ge(u_mm, 4 * l + 4)
                load_in(l, 0, 2)
                w_out = a["w_out"][l].rearrange("(k p) c -> p k c", p=P)
                load(1, by_k(1), w_out[:, :, 0:512])
                sp.wait_ge(proj_mm, pr_per * l + TILES)
                load(2, by_k(2), w_out[:, :, 512:1024])
                def up_rows(name, e):
                    return a[name][l].rearrange("e (p k) c -> p e k c", p=P)[:, e, :, :]

                def down_rows(e):
                    return a["w_down"][l].rearrange("e (h p k) c -> p e h k c", h=2, k=2)[:, e, :, :, :]

                def load_k(s, src):
                    load(s, by_k(s).unsqueeze(1), src)

                def load_f(s, e):
                    load(s, slot(s).rearrange("p (a h k c) -> p a h k c", a=1, h=2, k=2), down_rows(e))

                def load_expert(buffer, e):
                    load_k(buffer[0], up_rows("w_gate", e))
                    load_k(buffer[1], up_rows("w_up", e))
                    load_f(buffer[2], e)

                sp.wait_ge(proj_mm, pr_per * l + 2 * TILES)
                load_k(3, up_rows("w_gate", slice(0, 1)))
                sp.wait_ge(out_t_mm, TILES * (l + 1))
                sp.wait_ge(out_t_done, TILES * (l + 1))
                sp.wait_ge(conv_t_done, 4 * (l + 1))
                load_k(4, up_rows("w_up", slice(0, 1)))
                load_f(5, slice(0, 1))
                sp.wait_ge(h_ready, TILES * (l + 1))
                load_k(6, up_rows("w_gate", slice(1, 2)))
                load_k(7, up_rows("w_up", slice(1, 2)))
                sp.wait_ge(h_out[0], 3 * LANDED * (l + 1))
                sp.wait_ge(h_out[1], 2 * LANDED * (l + 1))
                sp.wait_ge(route_t_mm, 2 * TILES * (l + 1))
                load_f(8, slice(1, 2))
                sp.wait_ge(table_ready, l + 1)
                for r in range(2):
                    res = sp.value_load(table[0:1, T_RESIDENT + r:T_RESIDENT + r + 1], min_val=0, max_val=EXPERTS - 1)
                    if r == 0:
                        sp.wait_ge(mixout_mm, TILES * (l + 1))
                    else:
                        sp.wait_ge(block_done, N_BLOCKS * l + BLOCKS.index(("r", PARTS - 1)) + 1)
                    load_expert(BUF_A, bass.ds(res, 1))
                    for n in range(2 if r == 0 else 8, 8 if r == 0 else STREAMED):
                        e = sp.value_load(table[0:1, T_STREAM + n:T_STREAM + n + 1], min_val=0, max_val=EXPERTS - 1)
                        sp.wait_ge(block_done, N_BLOCKS * l + BLOCKS.index(("s", n - 2)) + 1)
                        load_expert((BUF_B, BUF_C)[n % 2], bass.ds(e, 1))
                        if n == 3 and l + 1 < DEPTH:
                            load_b_ada(l + 1)
                            load_small(sp, l + 1)
                sp.wait_ge(block_done, N_BLOCKS * l + BLOCKS.index(("r", 2 * PARTS - 1)) + 1)
                for s in range(2):
                    sp.dma_start(gate2_bc[:, s, :], mod_dram[s, 5 * D:6 * D].partition_broadcast(P)).then_inc(bc2_in, LANDED)
                sp.dma_start(ln2_g_bc, a["ln2_g"][l].partition_broadcast(P)).then_inc(bc2_in, LANDED)
                sp.dma_start(ln2_b_bc, a["ln2_b"][l].partition_broadcast(P)).then_inc(bc2_in, LANDED)
                if l + 1 < DEPTH:
                    load_ada(l + 1, 0)
                    load_ada(l + 1, 1)
                    sp.wait_ge(block_done, N_BLOCKS * (l + 1) - 1)
                    load_ada(l + 1, 2)
                    load_ada(l + 1, 3)
                    for t in range(4):
                        picks_landed(sp, l, t)
                    sp.wait_ge(ada_mm, 3 * (l + 1) + 1)
                    load_in(l + 1, 0, 3)
                    load_in(l + 1, 1, 4)
                    load_ada(l + 1, 4)
                    load_ada(l + 1, 5)
            sp.wait_ge(x_done, TILES * DEPTH)
            sp.dma_start(a["y_prompt"][0].rearrange("(t p) d -> p t d", p=P), x[:, 0:4, :]).then_inc(final_out, LANDED)
            sp.dma_start(a["y_sample"][0], x[0:DEC, 4, :]).then_inc(final_out, LANDED)
            sp.wait_ge(final_out, 2 * LANDED)

        @block.gpsimd
        def _(pool):
            steps = [0]

            def seq(ins):
                steps[0] += 1
                ins.then_inc(pool_step, 1)
                pool.wait_ge(pool_step, steps[0])

            seq(pool.memset(ident[:, :], 0.0))
            seq(pool.affine_select(out=ident[:, :], in_=ident[:, :], compare_op=ALU.not_equal, fill=1.0,
                                   base=0, pattern=[[-1, P]], channel_multiplier=1))
            seq(pool.memset(ones[:, :], 1.0))
            seq(pool.memset(conv_mean[:, :], 1.0 / CONV))
            seq(pool.affine_select(out=before[:, :], in_=ones[:, :], compare_op=ALU.is_gt, fill=0.0,
                                   base=0, pattern=[[1, P]], channel_multiplier=-1))
            four = ones[:, 0:16].rearrange("p (j i) -> p j i", j=4)
            seq(pool.affine_select(out=lower[:, :, :], in_=four, compare_op=ALU.is_gt, fill=0.0,
                                   base=0, pattern=[[1, 4], [-1, 4]], channel_multiplier=0))
            seq(pool.affine_select(out=upper[:, :, :], in_=four, compare_op=ALU.is_gt, fill=0.0,
                                   base=0, pattern=[[-1, 4], [1, 4]], channel_multiplier=0))
            seq(pool.iota(token_i[:, :], pattern=[[P, TILES]], base=0, channel_multiplier=1))
            seq(pool.memset(zeros, 0.0))
            pool.memset(total[:, :], 0.0).then_inc(const_ready, 1)

            for l in range(DEPTH):
                if l == 0:
                    pool.dma_start(y_dram[EXPERTS * TM:, :].rearrange("(n p) d -> p n d", p=P),
                                   zeros.unsqueeze(1).to_broadcast([P, (MAX_TILES - EXPERTS) * TM // P, D])).then_inc(y_zeroed, LANDED)
                for n in range(4 * l * POOL_TAPS, 4 * (l + 1) * POOL_TAPS):
                    w = n % POOL_TAPS
                    pool.wait_ge(tap_scaled, n + 1)
                    if w:
                        ins = pool.tensor_tensor(pool_sum, pool_sum, scaled[n % 2], ALU.add)
                    else:
                        if n > 4 * l * POOL_TAPS:
                            pool.wait_ge(conv_done, n // POOL_TAPS)
                        ins = pool.tensor_copy(pool_sum, scaled[n % 2])
                    ins.then_inc(tap_added, 1)
                    pool.wait_ge(tap_added, n + 1)
                pool.wait_ge(mod_ready, 3 * (l + 1))
                for s in range(2):
                    dst = mod_dram[s].rearrange("(r j c) -> j r c", j=4, c=512)
                    pool.dma_start(dst[:, 1:3, :], mod_row[s:s + 97:32, 1:3, :]).then_inc(mod_out, LANDED)
                pool.wait_ge(ada_mm, 3 * (l + 1))
                pool.wait_ge(conv_done, 4 * (l + 1))
                pool.dma_start(cache_k_row[:, :, :],
                               a["cache_k"][l, 0].rearrange("(t p) h m c -> p t (h m c)", p=P)).then_inc(cache_k_in, LANDED)
                if l:
                    pool.wait_ge(picked_read, TILES * l)
                pool.dma_start(cache_v[:, :, :], a["cache_v"][l, 0].rearrange("(t p) h c -> p t (h c)", p=P)).then_inc(cache_v_in, LANDED)
                pool.wait_ge(new_conv_ready, 2 * (l + 1))
                pool.dma_start(a["conv_prompt"][l, 0], new_conv[0:STATE, 0, :]).then_inc(new_conv_out, LANDED)
                pool.dma_start(a["conv_sample"][l, 0], new_conv[0:STATE, 1, :]).then_inc(new_conv_out, LANDED)
                for t in range(TILES):
                    i = TILES + t
                    pool.wait_ge(proj_act, pr_per * l + i + 1)
                    pool.wait_ge(proj_rope, rope_per * l + i + 1)
                    dst = a["k_sample"][l, 0] if t == 4 else a["k_prompt"][l, 0, t * P:(t + 1) * P]
                    pool.dma_start(dst.rearrange("t h m c -> t (h m c)"),
                                   qk_row[0:ROWS[t], i % 2, :]).then_inc(k_out[i % 2], LANDED)
                pool.wait_ge(conv_normed, 4 * (l + 1))
                seq(pool.memset(q_pad[:, :, :, :], 0.0))

                def pad_q(i):
                    t, h, b = i // 4, i % 4, i % 4
                    r = ROWS[t]
                    pool.wait_ge(qk_t_done, qt_per * l + t + 1)
                    if i >= 4:
                        pool.wait_ge(score_mm, at_per * l + i - 3)
                    for m in range(2):
                        half = slice(HD * m, HD * m + HD)
                        ins = pool.tensor_copy(q_pad[half, b, m, 0:r], q_t[half, h, COL[t]:COL[t] + r])
                    ins.then_inc(q_padded, 1)

                for i in range(4):
                    pad_q(i)
                def store_v(t):
                    pool.wait_ge(proj_act, pr_per * l + 2 * TILES + t + 1)
                    dst = a["v_sample"][l, 0] if t == 4 else a["v_prompt"][l, 0, t * P:(t + 1) * P]
                    pool.dma_start(dst.rearrange("t h c -> t (h c)"), v_row[0:ROWS[t], t, :]).then_inc(v_out, LANDED)

                for i in range(4, at_per):
                    pad_q(i)
                    if i % 4 == 2 and i > 4:
                        store_v(i // 4)
                    if i == 4:
                        store_v(0)
                pool.wait_ge(mod_out, 2 * LANDED * (l + 1))
                pool.wait_ge(proj_mm, pr_per * (l + 1))
                for s in range(2):
                    pool.dma_start(gate_bc[:, s, :], mod_dram[s, 2 * D:3 * D].partition_broadcast(P)).then_inc(bc1_in, LANDED)
                pool.dma_start(ln_g_bc, a["ln1_g"][l].partition_broadcast(P)).then_inc(bc1_in, LANDED)
                pool.dma_start(ln_b_bc, a["ln1_b"][l].partition_broadcast(P)).then_inc(bc1_in, LANDED)
                pool.wait_ge(score_mm, at_per * (l + 1))
                for s in range(2):
                    pool.dma_start(shift_bc[:, s, :], mod_dram[s, 3 * D:4 * D].partition_broadcast(P)).then_inc(bcf_in, LANDED)
                    pool.dma_start(scale_bc[:, s, :], mod_dram[s, 4 * D:5 * D].partition_broadcast(P)).then_inc(bcf_in, LANDED)
                pool.wait_ge(bcf_in, 4 * LANDED * (l + 1))
                seq(pool.tensor_scalar(scale_bc[:, :, :], scale_bc[:, :, :], 1.0, 0.0, ALU.add, ALU.add))
                pool.wait_ge(bc1_in, 4 * LANDED * (l + 1))
                for t in range(TILES):
                    r, b, s = ROWS[t], t % 2, t // 4
                    pool.wait_ge(normed, TILES * l + t + 1)
                    seq(pool.tensor_tensor(x[0:r, t, :], norm_row[0:r, b, :], ln_g_bc[0:r, :], ALU.mult))
                    seq(pool.tensor_tensor(x[0:r, t, :], x[0:r, t, :], ln_b_bc[0:r, :], ALU.add))
                    if t >= 2:
                        pool.wait_ge(route_t_mm, 2 * (TILES * l + t - 1))
                        pool.wait_ge(h_out[b], LANDED * (3 * l + t // 2 if b == 0 else 2 * l + t // 2))
                    seq(pool.tensor_tensor(h_row[0:r, b, :], x[0:r, t, :], scale_bc[0:r, s, :], ALU.mult))
                    pool.tensor_tensor(h_row[0:r, b, :], h_row[0:r, b, :], shift_bc[0:r, s, :], ALU.add).then_inc(h_ready, 1)
                    pool.wait_ge(h_ready, TILES * l + t + 1)
                    pool.dma_start(h_dram[t * P:t * P + r, :], h_row[0:r, b, :]).then_inc(h_out[b], LANDED)
                pool.wait_ge(index_ready, l + 1)
                pool.wait_ge(h_out[0], 3 * LANDED * (l + 1))
                pool.wait_ge(h_out[1], 2 * LANDED * (l + 1))
                pool.wait_ge(table_ready, l + 1)
                tiles = pool.value_load(table[0:1, T_TILES:T_TILES + 1], min_val=EXPERTS, max_val=MAX_TILES)
                base = pool.value_load(table[0:1, T_BASE:T_BASE + 1], min_val=0, max_val=DEPTH * MAX_TILES)
                pool.indirect_dma_start(landing_row, None, h_dram,
                                        bass.IndirectOffsetOnAxis(slot_token[:, 0:1], 0)).then_inc(gathered, LANDED)
                with pool.Fori(0, tiles + 1) as i:
                    pool.wait_ge(gathered, (base + 2 * l + i + 1) * LANDED)
                    pool.sem_inc(pool_held, 1)
                    pool.tensor_copy(slot_now[:, :], slot_token[:, bass.ds(i + 1, 1)]).then_inc(index_now, 1)
                    pool.wait_ge(tok_mm, base + l + i + 1)
                    pool.sem_inc(pool_held, 1)
                    pool.tensor_copy(gathered_row, landing_row).then_inc(rows_ready, 1)
                    pool.wait_ge(index_now, base + l + i + 1)
                    pool.wait_ge(rows_ready, base + l + i + 1)
                    pool.sem_inc(pool_held, 1)
                    pool.indirect_dma_start(landing_row, None, h_dram,
                                            bass.IndirectOffsetOnAxis(slot_now[:, 0:1], 0)).then_inc(gathered, LANDED)
                pool.wait_ge(gathered, (base + tiles + 2 * l + 2) * LANDED)
                pool.sem_inc(pool_held, 1)
                pool.wait_ge(y_out, LANDED * (base + tiles + 1))
                pool.sem_inc(pool_held, 1)
                pool.wait_ge(bc2_in, 4 * LANDED * (l + 1))
                def pick_rows(t):
                    r, b = ROWS[t], t % 4
                    for k in range(TOP):
                        pool.indirect_dma_start(picked[b][0:r, k, :], None, y_dram,
                                                bass.IndirectOffsetOnAxis(slot_of[0:r, k, t:t + 1], 0)).then_inc(picked_in[b], LANDED)

                for t in range(4):
                    pick_rows(t)
                pool.wait_ge(picked_read, TILES * l + 1)
                pick_rows(4)
                for t in range(TILES):
                    r, b = ROWS[t], t % 2
                    pool.wait_ge(normed2, TILES * l + t + 1)
                    seq(pool.tensor_tensor(x[0:r, t, :], mixed[0:r, b, :], ln2_g_bc[0:r, :], ALU.mult))
                    pool.tensor_tensor(x[0:r, t, :], x[0:r, t, :], ln2_b_bc[0:r, :], ALU.add).then_inc(x_done, 1)
            for n, s in ((2 * DEPTH, new_conv_out), (2 * DEPTH, k_out[0]), (3 * DEPTH, k_out[1]), (TILES * DEPTH, v_out)):
                pool.wait_ge(s, n * LANDED)

        @block.scalar
        def _(act):
            A = nc.scalar.activation
            act.sem_inc(y_done, 1)
            act.sem_inc(y_out, LANDED)
            act.wait_ge(c_in, 2 * LANDED)
            A(c_silu[:, :], c_row[:, :], ACT.Silu).then_inc(c_silu_ready, 1)

            def lambda_exp(l):
                act.wait_ge(lam_ready, 2 * l + 1)
                A(lam_e[:, 2:4], lam_e[:, 0:2], ACT.Exp).then_inc(lam_exp, 1)

            lambda_exp(0)
            for l in range(DEPTH):
                act.wait_ge(cols_ready, l + 1)
                for t in range(TILES):
                    r, s = ROWS[t], t // 4
                    act.wait_ge(xt_mm, xt_per * l + 2 * t + 2)
                    for k in range(4):
                        ins = A(h_t[:, 4 + k, COL[t]:COL[t] + r], bank(5)[:, k * P:k * P + r], ACT.Identity,
                                bias=cols[:, 16 * s + 4 + k:16 * s + 5 + k], scale=cols[:, 16 * s + 12 + k:16 * s + 13 + k])
                    ins.then_inc(ht_act, 1)
                for j in range(4):
                    act.wait_ge(u_mm, 4 * l + j + 1)
                    if j >= 2:
                        act.wait_ge(glu_done, 4 * l + j - 1)
                    A(sig[:, j % 2, 0:SEQ], bank(2 * (j % 2) + 1), ACT.Sigmoid)
                    A(sig[:, j % 2, SEQ:NTOK], bank(6 + j % 2)[:, DEC:2 * DEC], ACT.Sigmoid).then_inc(sig_done, 1)
                    act.wait_ge(glu_done, 4 * l + j + 1)
                    for w in range(POOL_TAPS):
                        n = (4 * l + j) * POOL_TAPS + w
                        if n >= 2:
                            act.wait_ge(tap_added, n - 1)
                        c = DVE_TAPS + w
                        A(scaled[n % 2], glu[:, j, c:c + CW], ACT.Copy,
                          scale=cols[:, 64 + TAPS * j + c:65 + TAPS * j + c]).then_inc(tap_scaled, 1)
                act.wait_ge(conv_done, 4 * (l + 1))

                def leave_t(i):
                    act.wait_ge(qk_t_mm, qt_per * l + i + 1)
                    kind, t = i // TILES, i % TILES
                    r = ROWS[t] if kind < 2 else P
                    if kind == 0:
                        dst = q_t[:, :, COL[t]:COL[t] + r]
                    elif kind == 1 and t < 4:
                        dst = k_t[:, :, t * P:t * P + r]
                    elif kind == 1:
                        dst = ks_t[:, :, PAST:KEYS_S]
                    else:
                        dst = ks_t[:, :, t * P:t * P + P]
                    src = bank(4 + i % 2).rearrange("p (h t) -> p h t", h=HEADS)[:, :, 0:r]
                    A(dst, src, ACT.Copy).then_inc(qk_t_done, 1)

                if l:
                    act.wait_ge(picked_read, TILES * l)
                for i in range(3 * TILES):
                    t, r = i % TILES, ROWS[i % TILES]
                    if i <= 2 * TILES:
                        act.wait_ge(proj_mm, pr_per * l + i + 1)
                    if i < 2 * TILES:
                        if i >= 2:
                            act.wait_ge(qk_t_mm, qt_per * l + i - 1)
                        if i >= TILES + 2:
                            act.wait_ge(k_out[i % 2], LANDED * ((3 if i % 2 else 2) * l + (i - TILES) // 2))
                        A(qk_row[0:r, i % 2, :], bank(i % 4)[0:r, :], ACT.Copy).then_inc(proj_act, 1)
                    elif i == 2 * TILES:
                        A(v_row[0:r, t, :], bank(i % 4)[0:r, :], ACT.Copy).then_inc(proj_act, 1)
                    if 2 <= i < 2 * TILES + 4:
                        leave_t(i - 2)
                    if i == 2:
                        for b in range(2):
                            act.wait_ge(new_conv_mm, 2 * l + b + 1)
                            A(new_conv[0:STATE, b, :], bank(6 + b)[0:STATE, :], ACT.Copy).then_inc(new_conv_ready, 1)
                    if i == TILES - 1:
                        for j in range(4):
                            act.wait_ge(centred, 4 * l + j + 1)
                            A(glu[:, j, 0:CW], mix_t[:, 4 + j, 0:CW], ACT.Square).then_inc(squared, 1)
                    if i == TILES + 2:
                        act.wait_ge(conv_stat_mm, 2 * l + 2)
                        A(glu[:, 0, 0:CW].rearrange("p (b c) -> p b c", b=2), pair[3][:, :, 0:HALF], ACT.Sqrt,
                          bias=eps[:, :]).then_inc(conv_std, 1)
                    if i == 2 * TILES + 2:
                        for j in range(4):
                            act.wait_ge(conv_normed, 4 * l + j + 1)
                            A(mix_t[:, 4 + j, 0:CW], mix_t[:, 4 + j, 0:CW], ACT.Silu,
                              bias=cols[:, 40 + j:41 + j], scale=cols[:, 36 + j:37 + j]).then_inc(conv_t_done, 1)

                def exps(i):
                    r, keys, b = ROWS[i // 4], (KEYS_S if i // 4 == 4 else (i // 4 + 1) * P), i % 2
                    act.wait_ge(max_done, at_per * l + i + 1)
                    if i >= 2:
                        act.wait_ge(attn_done, at_per * l + i - 1)
                    for m in range(2):
                        ins = A(prob[0:r, b, m, 0:keys], pair[b][0:r, m, 0:keys], ACT.Exp,
                                bias=neg_max[0:r, b, m:m + 1], scale=SCALE, accum_out=row_sum[0:r, b, m:m + 1])
                    ins.then_inc(exp_done, 1)

                def leave_attn_t(i):
                    t = i // 4
                    act.wait_ge(attn_t_mm, at_per * l + i + 1)
                    if i >= 2:
                        act.wait_ge(pv_mm, at_per * l + i - 1)
                    if t < 4:
                        ins = A(attn_t[:, i % 2, 0:(t + 1) * P], bank(4)[:, 0:(t + 1) * P], ACT.Copy)
                    else:
                        A(attn_t[:, i % 2, 0:2 * P].rearrange("p (k t) -> p k t", k=2)[:, :, 0:DEC],
                          bank(4)[:, 0:2 * P].rearrange("p (k t) -> p k t", k=2)[:, :, 0:DEC], ACT.Copy)
                        ins = A(attn_t[0:DEC, i % 2, 2 * P:2 * P + DEC], bank(4)[0:DEC, 2 * P:2 * P + DEC], ACT.Copy)
                    ins.then_inc(attn_t_done, 1)

                def leave_out(t):
                    act.wait_ge(pv_mm, at_per * l + 4 * t + 4)
                    if t >= 1:
                        act.wait_ge(out_t_mm, TILES * l + t)
                    A(out_row[0:ROWS[t], :], bank(6 + t % 2)[0:ROWS[t], :], ACT.Copy).then_inc(out_row_done, 1)

                def head_sqrt(t):
                    act.wait_ge(head_ss_done, TILES * l + t + 1)
                    A(head_ss[0:ROWS[t], 1, :], head_ss[0:ROWS[t], 0, :], ACT.Sqrt, bias=eps[0:ROWS[t], :],
                      scale=1.0 / P).then_inc(head_std, 1)

                act.wait_ge(new_conv_out, 2 * LANDED * (l + 1))
                exps(0)
                for i in range(at_per + 2):
                    if i + 1 < at_per:
                        exps(i + 1)
                    if i < at_per:
                        leave_attn_t(i)
                    if i % 4 == 3 and i < at_per - 4:
                        t = i // 4 + 1
                        act.wait_ge(proj_mm, pr_per * l + 2 * TILES + t + 1)
                        A(v_row[0:ROWS[t], t, :], bank(5)[0:ROWS[t], :], ACT.Copy).then_inc(proj_act, 1)
                    if i >= 4 and i % 4 == 0:
                        leave_out(i // 4 - 1)
                    if i >= 5 and i % 4 == 1:
                        head_sqrt(i // 4 - 1)

                for t in range(TILES + 2):
                    if t < TILES:
                        act.wait_ge(var_done, TILES * l + t + 1)
                        A(std[0:ROWS[t], 0:1], mean_var[0:ROWS[t], 1:2], ACT.Sqrt, bias=eps[0:ROWS[t], :]).then_inc(std_done, 1)
                    if t >= 2:
                        u = t - 2
                        for hf in range(2):
                            act.wait_ge(route_t_mm, 2 * (TILES * l + u) + hf + 1)
                            if u >= 1:
                                act.wait_ge(logit_mm, TILES * l + u)
                            A(route_t[hf][:, :, 0:ROWS[u]],
                              bank(4 + hf).rearrange("p (k t) -> p k t", k=4)[:, :, 0:ROWS[u]], ACT.Copy).then_inc(route_t_done, 1)
                act.wait_ge(logit_max, l + 1)
                A(score[:, :, :], logits[:, :, :], ACT.Exp).then_inc(logit_exp, 1)

                act.wait_ge(table_ready, l + 1)
                tiles = act.value_load(table[0:1, T_TILES:T_TILES + 1], min_val=EXPERTS, max_val=MAX_TILES)
                base = act.value_load(table[0:1, T_BASE:T_BASE + 1], min_val=0, max_val=DEPTH * MAX_TILES)
                act.wait_ge(tok_mm, base + l + 2)
                A(tok_t[:, :, :], bank(2).rearrange("p (k t) -> p k t", k=KD), ACT.Copy).then_inc(tok_done, 1)
                with act.Fori(0, tiles) as i:
                    for hf in range(2):
                        act.wait_ge(up_mm, (base + i) * 2 + hf + 1)
                        A(silu_g[TM:2 * TM, hf * 256:hf * 256 + 256], bank(hf)[0:TM, 0:256], ACT.Silu).then_inc(silu_done, 1)
                    act.wait_ge(tok_mm, base + l + i + 3)
                    A(tok_t[:, :, :], bank(2).rearrange("p (k t) -> p k t", k=KD), ACT.Copy).then_inc(tok_done, 1)
                    act.wait_ge(y_out, (base + i + 1) * LANDED)
                    act.wait_ge(y_mm, base + i + 1)
                    for n in range(2):
                        ins = A(y_row[:, n * 512:(n + 1) * 512], bank(4)[n * TM:(n + 1) * TM, :], ACT.Copy)
                    ins.then_inc(y_done, 1)
                    act.wait_ge(y_done, base + i + 2)
                    act.dma_start(y_dram[bass.ds(i * TM, TM), :], y_row).then_inc(y_out, LANDED)
                for t in range(TILES):
                    r, b = ROWS[t], t % 2
                    picks_landed(act, l, t)
                    if t >= 2:
                        act.wait_ge(x_done, TILES * l + t - 1)
                    A(mixed[0:r, b, :], picked[t % 4][0:r, 0, :], ACT.Copy, scale=pick[0:r, 2, t:t + 1]).then_inc(pick_scaled, 1)
                    act.wait_ge(var2_done, TILES * l + t + 1)
                    A(std[0:r, 0:1], mean_var[0:r, 1:2], ACT.Sqrt, bias=eps[0:r, :]).then_inc(std2_done, 1)
                    if l + 1 < DEPTH and t == 2:
                        lambda_exp(l + 1)

        @block.vector
        def _(dve):
            V = nc.vector
            steps = [0]

            def seq(ins):
                steps[0] += 1
                ins.then_inc(dve_step, 1)
                dve.wait_ge(dve_step, steps[0])

            seq(V.memset(mod_row[:, :, :], 0.0))
            seq(V.memset(c_t[:, :, :], 0.0))
            seq(V.memset(reset[:, :, :], 1.0))
            seq(V.memset(reset[:, :, 0:1], 0.0))
            seq(V.memset(logits[:, :, :], 0.0))
            V.memset(cnt[:, 5, :], 1.0).then_inc(setup_dve, 1)
            dve.wait_ge(const_ready, 1)
            seq(V.tensor_copy(token_f[:, :], token_i[:, :]))
            dve.wait_ge(c_mm, 1)
            V.tensor_copy(c_t[:, :, 0:2], bank(7)[:, 0:16].rearrange("p (s k) -> p k s", s=2)).then_inc(c_ready, 1)

            def layer_norm_tail(out, src, r, ready, need):
                dve.wait_ge(ready, need)
                seq(V.reciprocal(std[0:r, 1:2], std[0:r, 0:1]))
                return V.tensor_scalar(out, src, mean_var[0:r, 0:1], std[0:r, 1:2], ALU.subtract, ALU.mult)

            def statistics(src, r):
                for hf in range(2):
                    seq(V.bn_stats(stats[0:r, hf, :], src[:, hf * 512:hf * 512 + 512]))
                return V.bn_aggr(mean_var[0:r, :], stats[0:r, :, :])

            def add_bias(l, n):
                dve.wait_ge(ada_in, 4 * LANDED * (l + 1))
                dve.wait_ge(ada_mm, 3 * l + n + 1)
                V.tensor_tensor(mod_row[:, n, :], bank(ADA_BANK[n]), mod_row[:, n, :], ALU.add).then_inc(mod_ready, 1)

            def prepare_lambda(l):
                add_bias(l, 0)
                dve.wait_ge(small_in, 7 * LANDED * (l + 1))
                seq(V.tensor_tensor(lam_prod[:, :, :], lam_qk[:, 0::2, :], lam_qk[:, 1::2, :], ALU.mult))
                V.reduce_sum(lam_e[:, 0:2], lam_prod[:, :, :], AX_X).then_inc(lam_ready, 1)

            def prepare_columns(l):
                dve.wait_ge(lam_exp, l + 1)
                seq(V.tensor_tensor(lam_e[:, 4:5], lam_e[:, 3:4], lam_e[:, 2:3], ALU.subtract))
                V.tensor_scalar(lam_e[:, 5:6], lam_e[:, 4:5], -lam_init(l), None, ALU.add).then_inc(lam_ready, 1)
                dve.wait_ge(cols_mm, l + 1)
                V.tensor_copy(cols[:, 32:312], bank(4)[:, 32:312])
                seq(V.tensor_copy(cols[:, 0:32].rearrange("p (s j b) -> p s j b", s=2, j=4),
                                  bank(5).rearrange("p (b j x) -> p x j b", b=4, j=4)[:, 0:2, :, :]))
                by_stream = cols[:, 0:32].rearrange("p (s k) -> p s k", s=2)
                seq(V.tensor_scalar(by_stream[:, :, 8:16], by_stream[:, :, 8:16], 1.0, None, ALU.add))
                seq(V.tensor_scalar(cols[:, 44:45], cols[:, 44:45], 1.0 - lam_init(l), None, ALU.mult))
                seq(V.memset(glu[:, :, 0:STATE], 0.0))
                V.tensor_copy(glu[:, :, STATE + SEQ:STATE + SEQ + STATE],
                              cols[:, 192:312].rearrange("p (j t) -> p j t", j=4)).then_inc(cols_ready, 1)

            prepare_lambda(0)
            prepare_columns(0)
            for l in range(DEPTH):
                for t in range(TILES):
                    r, s = ROWS[t], t // 4
                    dve.wait_ge(xt_mm, xt_per * l + 2 * t + 1)
                    if t == 0:
                        dve.wait_ge(cols_ready, l + 1)
                    for k in range(4):
                        ins = V.tensor_scalar(h_t[:, k, COL[t]:COL[t] + r], bank(4)[:, k * P:k * P + r],
                                              cols[:, 16 * s + 8 + k:16 * s + 9 + k], cols[:, 16 * s + k:16 * s + k + 1],
                                              ALU.mult, ALU.add)
                    ins.then_inc(ht_dve, 1)
                for j in range(4):
                    dve.wait_ge(sig_done, 4 * l + j + 1)
                    V.tensor_tensor(glu[:, j, STATE:STATE + SEQ], bank(2 * (j % 2)), sig[:, j % 2, 0:SEQ], ALU.mult)
                    V.tensor_tensor(glu[:, j, GW - DEC:GW], bank(6 + j % 2)[:, 0:DEC], sig[:, j % 2, SEQ:NTOK],
                                    ALU.mult).then_inc(glu_done, 1)
                    dve.wait_ge(glu_done, 4 * l + j + 1)
                    acc = mix_t[:, 4 + j, 0:CW]
                    tap = cols[:, 64 + TAPS * j:64 + TAPS * (j + 1)]
                    if j == 2 and l == 0:
                        dve.wait_ge(y_zeroed, LANDED)
                    V.tensor_scalar(acc, glu[:, j, 0:CW], tap[:, 0:1], cols[:, 32 + j:33 + j], ALU.mult, ALU.add).then_inc(conv_step, 1)
                    V.tensor_scalar(odd_sum, glu[:, j, 1:1 + CW], tap[:, 1:2], None, ALU.mult).then_inc(conv_step, 1)
                    for w in range(2, DVE_TAPS):
                        dve.wait_ge(conv_step, DVE_TAPS * (4 * l + j) + w - 1)
                        out = odd_sum if w % 2 else acc
                        V.scalar_tensor_tensor(out=out, in0=glu[:, j, w:w + CW], scalar=tap[:, w:w + 1], in1=out,
                                               op0=ALU.mult, op1=ALU.add).then_inc(conv_step, 1)
                    dve.wait_ge(conv_step, DVE_TAPS * (4 * l + j + 1))
                    seq(V.tensor_tensor(acc, acc, odd_sum, ALU.add))
                    dve.wait_ge(tap_added, POOL_TAPS * (4 * l + j + 1))
                    V.tensor_tensor(acc, acc, pool_sum, ALU.add).then_inc(conv_done, 1)
                    if j in (0, 2):
                        add_bias(l, 1 + j // 2)

                for i in range(2 * TILES):
                    t, r = i % TILES, ROWS[i % TILES]
                    dve.wait_ge(proj_act, pr_per * l + i + 1)
                    src = qk_row[0:r, i % 2, :].rearrange("p (g c) -> p g c", g=8)
                    cos = rope[0:r, t, 0:16].unsqueeze(1).to_broadcast([r, 8, 16])
                    sin = rope[0:r, t, 16:32].unsqueeze(1).to_broadcast([r, 8, 16])
                    V.tensor_tensor(rope_t[0:r, 0, :, :], src[:, :, 0:16], cos, ALU.mult)
                    V.tensor_tensor(rope_t[0:r, 1, :, 0:8], src[:, :, 8:16], sin[:, :, 0:8], ALU.mult)
                    seq(V.tensor_tensor(rope_t[0:r, 1, :, 8:16], src[:, :, 0:8], sin[:, :, 8:16], ALU.mult))
                    V.tensor_tensor(src[:, :, 0:16],
                                    rope_t[0:r, 0, :, :], rope_t[0:r, 1, :, :], ALU.add).then_inc(proj_rope, 1)
                    dve.wait_ge(proj_rope, rope_per * l + i + 1)
                    if i == TILES - 2:
                        dve.wait_ge(conv_stat_mm, 2 * l + 1)
                        for j in range(4):
                            view = mix_t[:, 4 + j, 0:CW].rearrange("p (b c) -> p b c", b=2)
                            V.tensor_tensor(view, view, pair[3][:, :, 0:HALF], ALU.subtract).then_inc(centred, 1)
                    if i == TILES + 3:
                        dve.wait_ge(conv_std, l + 1)
                        seq(V.reciprocal(glu[:, 1, 0:CW], glu[:, 0, 0:CW]))
                        for j in range(4):
                            V.tensor_tensor(mix_t[:, 4 + j, 0:CW], mix_t[:, 4 + j, 0:CW], glu[:, 1, 0:CW], ALU.mult).then_inc(conv_normed, 1)
                def maxima(i):
                    t, b = i // 4, i % 2
                    r, keys = ROWS[t], (KEYS_S if t == 4 else (t + 1) * P)
                    dve.wait_ge(score_mm, at_per * l + i + 1)
                    if t < 4:
                        seq(V.memset(pair[b][0:64, :, keys - 64:keys], NEG))
                    seq(V.reduce_max(row_max[0:r, b, :], pair[b][0:r, :, 0:keys], AX_X))
                    V.tensor_scalar(neg_max[0:r, b, :], row_max[0:r, b, :], -SCALE, None, ALU.mult).then_inc(max_done, 1)

                def combine(i):
                    t, b = i // 4, i % 2
                    r, keys = ROWS[t], (KEYS_S if t == 4 else (t + 1) * P)
                    dve.wait_ge(exp_done, at_per * l + i + 1)
                    seq(V.reciprocal(row_inv[0:r, b, :], row_sum[0:r, b, :]))
                    if i >= 2:
                        dve.wait_ge(attn_t_mm, at_per * l + i - 1)
                    V.tensor_scalar(attn[0:r, b, 0:keys], prob[0:r, b, 0, 0:keys], row_inv[0:r, b, 0:1], None, ALU.mult)
                    seq(V.tensor_scalar(row_inv[0:r, b, 1:2], row_inv[0:r, b, 1:2], lam_e[0:r, 5:6], None, ALU.mult))
                    V.scalar_tensor_tensor(out=attn[0:r, b, 0:keys], in0=prob[0:r, b, 1, 0:keys], scalar=row_inv[0:r, b, 1:2],
                                           in1=attn[0:r, b, 0:keys], op0=ALU.mult, op1=ALU.add).then_inc(attn_done, 1)

                def head_squares(t):
                    r = ROWS[t]
                    dve.wait_ge(out_row_done, TILES * l + t + 1)
                    seq(V.tensor_tensor(square[0:r, :], out_row[0:r, :], out_row[0:r, :], ALU.mult))
                    V.reduce_sum(head_ss[0:r, 0, :], square[0:r, :].rearrange("p (h c) -> p h c", h=4), AX_X).then_inc(head_ss_done, 1)

                def head_norm(t):
                    r = ROWS[t]
                    dve.wait_ge(head_std, TILES * l + t + 1)
                    seq(V.reciprocal(head_ss[0:r, 2, :], head_ss[0:r, 1, :]))
                    view = out_row[0:r, :].rearrange("p (h c) -> p h c", h=4)
                    V.tensor_tensor(view, view, head_ss[0:r, 2, :].unsqueeze(2).to_broadcast([r, 4, P]), ALU.mult).then_inc(out_normed, 1)

                def leave_out_t(t):
                    dve.wait_ge(out_t_mm, TILES * l + t + 1)
                    V.tensor_scalar(mix_t[:, 0:4, MCOL[t]:MCOL[t] + ROWS[t]],
                                    bank(6 + t % 2).rearrange("p (h t) -> p h t", h=4)[:, :, 0:ROWS[t]],
                                    cols[:, 44:45], None, ALU.mult).then_inc(out_t_done, 1)

                dve.wait_ge(mod_out, 2 * LANDED * (l + 1))
                dve.wait_ge(k_out[0], 2 * LANDED * (l + 1))
                dve.wait_ge(k_out[1], 3 * LANDED * (l + 1))
                maxima(0)
                for i in range(at_per + 3):
                    if i + 1 < at_per:
                        maxima(i + 1)
                    if i < at_per:
                        combine(i)
                    if i >= 4 and i % 4 == 0:
                        head_squares(i // 4 - 1)
                    if i >= 5 and i % 4 == 1:
                        head_norm(i // 4 - 1)
                    if i >= 6 and i % 4 == 2:
                        leave_out_t(i // 4 - 1)

                dve.wait_ge(bc1_in, 4 * LANDED * (l + 1))
                dve.wait_ge(v_out, TILES * LANDED * (l + 1))
                for t in range(TILES):
                    r, b, s = ROWS[t], t % 2, t // 4
                    dve.wait_ge(mixout_mm, TILES * l + t + 1)
                    if t >= 2:
                        dve.wait_ge(h_ready, TILES * l + t - 1)
                    row = norm_row[0:r, b, :]
                    V.tensor_tensor(row.rearrange("p (n c) -> p n c", n=2), pair[b][0:r, :, :],
                                    gate_bc[0:r, s, :].rearrange("p (n c) -> p n c", n=2), ALU.mult).then_inc(mix_read, 1)
                    dve.wait_ge(mix_read, TILES * l + t + 1)
                    seq(V.scalar_tensor_tensor(out=row, in0=x[0:r, t, :], scalar=ALPHA, in1=row, op0=ALU.mult, op1=ALU.add))
                    statistics(row, r).then_inc(var_done, 1)
                    dve.wait_ge(var_done, TILES * l + t + 1)
                    layer_norm_tail(row, row, r, std_done, TILES * l + t + 1).then_inc(normed, 1)

                dve.wait_ge(logit_mm, TILES * (l + 1))
                V.tensor_copy(logits[:, 0:4, :], bank(6)[:, 0:64].rearrange("p (t e) -> p t e", t=4))
                seq(V.tensor_copy(logits[0:DEC, 4, :], bank(6)[0:DEC, 64:80]))
                t_max, t_sum, t_inv = small[:, 0, 0:TILES], small[:, 1, 0:TILES], small[:, 2, 0:TILES]

                def over_e(v):
                    return v.unsqueeze(2).to_broadcast([P, TILES, EXPERTS])

                seq(V.reduce_max(t_max, logits[:, :, :], AX_X))
                V.tensor_tensor(logits[:, :, :], logits[:, :, :], over_e(t_max), ALU.subtract).then_inc(logit_max, 1)
                dve.wait_ge(logit_exp, l + 1)
                seq(V.reduce_sum(t_sum, score[:, :, :], AX_X))
                seq(V.reciprocal(t_inv, t_sum))
                seq(V.tensor_tensor(score[:, :, :], score[:, :, :], over_e(t_inv), ALU.mult))
                seq(V.tensor_tensor(sel[:, :, :], score[:, :, :], b_router[:, :].unsqueeze(1).to_broadcast([P, TILES, EXPERTS]), ALU.add))

                def count_better(out, v, n):
                    shape = [P, n, 4, 4]
                    vi = v.unsqueeze(2).to_broadcast(shape)
                    vj = v.unsqueeze(3).to_broadcast(shape)
                    ge, gt = cmp_ge[:, 0:n, :, :], cmp_gt[:, 0:n, :, :]
                    V.tensor_tensor(ge, vi, vj, ALU.is_ge)
                    seq(V.tensor_tensor(gt, vi, vj, ALU.is_gt))
                    V.tensor_tensor(ge, ge, lower[:, :, :].unsqueeze(1).to_broadcast(shape), ALU.mult)
                    seq(V.tensor_tensor(gt, gt, upper[:, :, :].unsqueeze(1).to_broadcast(shape), ALU.mult))
                    seq(V.tensor_tensor(ge, ge, gt, ALU.add))
                    seq(V.reduce_sum(out, ge, AX_X))

                by_group = "p t (g i) -> p (t g) i"
                sel_g = sel[:, :, :].rearrange(by_group, g=GROUPS)
                worse_g = worse[:, :, :].rearrange(by_group, g=GROUPS)
                mask_g = mask[:, :, :].rearrange(by_group, g=GROUPS)
                count_better(worse_g, sel_g, TILES * GROUPS)
                seq(V.tensor_scalar(mask_g, worse_g, float(TOP), None, ALU.is_lt))
                seq(V.tensor_tensor(worse_g, mask_g, sel_g, ALU.mult))
                group_score, group_rank = small[:, 3, :], small[:, 4, :]
                seq(V.reduce_sum(group_score, worse_g, AX_X))
                count_better(group_rank.rearrange("p (t g) -> p t g", t=TILES), group_score.rearrange("p (t g) -> p t g", t=TILES), TILES)
                seq(V.tensor_scalar(group_rank, group_rank, 1.0, None, ALU.is_lt))
                seq(V.tensor_tensor(mask_g, mask_g, group_rank.unsqueeze(2).to_broadcast([P, TILES * GROUPS, PER_GROUP]), ALU.mult))
                V.memset(mask[DEC:P, 4, :], 0.0).then_inc(mask_ready, 1)
                dve.wait_ge(mask_ready, l + 1)
                seq(V.tensor_tensor_scan(worse[:, :, :].rearrange("p t e -> p (t e)"), reset[:, :, :].rearrange("p t e -> p (t e)"),
                                         mask[:, :, :].rearrange("p t e -> p (t e)"), 0.0, ALU.mult, ALU.add))
                for k in range(TOP):
                    ins = V.scalar_tensor_tensor(out=picks[:, 2 + k, :, :], in0=worse[:, :, :], scalar=float(k + 1), in1=mask[:, :, :],
                                                 op0=ALU.is_equal, op1=ALU.mult)
                seq(ins)
                dve.wait_ge(rank_mm, l + 1)
                seq(V.tensor_scalar(cnt[:, 0, :], bank(7)[:, 80:96], float(TM - 1), None, ALU.add))
                seq(V.tensor_copy(cnt_i[:, 0, :], cnt[:, 0, :]))
                seq(V.tensor_scalar(cnt_i[:, 1, :], cnt_i[:, 0, :], TM.bit_length() - 1, None, ALU.arith_shift_right))
                seq(V.tensor_copy(cnt[:, 1, :], cnt_i[:, 1, :]))
                seq(V.tensor_scalar(cnt[:, 1, :], cnt[:, 1, :], 1.0, None, ALU.max))
                key, key2, streams, place = (keys_e[:, n, :] for n in range(4))
                tiles_e, counts = cnt[:, 1, :], bank(7)[:, 80:96]
                number = plan[:, 32:48]
                top = small[:, 5, 0:2]
                seq(V.tensor_tensor(key, counts, plan[:, 0:16], ALU.mult))
                seq(V.tensor_tensor(key, key, plan[:, 16:32], ALU.add))
                seq(V.reduce_max(top[:, 0:1], key, AX_X))
                seq(V.tensor_scalar(resident[:, 0, :], key, top[:, 0:1], None, ALU.is_equal))
                seq(V.scalar_tensor_tensor(out=key2, in0=resident[:, 0, :], scalar=-1e6, in1=key, op0=ALU.mult, op1=ALU.add))
                seq(V.reduce_max(top[:, 1:2], key2, AX_X))
                seq(V.tensor_scalar(resident[:, 1, :], key2, top[:, 1:2], None, ALU.is_equal))
                seq(V.tensor_tensor(streams, resident[:, 0, :], resident[:, 1, :], ALU.add))
                seq(V.tensor_scalar(streams, streams, -1.0, 1.0, ALU.mult, ALU.add))
                seq(V.tensor_tensor_scan(place, cnt[:, 5, :], streams, 0.0, ALU.mult, ALU.add))
                seq(V.tensor_tensor(place, place, streams, ALU.mult))
                wide = [P, STREAMED, EXPERTS]
                seq(V.tensor_tensor(onehot[:, :, :], place.unsqueeze(1).to_broadcast(wide),
                                    plan[:, 48:62].unsqueeze(2).to_broadcast(wide), ALU.is_equal))
                V.tensor_tensor(stream_pick[:, 0, :, :], onehot[:, :, :], tiles_e.unsqueeze(1).to_broadcast(wide), ALU.mult)
                V.tensor_tensor(stream_pick[:, 1, :, :], onehot[:, :, :], number.unsqueeze(1).to_broadcast(wide), ALU.mult)
                both = [P, 2, EXPERTS]
                V.tensor_tensor(res_pick[:, 0, :, :], resident[:, :, :], tiles_e.unsqueeze(1).to_broadcast(both), ALU.mult)
                seq(V.tensor_tensor(res_pick[:, 1, :, :], resident[:, :, :], number.unsqueeze(1).to_broadcast(both), ALU.mult))
                V.reduce_sum(stream_n[:, :, :], stream_pick[:, :, :, :], AX_X)
                seq(V.reduce_sum(res_n[:, :, :], res_pick[:, :, :, :], AX_X))
                seq(V.tensor_scalar(res_n[:, 0, :], res_n[:, 0, :], float(PARTS), None, ALU.max))
                thirds = [P, 2, PARTS]
                seq(V.tensor_scalar(part_n[:, :, :], res_n[:, 0, :].unsqueeze(2).to_broadcast(thirds), 43.0, None, ALU.mult))
                seq(V.tensor_tensor(part_n[:, :, :], part_n[:, :, :], plan[:, 62:65].unsqueeze(1).to_broadcast(thirds), ALU.add))
                seq(V.tensor_copy(cnt_i[:, :, 0:PARTS], part_n[:, :, :]))
                seq(V.tensor_scalar(cnt_i[:, :, 8:8 + PARTS], cnt_i[:, :, 0:PARTS], 7, None, ALU.arith_shift_right))
                seq(V.tensor_copy(part_n[:, :, :], cnt_i[:, :, 8:8 + PARTS]))
                n_b, end_b, start_b, one_b = (block_n[:, n, :] for n in range(4))
                groups = n_b[:, 0:18].rearrange("p (g b) -> p g b", b=3)
                V.tensor_copy(groups[:, :, 0:2], stream_n[:, 0, 0:12].rearrange("p (g b) -> p g b", b=2))
                V.tensor_copy(groups[:, :, 2], part_n[:, :, :].rearrange("p r q -> p (r q)"))
                V.memset(one_b, 1.0)
                seq(V.tensor_copy(n_b[:, 18:20], stream_n[:, 0, 12:14]))
                seq(V.tensor_tensor_scan(end_b, one_b, n_b, 0.0, ALU.mult, ALU.add))
                seq(V.tensor_tensor(start_b, end_b, n_b, ALU.subtract))
                V.tensor_copy(table[:, T_COUNT:T_COUNT + N_BLOCKS], n_b)
                V.tensor_copy(table[:, T_START:T_START + N_BLOCKS], start_b)
                V.tensor_copy(table[:, T_STREAM:T_STREAM + STREAMED], stream_n[:, 1, :])
                V.tensor_copy(table[:, T_RESIDENT:T_RESIDENT + 2], res_n[:, 1, :])
                V.tensor_copy(table[:, T_TILES:T_TILES + 1], end_b[:, 19:20])
                seq(V.tensor_copy(table[:, T_BASE:T_BASE + 1], total[:, :]))
                V.tensor_tensor(total[:, :], total[:, :], end_b[:, 19:20], ALU.add).then_inc(table_ready, 1)
                start_g = start_b[:, 0:18].rearrange("p (g b) -> p g b", b=3)
                V.tensor_copy(stream_start[:, 0:12].rearrange("p (g b) -> p g b", b=2), start_g[:, :, 0:2])
                part_at = start_g[:, :, 2].rearrange("p (r q) -> p r q", r=2)
                V.tensor_copy(res_vals[:, 0, :], part_at[:, :, 0])
                V.tensor_copy(res_vals[:, 1, :], part_n[:, :, 0])
                V.tensor_tensor(res_vals[:, 2, :], part_at[:, :, 1], part_at[:, :, 0], ALU.subtract)
                V.tensor_tensor(res_vals[:, 3, :], part_n[:, :, 0], part_n[:, :, 1], ALU.add)
                V.tensor_tensor(res_vals[:, 4, :], part_at[:, :, 2], part_at[:, :, 1], ALU.subtract)
                seq(V.tensor_copy(stream_start[:, 12:14], start_b[:, 18:20]))
                V.tensor_tensor(res_vals[:, 2, :], res_vals[:, 2, :], part_n[:, :, 0], ALU.subtract)
                seq(V.tensor_tensor(res_vals[:, 4, :], res_vals[:, 4, :], part_n[:, :, 1], ALU.subtract))
                by_e = [P, EXPERTS, STREAMED]
                V.tensor_tensor(stream_at[:, :, :], onehot[:, :, :].rearrange("p s e -> p e s"),
                                stream_start.unsqueeze(1).to_broadcast(by_e), ALU.mult)
                for r in range(2):
                    five = [P, 5, EXPERTS]
                    ins = V.tensor_tensor(res_wide[:, :, r, :], resident[:, r, :].unsqueeze(1).to_broadcast(five),
                                          res_vals[:, :, r].unsqueeze(2).to_broadcast(five), ALU.mult)
                seq(ins)
                V.reduce_sum(cnt[:, 3, :], stream_at[:, :, :], AX_X)
                seq(V.tensor_tensor(res_by_e[:, :, :], res_wide[:, :, 0, :], res_wide[:, :, 1, :], ALU.add))
                seq(V.tensor_tensor(res_by_e[:, 0, :], res_by_e[:, 0, :], cnt[:, 3, :], ALU.add))
                seq(V.tensor_scalar(res_by_e[:, :, :], res_by_e[:, :, :], float(TM), None, ALU.mult))
                ranks = bank(7)[:, 0:80].rearrange("p (t e) -> p t e", t=TILES)

                def over_t(v):
                    return v.unsqueeze(1).to_broadcast([P, TILES, EXPERTS])

                V.tensor_tensor(sel[:, :, :], ranks, over_t(res_by_e[:, 0, :]), ALU.add)
                V.tensor_tensor(past[:, 0, :, :], ranks, over_t(res_by_e[:, 1, :]), ALU.is_ge)
                seq(V.tensor_tensor(past[:, 1, :, :], ranks, over_t(res_by_e[:, 3, :]), ALU.is_ge))
                V.tensor_tensor(past[:, 0, :, :], past[:, 0, :, :], over_t(res_by_e[:, 2, :]), ALU.mult)
                seq(V.tensor_tensor(past[:, 1, :, :], past[:, 1, :, :], over_t(res_by_e[:, 4, :]), ALU.mult))
                seq(V.tensor_tensor(sel[:, :, :], sel[:, :, :], past[:, 0, :, :], ALU.add))
                seq(V.tensor_tensor(sel[:, :, :], sel[:, :, :], past[:, 1, :, :], ALU.add))
                V.tensor_tensor(picks[:, 0, :, :], picks[:, 2, :, :], sel[:, :, :], ALU.mult)
                seq(V.tensor_tensor(picks[:, 1, :, :], picks[:, 3, :, :], sel[:, :, :], ALU.mult))
                V.tensor_tensor(picks[:, 2, :, :], picks[:, 2, :, :], score[:, :, :], ALU.mult)
                seq(V.tensor_tensor(picks[:, 3, :, :], picks[:, 3, :, :], score[:, :, :], ALU.mult))
                seq(V.reduce_sum(pick[:, :, :], picks[:, :, :, :], AX_X))
                V.tensor_copy(slot_of[:, :, :], pick[:, 0:2, :]).then_inc(slots_ready, 1)
                dve.wait_ge(slots_ready, l + 1)
                picked_tile, offset = small[:, 6, 0:TOP * TILES], small[:, 7, 0:TOP * TILES]
                seq(V.tensor_scalar(cnt_i[:, 0, 0:TOP * TILES], slot_of[:, :, :].rearrange("p k t -> p (k t)"), TM.bit_length() - 1, None,
                                    ALU.arith_shift_right))
                seq(V.tensor_copy(picked_tile, cnt_i[:, 0, 0:TOP * TILES]))
                seq(V.scalar_tensor_tensor(out=offset, in0=picked_tile, scalar=-float(TM),
                                           in1=pick[:, 0:2, :].rearrange("p k t -> p (k t)"), op0=ALU.mult, op1=ALU.add))
                hot = [P, TOP * TILES, MAX_TILES + 2]
                seq(V.tensor_tensor(tile_hot, picked_tile.unsqueeze(2).to_broadcast(hot),
                                    plan[:, 65:65 + MAX_TILES + 2].unsqueeze(1).to_broadcast(hot), ALU.is_equal))
                hot = [P, TOP * TILES, TM]
                V.tensor_tensor(offset_hot, offset.unsqueeze(2).to_broadcast(hot), plan[:, 65:65 + TM].unsqueeze(1).to_broadcast(hot), ALU.is_equal)
                for k in range(TOP):
                    view = tile_hot[:, k * TILES:(k + 1) * TILES, :]
                    ins = V.tensor_tensor(view, view, token_f[:, :].unsqueeze(2).to_broadcast([P, TILES, MAX_TILES + 2]), ALU.mult)
                ins.then_inc(hot_ready, 1)
                seq(V.tensor_tensor(t_sum, pick[:, 2, :], pick[:, 3, :], ALU.add))
                seq(V.tensor_scalar(t_sum[DEC:P, 4:5], t_sum[DEC:P, 4:5], 1.0, None, ALU.add))
                seq(V.reciprocal(t_inv, t_sum))
                for k in range(TOP):
                    seq(V.tensor_tensor(pick[:, 2 + k, :], pick[:, 2 + k, :], t_inv, ALU.mult))
                dve.wait_ge(slot_mm, l + 1)
                V.tensor_copy(slot_token[:, :], bank(5)[0:TM, 0:MAX_TILES + 2]).then_inc(index_ready, 1)

                tiles = dve.value_load(table[0:1, T_TILES:T_TILES + 1], min_val=EXPERTS, max_val=MAX_TILES)
                base = dve.value_load(table[0:1, T_BASE:T_BASE + 1], min_val=0, max_val=DEPTH * MAX_TILES)
                with dve.Fori(0, tiles) as i:
                    for hf in range(2):
                        c = slice(hf * 256, hf * 256 + 256)
                        dve.wait_ge(silu_done, (base + i) * 2 + hf + 1)
                        V.tensor_tensor(act_row[0:TM, c], silu_g[TM:2 * TM, c], bank(hf)[TM:2 * TM, 0:256], ALU.mult).then_inc(act_done, 1)
                        dve.wait_ge(act_t_mm, (base + i) * 2 + hf + 1)
                        V.tensor_copy(act_t[:, 2 * hf:2 * hf + 2, :],
                                      bank((3, 5)[hf])[:, 0:2 * TM].rearrange("p (f t) -> p f t", f=2)).then_inc(act_t_done, 1)

                dve.wait_ge(bc2_in, 4 * LANDED * (l + 1))
                for t in range(TILES):
                    r, b, s = ROWS[t], t % 2, t // 4
                    picks_landed(dve, l, t)
                    dve.wait_ge(pick_scaled, TILES * l + t + 1)
                    row = mixed[0:r, b, :]
                    V.scalar_tensor_tensor(out=row, in0=picked[t % 4][0:r, 1, :], scalar=pick[0:r, 3, t:t + 1], in1=row,
                                           op0=ALU.mult, op1=ALU.add).then_inc(picked_read, 1)
                    dve.wait_ge(picked_read, TILES * l + t + 1)
                    seq(V.tensor_tensor(row, row, gate2_bc[0:r, s, :], ALU.mult))
                    seq(V.scalar_tensor_tensor(out=row, in0=x[0:r, t, :], scalar=ALPHA, in1=row, op0=ALU.mult, op1=ALU.add))
                    statistics(row, r).then_inc(var2_done, 1)
                    dve.wait_ge(var2_done, TILES * l + t + 1)
                    layer_norm_tail(row, row, r, std2_done, TILES * l + t + 1).then_inc(normed2, 1)
                    if l + 1 < DEPTH and t == 2:
                        prepare_lambda(l + 1)
                    if l + 1 < DEPTH and t == 3:
                        prepare_columns(l + 1)

        @block.tensor
        def _(pe):
            mm, tr = nc.tensor.matmul, nc.tensor.transpose
            fills = [0] * ALL_SLOTS

            def weights(s):
                fills[s] += 1
                pe.wait_ge(landed[s], LANDED * fills[s])

            pe.sem_inc(tok_mm, 1)
            pe.wait_ge(const_ready, 1)
            pe.wait_ge(c_silu_ready, 1)
            tr(bank(7)[:, 0:16], c_silu[:, :], ident[0:16, 0:16]).then_inc(c_mm, 1)
            pe.wait_ge(c_ready, 1)

            def modulation(l, n):
                s4 = ADA_SLOTS[l][4 * n:4 * n + 4]
                for s in s4:
                    weights(s)
                for k in range(KD):
                    for j in range(4):
                        ins = mm(bank(ADA_BANK[n])[32 * j:32 * j + 32, :], c_t[:, k, :], by_k(s4[j])[:, k, :],
                                 start=(k == 0), stop=(k == KD - 1))
                ins.then_inc(ada_mm, 1)

            def columns(l):
                pe.wait_ge(mod_ready, 3 * l + 1)
                for b in range(4):
                    tr(bank(5)[:, b * P:(b + 1) * P], mod_row[:, 0, b * P:(b + 1) * P], ident[:, :])
                pe.wait_ge(small_in, 7 * LANDED * (l + 1))
                c = bank(4)
                tr(c[:, 32:45], vec_row[:, :], ident[0:13, 0:13])
                tr(c[:, 45:64], ident[0:19, :], ident[0:19, 0:19])
                for j in range(4):
                    tr(c[:, 64 + TAPS * j:64 + TAPS * (j + 1)], conv_w_row[:, j * P:(j + 1) * P], ident[0:TAPS, 0:TAPS])
                tr(c[:, 188:192], ident[0:4, :], ident[0:4, 0:4])
                for j in range(4):
                    ins = tr(c[:, 192 + STATE * j:192 + STATE * (j + 1)], state_row[:, j * P:(j + 1) * P], ident[0:STATE, 0:STATE])
                ins.then_inc(cols_mm, 1)

            modulation(0, 0)
            columns(0)
            for l in range(DEPTH):
                if l == 0:
                    pe.wait_ge(x_in, 2 * LANDED)
                for t in range(TILES):
                    r = ROWS[t]
                    if l:
                        pe.wait_ge(x_done, TILES * (l - 1) + t + 1)
                    for hf in range(2):
                        if hf == 0 and t == 0:
                            pe.wait_ge(cols_ready, l + 1)
                        if t:
                            pe.wait_ge((ht_dve, ht_act)[hf], TILES * l + t)
                        for k in range(4):
                            c0 = (4 * hf + k) * P
                            ins = tr(bank(4 + hf)[:, k * P:k * P + r], x[0:r, t, c0:c0 + P], ident[0:r, 0:r])
                        ins.then_inc(xt_mm, 1)
                pe.wait_ge(ht_dve, TILES * (l + 1))
                pe.wait_ge(ht_act, TILES * (l + 1))
                weights(0)
                weights(1)
                for j in range(4):
                    if j >= 2:
                        pe.wait_ge(glu_done, 4 * l + j - 1)
                    for part, s in ((1, 1), (0, 0)):
                        for k in range(KD):
                            mm(bank(2 * (j % 2) + part), by_k(s)[:, k, j * P:(j + 1) * P], h_t[:, k, 0:SEQ],
                               start=(k == 0), stop=(k == KD - 1))
                        for k in range(KD):
                            ins = mm(bank(6 + j % 2)[:, part * DEC:(part + 1) * DEC], by_k(s)[:, k, j * P:(j + 1) * P],
                                     h_t[:, k, SEQ:NTOK], start=(k == 0), stop=(k == KD - 1))
                    ins.then_inc(u_mm, 1)
                    if j in (0, 2):
                        modulation(l, 1 + j // 2)

                def project(i):
                    t, r, s = i % TILES, ROWS[i % TILES], (2, 3, 0)[i // TILES]
                    if t == 0:
                        weights(s)
                    if i < 4:
                        pe.wait_ge(glu_done, 4 * l + 4)
                    else:
                        pe.wait_ge(proj_act, pr_per * l + i - 3)
                    for k in range(KD):
                        ins = mm(bank(i % 4)[0:r, :], h_t[:, k, COL[t]:COL[t] + r], by_k(s)[:, k, :],
                                 start=(k == 0), stop=(k == KD - 1))
                    ins.then_inc(proj_mm, 1)

                def turn(i):
                    if i == 0:
                        pe.wait_ge(mod_ready, 3 * (l + 1))
                    if i >= 2:
                        pe.wait_ge(qk_t_done, qt_per * l + i - 1)
                    if i < 2 * TILES:
                        r = ROWS[i % TILES]
                        pe.wait_ge(proj_act, pr_per * l + i + 1)
                        pe.wait_ge(proj_rope, rope_per * l + i + 1)
                        src = qk_row[0:r, i % 2, :]
                    else:
                        r = P
                        pe.wait_ge(cache_k_in, LANDED * (l + 1))
                        src = cache_k_row[:, i - 2 * TILES, :]
                    for h in range(HEADS):
                        ins = tr(bank(4 + i % 2)[:, h * P:h * P + r], src[:, h * P:(h + 1) * P], ident[0:r, 0:r])
                    ins.then_inc(qk_t_mm, 1)

                if l == 0:
                    pe.wait_ge(setup_in, n_setup * LANDED)
                for i in range(3 * TILES):
                    if i <= 2 * TILES:
                        project(i)
                    if 2 <= i < qt_per + 2:
                        turn(i - 2)
                    if i == 2:
                        for b, c0 in enumerate((SEQ, GW - STATE)):
                            for j in range(4):
                                ins = tr(bank(6 + b)[0:STATE, j * P:(j + 1) * P], glu[:, j, c0:c0 + STATE], ident[:, :])
                            ins.then_inc(new_conv_mm, 1)
                    if i == TILES - 2:
                        pe.wait_ge(conv_done, 4 * (l + 1))
                        pe.wait_ge(new_conv_ready, 2 * (l + 1))
                        for b in range(2):
                            for j in range(4):
                                ins = mm(pair[3][:, b, 0:HALF], conv_mean[:, :], mix_t[:, 4 + j, b * HALF:(b + 1) * HALF],
                                         start=(j == 0), stop=(j == 3))
                        ins.then_inc(conv_stat_mm, 1)
                    if i == TILES + 1:
                        pe.wait_ge(squared, 4 * (l + 1))
                        for b in range(2):
                            for j in range(4):
                                ins = mm(pair[3][:, b, 0:HALF], conv_mean[:, :], glu[:, j, b * HALF:(b + 1) * HALF],
                                         start=(j == 0), stop=(j == 3))
                        ins.then_inc(conv_stat_mm, 1)

                def scores(i):
                    t, h, b = i // 4, i % 4, i % 2
                    r, keys = ROWS[t], (KEYS_S if t == 4 else (t + 1) * P)
                    kt = ks_t if t == 4 else k_t
                    if i >= 2:
                        pe.wait_ge(exp_done, at_per * l + i - 1)
                    pe.wait_ge(q_padded, at_per * l + i + 1)
                    for m in range(2):
                        ins = mm(pair[b][0:r, m, 0:keys], q_pad[:, i % 4, m, 0:r], kt[:, h, 0:keys], start=True, stop=True)
                    ins.then_inc(score_mm, 1)

                def key_blocks(t):
                    if t < 4:
                        return [(n * P, P, v_row[:, n, :]) for n in range(t + 1)]
                    return [(0, P, cache_v[:, 0, :]), (P, P, cache_v[:, 1, :]), (2 * P, DEC, v_row[0:DEC, 4, :])]

                def turn_attn(i):
                    t, b = i // 4, i % 2
                    r = ROWS[t]
                    pe.wait_ge(attn_done, at_per * l + i + 1)
                    if i >= 1:
                        pe.wait_ge(attn_t_done, at_per * l + i)
                    for c0, w, _ in key_blocks(t):
                        ins = tr(bank(4)[0:w, c0:c0 + r], attn[0:r, b, c0:c0 + w], ident[0:r, 0:r])
                    ins.then_inc(attn_t_mm, 1)

                def values(i):
                    t, h = i // 4, i % 4
                    r = ROWS[t]
                    pe.wait_ge(attn_t_done, at_per * l + i + 1)
                    if h == 0:
                        pe.wait_ge(proj_act, pr_per * l + 2 * TILES + t + 1)
                    if t == 4 and h == 0:
                        pe.wait_ge(cache_v_in, LANDED * (l + 1))
                    if h == 0 and t >= 2:
                        pe.wait_ge(out_t_done, TILES * l + t - 1)
                    blocks = key_blocks(t)
                    for n, (c0, w, v) in enumerate(blocks):
                        ins = mm(bank(6 + t % 2)[0:r, h * P:(h + 1) * P], attn_t[0:w, i % 2, c0:c0 + r], v[:, h * P:(h + 1) * P],
                                 start=(n == 0), stop=(n == len(blocks) - 1))
                    ins.then_inc(pv_mm, 1)

                def project_v_part(t, quarter):
                    if quarter == 0 and t >= 2:
                        pe.wait_ge(proj_act, pr_per * l + 2 * TILES + t)
                    for k in (2 * quarter, 2 * quarter + 1):
                        ins = mm(bank(5)[0:ROWS[t], :], h_t[:, k, COL[t]:COL[t] + ROWS[t]], by_k(0)[:, k, :],
                                 start=(k == 0), stop=(k == KD - 1))
                    if quarter == 3:
                        ins.then_inc(proj_mm, 1)

                def turn_out(t):
                    r = ROWS[t]
                    pe.wait_ge(out_normed, TILES * l + t + 1)
                    for h in range(HEADS):
                        ins = tr(bank(6 + t % 2)[:, h * P:h * P + r], out_row[0:r, h * P:(h + 1) * P], ident[0:r, 0:r])
                    ins.then_inc(out_t_mm, 1)

                pe.wait_ge(qk_t_done, qt_per * (l + 1))
                pe.wait_ge(proj_act, pr_per * l + 2 * TILES + 1)
                pe.wait_ge(conv_std, l + 1)
                scores(0)
                scores(1)
                for i in range(at_per + 3):
                    if i + 2 < at_per:
                        scores(i + 2)
                    if i < at_per - 4:
                        project_v_part(i // 4 + 1, i % 4)
                    if i < at_per:
                        turn_attn(i)
                    if 1 <= i <= at_per:
                        values(i - 1)
                    if i >= 6 and i % 4 == 2:
                        turn_out(i // 4 - 1)

                weights(1)
                weights(2)
                pe.wait_ge(conv_t_done, 4 * (l + 1))
                for t in range(TILES + 3):
                    if t < TILES:
                        r, b = ROWS[t], t % 2
                        pe.wait_ge(out_t_done, TILES * l + t + 1)
                        if t >= 2:
                            pe.wait_ge(mix_read, TILES * l + t - 1)
                        for n in range(2):
                            for k in range(KD):
                                ins = mm(pair[b][0:r, n, :], mix_t[:, k, MCOL[t]:MCOL[t] + r], by_k(1 + n)[:, k, :],
                                         start=(k == 0), stop=(k == KD - 1))
                        ins.then_inc(mixout_mm, 1)
                    if t >= 3:
                        u = t - 3
                        pe.wait_ge(route_t_done, 2 * (TILES * l + u + 1))
                        for k in range(KD):
                            ins = mm(bank(6)[0:ROWS[u], u * EXPERTS:(u + 1) * EXPERTS], route_t[k // 4][:, k % 4, 0:ROWS[u]],
                                     w_router[:, k, :], start=(k == 0), stop=(k == KD - 1))
                        ins.then_inc(logit_mm, 1)
                    if 2 <= t < TILES + 2:
                        u = t - 2
                        pe.wait_ge(h_ready, TILES * l + u + 1)
                        for hf in range(2):
                            if u >= 1:
                                pe.wait_ge(route_t_done, 2 * (TILES * l + u - 1) + hf + 1)
                            for k in range(4):
                                c0 = (4 * hf + k) * P
                                ins = tr(bank(4 + hf)[:, k * P:k * P + ROWS[u]], h_row[0:ROWS[u], u % 2, c0:c0 + P],
                                         ident[0:ROWS[u], 0:ROWS[u]])
                            ins.then_inc(route_t_mm, 1)
                pe.wait_ge(mask_ready, l + 1)
                for t in range(TILES):
                    for u in range(t + 1):
                        mm(bank(7)[:, t * EXPERTS:(t + 1) * EXPERTS], (ones if u < t else before)[:, :], mask[:, u, :],
                           start=(u == 0), stop=(u == t))
                for u in range(TILES):
                    ins = mm(bank(7)[:, 80:96], ones[:, :], mask[:, u, :], start=(u == 0), stop=(u == TILES - 1))
                ins.then_inc(rank_mm, 1)
                pe.wait_ge(hot_ready, l + 1)
                for n in range(TOP * TILES):
                    r = ROWS[n % TILES]
                    ins = mm(bank(5)[0:TM, 0:MAX_TILES + 2], offset_hot[0:r, n, :], tile_hot[0:r, n, :],
                             start=(n == 0), stop=(n == TOP * TILES - 1))
                ins.then_inc(slot_mm, 1)

                pe.wait_ge(table_ready, l + 1)
                base = pe.value_load(table[0:1, T_BASE:T_BASE + 1], min_val=0, max_val=DEPTH * MAX_TILES)

                def turn_tokens():
                    for k in range(KD):
                        ins = tr(bank(2)[:, k * TM:(k + 1) * TM], gathered_row[:, k::KD], ident[0:TM, 0:TM])
                    ins.then_inc(tok_mm, 1)

                pe.wait_ge(index_ready, l + 1)
                pe.wait_ge(rows_ready, base + l + 1)
                pe.sem_inc(pe_held, 1)
                turn_tokens()
                def block_of_table(k):
                    return (pe.value_load(table[0:1, T_COUNT + k:T_COUNT + k + 1], min_val=1, max_val=NTOK // TM),
                            pe.value_load(table[0:1, T_START + k:T_START + k + 1], min_val=0, max_val=MAX_TILES - 1))

                following = block_of_table(0)
                for k, (kind, n) in enumerate(BLOCKS):
                    n_tiles, start = following
                    buffer = BUF_A if kind == "r" else (BUF_B, BUF_C)[n % 2]
                    if kind == "s" or n % PARTS == 0:
                        for s in buffer:
                            weights(s)
                    with pe.Fori(0, n_tiles) as g:
                        i = base + start + g
                        pe.wait_ge(tok_done, i + l + 1)

                        def up(hf, ks):
                            for k in ks:
                                for n in range(2):
                                    ins = mm(bank(hf)[n * TM:(n + 1) * TM, 0:256], tok_t[:, k, :],
                                             by_k(buffer[n])[:, k, hf * 256:hf * 256 + 256], start=(k == 0), stop=(k == KD - 1))
                            return ins

                        def turn_act(hf):
                            pe.wait_ge(act_done, i * 2 + hf + 1)
                            pe.sem_inc(pe_held, 1)
                            for f in range(2):
                                ins = tr(bank((3, 5)[hf])[:, f * TM:(f + 1) * TM], act_row[0:TM, 256 * hf + f:256 * (hf + 1):2], ident[0:TM, 0:TM])
                            ins.then_inc(act_t_mm, 1)

                        def down(hf):
                            pe.wait_ge(act_t_done, i * 2 + hf + 1)
                            for f in range(2 * hf, 2 * hf + 2):
                                for n in range(2):
                                    ins = mm(bank(4)[n * TM:(n + 1) * TM, :], act_t[:, f, :], by_f(buffer[2])[:, f, n * 512:(n + 1) * 512],
                                             start=(f == 0), stop=(f == 3))
                            return ins

                        up(0, range(KD)).then_inc(up_mm, 1)
                        up(1, range(KD - 2))
                        turn_act(0)
                        up(1, range(KD - 2, KD)).then_inc(up_mm, 1)
                        pe.wait_ge(y_done, i + 1)
                        down(0)
                        turn_act(1)
                        pe.wait_ge(rows_ready, i + l + 2)
                        pe.sem_inc(pe_held, 1)
                        turn_tokens()
                        down(1).then_inc(y_mm, 1)
                    if k + 1 < N_BLOCKS:
                        following = block_of_table(k + 1)
                    pe.drain().then_inc(block_done, 1)
                tiles = pe.value_load(table[0:1, T_TILES:T_TILES + 1], min_val=EXPERTS, max_val=MAX_TILES)
                pe.wait_ge(tok_done, base + tiles + l + 1)
                pe.wait_ge(y_done, base + tiles + 1)
                pe.sem_inc(pe_held, 1)
                if l + 1 < DEPTH:
                    modulation(l + 1, 0)
                    columns(l + 1)


_INS = ["x_prompt", "x_sample", "cache_k", "cache_v", "state_conv", "c_prompt", "c_sample", "w_ada", "b_ada", "w_in",
        "lambda_qk", "subln_g", "conv_w", "conv_b", "conv_ln_g", "conv_ln_b", "w_out", "ln1_g", "ln1_b", "ln2_g", "ln2_b",
        "w_router", "b_router", "w_gate", "w_up", "w_down"]
_OUTS = [("y_prompt", (1, SEQ, D)), ("y_sample", (1, DEC, D)),
         ("k_prompt", (DEPTH, 1, SEQ, HEADS, 2, HD)), ("v_prompt", (DEPTH, 1, SEQ, HEADS, 2 * HD)),
         ("conv_prompt", (DEPTH, 1, STATE, CONV)),
         ("k_sample", (DEPTH, 1, DEC, HEADS, 2, HD)), ("v_sample", (DEPTH, 1, DEC, HEADS, 2 * HD)),
         ("conv_sample", (DEPTH, 1, STATE, CONV))]


def rope_table():
    half = 8
    inv = np.power(np.float32(500000.0), -np.arange(half, dtype=np.float32) * np.float32(2.0) / np.float32(16))
    pos = np.concatenate([np.arange(SEQ), PAST + np.arange(DEC), np.zeros(TILES * P - NTOK)]).astype(np.float32)
    ang = pos[:, None] * inv[None, :].astype(np.float32)
    cos, sin = np.cos(ang), np.sin(ang)
    return np.concatenate([cos, cos, -sin, sin], 1).astype(np.float32)


def plan_table():
    e = np.arange(EXPERTS)
    free = (e >= FIXED).astype(np.float32)
    return np.concatenate([free * EXPERTS, free * (EXPERTS - e), e, np.arange(1, STREAMED + 1), [86, 43, 0], np.arange(TM)]).astype(np.float32)[None]


def kernel(**inputs):
    import concourse.bacc as bacc
    from concourse.bass_utils import run_bass_kernel_spmd

    nc = bacc.Bacc("TRN2", target_bir_lowering=False, num_devices=1)
    arrays, aps = {}, {}
    constants = {"rope": rope_table(), "eps": np.full((P, 1), EPS, np.float32), "plan": plan_table()}
    for name in _INS + list(constants):
        v = np.ascontiguousarray(constants[name] if name in constants else inputs[name])
        arrays[f"in_{name}"] = v
        aps[name] = nc.dram_tensor(f"in_{name}", v.shape, F32, kind="ExternalInput").ap()
    for name, shape in _OUTS:
        aps[name] = nc.dram_tensor(f"out_{name}", shape, F32, kind="ExternalOutput").ap()
    build(nc, aps)
    r = run_bass_kernel_spmd(nc, [arrays], core_ids=[0])
    return tuple(r.results[0][f"out_{name}"] for name, _ in _OUTS)
```
